# Optimizing a Trainium2 kernel written in Bass

```python
import jax, jax.numpy as jnp
from jax import lax
import numpy as np
import math

D_MODEL = 1024
BATCH = 1
SEQ = 512
DEPTH = 1

N_MEM = 256
A_HEADS = 8
HEAD_DIM = 64
A_WIDTH = A_HEADS * HEAD_DIM
IDX_HEADS = 4
IDX_DIM = 64
TOPK_MAX = 256
Q_BLOCK = 128
B_GROUPS = 8
B_WIDTH = D_MODEL - A_WIDTH
CONV_B_WIDTH = 31
MIX_WIDTH = A_WIDTH + B_WIDTH
ROPE_THETA = 500000.0
ROT_DIM = HEAD_DIM // 4
CROSS_HEADS = 4
CROSS_HEAD_DIM = D_MODEL // CROSS_HEADS
D_FF = 2816
FFN_CONV_WIDTH = 3
EPS = 1e-6
IN_SPLITS = (A_WIDTH, HEAD_DIM, HEAD_DIM, IDX_HEADS * IDX_DIM, IDX_DIM, IDX_HEADS, 2 * B_WIDTH)
IN_COLS = sum(IN_SPLITS)


def rmsnorm(x, g):
    xf = x.astype(jnp.float32)
    y = xf * lax.rsqrt(jnp.mean(xf * xf, axis=-1, keepdims=True) + EPS)
    return (y * g.astype(jnp.float32)).astype(x.dtype)

def layernorm(x, g, b):
    xf = x.astype(jnp.float32)
    mu = jnp.mean(xf, axis=-1, keepdims=True)
    var = jnp.mean(jnp.square(xf - mu), axis=-1, keepdims=True)
    y = (xf - mu) * lax.rsqrt(var + EPS)
    return (y * g.astype(jnp.float32) + b.astype(jnp.float32)).astype(x.dtype)

def causal_dwconv(x, w, b):
    width, ch = w.shape
    y = lax.conv_general_dilated(
        x, w.astype(x.dtype)[:, None, :], window_strides=(1,),
        padding=[(width - 1, 0)], dimension_numbers=('NWC', 'WIO', 'NWC'),
        feature_group_count=ch)
    return y + b.astype(x.dtype)

def rope_tables(positions):
    freqs = ROPE_THETA ** (-jnp.arange(0, ROT_DIM, 2, dtype=jnp.float32) / ROT_DIM)
    ang = positions.astype(jnp.float32)[:, :, None, None] * freqs
    return jnp.cos(ang), jnp.sin(ang)

def partial_rope(x, cos, sin):
    xr = x[..., :ROT_DIM].astype(jnp.float32)
    x1, x2 = xr[..., :ROT_DIM // 2], xr[..., ROT_DIM // 2:]
    rot = jnp.concatenate([x1 * cos - x2 * sin, x2 * cos + x1 * sin], axis=-1)
    return jnp.concatenate([rot.astype(x.dtype), x[..., ROT_DIM:]], axis=-1)

def dsa_attention(q, k, v, qi, ki, wi):
    bsz, seq = q.shape[0], q.shape[1]
    nb = seq // Q_BLOCK
    topk = min(TOPK_MAX, seq // 4)
    qi = qi * (IDX_DIM ** -0.5)
    wi = wi * (IDX_HEADS ** -0.5)
    gather = jax.vmap(lambda a, i: a[i])
    key_pos = jnp.arange(seq)

    def block(args):
        bi, qb, qib, wib = args
        t = bi * Q_BLOCK + jnp.arange(Q_BLOCK)
        causal = key_pos[None, :] <= t[:, None]
        rel = jax.nn.relu(jnp.einsum('bqhd,bsd->bqhs', qib, ki).astype(jnp.float32))
        score = jnp.einsum('bqh,bqhs->bqs', wib.astype(jnp.float32), rel)
        score = jnp.where(causal[None], score, -jnp.inf)
        _, sel = lax.top_k(score, topk)
        k_sel = gather(k, sel)
        v_sel = gather(v, sel)
        valid = sel <= t[None, :, None]
        logits = jnp.einsum('bqhd,bqkd->bqhk', qb, k_sel).astype(jnp.float32) * (HEAD_DIM ** -0.5)
        logits = jnp.where(valid[:, :, None, :], logits, -jnp.inf)
        p = jax.nn.softmax(logits, axis=-1).astype(v.dtype)
        return jnp.einsum('bqhk,bqkd->bqhd', p, v_sel)

    to_blocks = lambda a: a.reshape(bsz, nb, Q_BLOCK, *a.shape[2:]).swapaxes(0, 1)
    out = lax.map(block, (jnp.arange(nb), to_blocks(q), to_blocks(qi), to_blocks(wi)))
    return out.swapaxes(0, 1).reshape(bsz, seq, A_WIDTH)

def hybrid_layer(x, mem, cos, sin, norm_mix_g, w_in, w_out, conv_b_w, conv_b_b, ln_b_g, ln_b_b,
                 norm_cross_g, norm_mem_g, w_q_cross, w_k_cross, w_v_cross, w_o_cross,
                 norm_ffn_g, w_gate, w_up, ffn_conv_w, ffn_conv_b, w_down):
    bsz, seq, _ = x.shape
    h = rmsnorm(x, norm_mix_g)
    proj = h @ w_in
    cuts = [int(c) for c in np.cumsum(IN_SPLITS)[:-1]]
    q, k, v, qi, ki, wi, glu = jnp.split(proj, cuts, axis=-1)
    q = partial_rope(q.reshape(bsz, seq, A_HEADS, HEAD_DIM), cos, sin)
    k = partial_rope(k[:, :, None, :], cos, sin)[:, :, 0]
    qi = partial_rope(qi.reshape(bsz, seq, IDX_HEADS, IDX_DIM), cos, sin)
    ki = partial_rope(ki[:, :, None, :], cos, sin)[:, :, 0]
    a_out = dsa_attention(q, k, v, qi, ki, wi)
    ga, gg = jnp.split(glu, 2, axis=-1)
    u = ga * jax.nn.sigmoid(gg)
    u = causal_dwconv(u, conv_b_w, conv_b_b)
    b_out = jax.nn.silu(layernorm(u, ln_b_g, ln_b_b))
    x = x + jnp.concatenate([a_out, b_out], axis=-1) @ w_out
    hq = rmsnorm(x, norm_cross_g)
    m = rmsnorm(mem, norm_mem_g)
    qc = (hq @ w_q_cross).reshape(bsz, seq, CROSS_HEADS, CROSS_HEAD_DIM)
    kc = (m @ w_k_cross).reshape(bsz, -1, CROSS_HEADS, CROSS_HEAD_DIM)
    vc = (m @ w_v_cross).reshape(bsz, -1, CROSS_HEADS, CROSS_HEAD_DIM)
    logits = jnp.einsum('bshd,bnhd->bhsn', qc, kc).astype(jnp.float32) * (CROSS_HEAD_DIM ** -0.5)
    p = jax.nn.softmax(logits, axis=-1).astype(vc.dtype)
    oc = jnp.einsum('bhsn,bnhd->bshd', p, vc).reshape(bsz, seq, D_MODEL)
    x = x + oc @ w_o_cross
    hf = rmsnorm(x, norm_ffn_g)
    g = causal_dwconv(hf @ w_gate, ffn_conv_w, ffn_conv_b)
    x = x + (jax.nn.silu(g) * (hf @ w_up)) @ w_down
    return x

def first_inputs(seed: int = 0) -> dict:
    key = jax.random.key(seed)
    ks = jax.random.split(key, 24)
    f32 = jnp.float32
    nrm = lambda k, shape, scale: jax.random.normal(k, shape, f32) * scale
    gain = lambda k, shape: 1.0 + 0.02 * jax.random.normal(k, shape, f32)
    L = DEPTH
    offsets = jax.random.randint(ks[2], (BATCH, 1), 0, 2048, dtype=jnp.int32)
    positions = offsets + jnp.arange(SEQ, dtype=jnp.int32)[None, :]
    return {
        'x': nrm(ks[0], (BATCH, SEQ, D_MODEL), 1.0),
        'mem': nrm(ks[1], (BATCH, N_MEM, D_MODEL), 1.0),
        'positions': positions,
        'norm_mix_g': gain(ks[3], (L, D_MODEL)),
        'w_in': nrm(ks[4], (L, D_MODEL, IN_COLS), D_MODEL ** -0.5),
        'w_out': nrm(ks[5], (L, MIX_WIDTH, D_MODEL), MIX_WIDTH ** -0.5),
        'conv_b_w': nrm(ks[6], (L, CONV_B_WIDTH, B_WIDTH), CONV_B_WIDTH ** -0.5),
        'conv_b_b': nrm(ks[7], (L, B_WIDTH), 0.02),
        'ln_b_g': gain(ks[8], (L, B_WIDTH)),
        'ln_b_b': nrm(ks[9], (L, B_WIDTH), 0.02),
        'norm_cross_g': gain(ks[10], (L, D_MODEL)),
        'norm_mem_g': gain(ks[11], (L, D_MODEL)),
        'w_q_cross': nrm(ks[12], (L, D_MODEL, D_MODEL), D_MODEL ** -0.5),
        'w_k_cross': nrm(ks[13], (L, D_MODEL, D_MODEL), D_MODEL ** -0.5),
        'w_v_cross': nrm(ks[14], (L, D_MODEL, D_MODEL), D_MODEL ** -0.5),
        'w_o_cross': nrm(ks[15], (L, D_MODEL, D_MODEL), D_MODEL ** -0.5),
        'norm_ffn_g': gain(ks[16], (L, D_MODEL)),
        'w_gate': nrm(ks[17], (L, D_MODEL, D_FF), D_MODEL ** -0.5),
        'w_up': nrm(ks[18], (L, D_MODEL, D_FF), D_MODEL ** -0.5),
        'ffn_conv_w': nrm(ks[19], (L, FFN_CONV_WIDTH, D_FF), FFN_CONV_WIDTH ** -0.5),
        'ffn_conv_b': nrm(ks[20], (L, D_FF), 0.02),
        'w_down': nrm(ks[21], (L, D_FF, D_MODEL), D_FF ** -0.5),
        'norm_final_g': gain(ks[22], (D_MODEL,)),
    }

def first_block(x, mem, positions, norm_mix_g, w_in, w_out, conv_b_w, conv_b_b, ln_b_g, ln_b_b,
              norm_cross_g, norm_mem_g, w_q_cross, w_k_cross, w_v_cross, w_o_cross,
              norm_ffn_g, w_gate, w_up, ffn_conv_w, ffn_conv_b, w_down, norm_final_g):
    cos, sin = rope_tables(positions)
    for l in range(DEPTH):
        x = hybrid_layer(x, mem, cos, sin, norm_mix_g[l], w_in[l], w_out[l], conv_b_w[l], conv_b_b[l],
                         ln_b_g[l], ln_b_b[l], norm_cross_g[l], norm_mem_g[l], w_q_cross[l], w_k_cross[l],
                         w_v_cross[l], w_o_cross[l], norm_ffn_g[l], w_gate[l], w_up[l], ffn_conv_w[l],
                         ffn_conv_b[l], w_down[l])
    return rmsnorm(x, norm_final_g)


DEPTH_2 = 2

SSM_GROUP = 16
N_GROUPS = D_MODEL // SSM_GROUP
SSM_STATE = 64
N_HEADS = 16
HEAD_DIM_2 = D_MODEL // N_HEADS
ATTN_DIM = N_HEADS * HEAD_DIM_2
D_FF_2 = 4 * D_MODEL
N_A_LAYERS = DEPTH_2 // 2
N_B_LAYERS = DEPTH_2 - N_A_LAYERS
RMS_EPS = 1e-6
DT_MIN = 1e-3
DT_MAX = 1e-1


def rmsnorm_2(x, g):
    xf = x.astype(jnp.float32)
    y = xf * lax.rsqrt(jnp.mean(xf * xf, axis=-1, keepdims=True) + RMS_EPS)
    return (y * g.astype(jnp.float32)).astype(x.dtype)

def sqrelu_mlp(h, w1, w2):
    a = jnp.square(jax.nn.relu(h @ w1))
    return a @ w2

def _ssm_binop(e1, e2):
    a1, b1 = e1
    a2, b2 = e2
    return a2 * a1, a2 * b1 + b2

def s5_mixer(u, log_dt, a_re, a_im, b_re, b_im, c_re, c_im, d_skip, w_glu):
    f32 = jnp.float32
    bsz, length, _ = u.shape
    uf = u.astype(f32).reshape(bsz, length, N_GROUPS, SSM_GROUP)
    lam = lax.complex(a_re.astype(f32), a_im.astype(f32))
    dt = jnp.exp(log_dt.astype(f32))[:, None]
    lam_bar = jnp.exp(lam * dt)
    b = lax.complex(b_re.astype(f32), b_im.astype(f32))
    b_bar = ((lam_bar - 1.0) / lam)[..., None] * b
    bu = jnp.einsum('blgc,gpc->blgp', uf.astype(jnp.complex64), b_bar)
    a_elems = jnp.broadcast_to(lam_bar, bu.shape)
    _, states = lax.associative_scan(_ssm_binop, (a_elems, bu), axis=1)
    c = lax.complex(c_re.astype(f32), c_im.astype(f32))
    y = jnp.real(jnp.einsum('blgp,gcp->blgc', states, c))
    y = y + d_skip.astype(f32).reshape(N_GROUPS, SSM_GROUP) * uf
    z = jax.nn.gelu(y.reshape(bsz, length, D_MODEL)).astype(u.dtype)
    zw = z @ w_glu
    val, gate = zw[..., :D_MODEL], zw[..., D_MODEL:]
    return val * jax.nn.sigmoid(gate)

def shared_kv(h, kv_norm, w_kvf, b_f):
    bsz, length, _ = h.shape
    kvf = rmsnorm_2(h, kv_norm) @ w_kvf
    k = kvf[..., :ATTN_DIM].reshape(bsz, length, N_HEADS, HEAD_DIM_2).transpose(0, 2, 1, 3)
    v = kvf[..., ATTN_DIM:2 * ATTN_DIM].reshape(bsz, length, N_HEADS, HEAD_DIM_2).transpose(0, 2, 1, 3)
    f_logit = kvf[..., 2 * ATTN_DIM:].astype(jnp.float32) + b_f.astype(jnp.float32)
    log_f = jax.nn.log_sigmoid(f_logit)
    cum_log_f = jnp.cumsum(log_f, axis=1).transpose(0, 2, 1)
    return k, v, cum_log_f

def fox_attention(hn, wq, wo, k, v, cum_log_f):
    bsz, length, _ = hn.shape
    nb = length // Q_BLOCK
    q = (hn @ wq) * (HEAD_DIM_2 ** -0.5)
    q_blocks = q.reshape(bsz, nb, Q_BLOCK, N_HEADS, HEAD_DIM_2).transpose(1, 0, 3, 2, 4)
    f_blocks = cum_log_f.reshape(bsz, N_HEADS, nb, Q_BLOCK).transpose(2, 0, 1, 3)
    pos_q = jnp.arange(length, dtype=jnp.int32).reshape(nb, Q_BLOCK)
    pos_k = jnp.arange(length, dtype=jnp.int32)

    def one_block(args):
        qb, fq, pq = args
        s = jnp.einsum('bhqd,bhkd->bhqk', qb, k).astype(jnp.float32)
        s = s + fq[..., None] - cum_log_f[:, :, None, :]
        mask = pq[:, None] >= pos_k[None, :]
        s = jnp.where(mask[None, None], s, -jnp.inf)
        p = jax.nn.softmax(s, axis=-1)
        return jnp.einsum('bhqk,bhkd->bhqd', p.astype(v.dtype), v)

    o = lax.map(one_block, (q_blocks, f_blocks, pos_q))
    o = o.transpose(1, 0, 3, 2, 4).reshape(bsz, length, ATTN_DIM)
    return o @ wo

def second_inputs(seed: int = 0) -> dict:
    key = jax.random.key(seed)
    ks = jax.random.split(key, 20)
    f32 = jnp.float32

    def nrm(k, shape, scale):
        return scale * jax.random.normal(k, shape, f32)

    x = nrm(ks[0], (BATCH, SEQ, D_MODEL), 1.0)
    mix_norm = 1.0 + nrm(ks[1], (DEPTH_2, D_MODEL), 0.05)
    mlp_norm = 1.0 + nrm(ks[2], (DEPTH_2, D_MODEL), 0.05)
    mlp_w1 = nrm(ks[3], (DEPTH_2, D_MODEL, D_FF_2), D_MODEL ** -0.5)
    mlp_w2 = nrm(ks[4], (DEPTH_2, D_FF_2, D_MODEL), 0.5 * D_FF_2 ** -0.5)
    ssm_log_dt = jax.random.uniform(ks[5], (N_A_LAYERS, N_GROUPS), f32,
                                    math.log(DT_MIN), math.log(DT_MAX))
    ssm_a_re = -0.5 + nrm(ks[6], (N_A_LAYERS, N_GROUPS, SSM_STATE), 0.01)
    ssm_a_im = math.pi * jnp.arange(SSM_STATE, dtype=f32) + nrm(ks[7], (N_A_LAYERS, N_GROUPS, SSM_STATE), 0.01)
    ssm_b_re = nrm(ks[8], (N_A_LAYERS, N_GROUPS, SSM_STATE, SSM_GROUP), (2 * SSM_GROUP) ** -0.5)
    ssm_b_im = nrm(ks[9], (N_A_LAYERS, N_GROUPS, SSM_STATE, SSM_GROUP), (2 * SSM_GROUP) ** -0.5)
    ssm_c_re = nrm(ks[10], (N_A_LAYERS, N_GROUPS, SSM_GROUP, SSM_STATE), (2 * SSM_STATE) ** -0.5)
    ssm_c_im = nrm(ks[11], (N_A_LAYERS, N_GROUPS, SSM_GROUP, SSM_STATE), (2 * SSM_STATE) ** -0.5)
    ssm_d = nrm(ks[12], (N_A_LAYERS, D_MODEL), 1.0)
    ssm_w_glu = nrm(ks[13], (N_A_LAYERS, D_MODEL, 2 * D_MODEL), D_MODEL ** -0.5)
    kv_norm = 1.0 + nrm(ks[14], (D_MODEL,), 0.05)
    w_kvf = nrm(ks[15], (D_MODEL, 2 * ATTN_DIM + N_HEADS), D_MODEL ** -0.5)
    b_f = jax.random.uniform(ks[16], (N_HEADS,), f32, 0.5, 3.0)
    attn_wq = nrm(ks[17], (N_B_LAYERS, D_MODEL, ATTN_DIM), D_MODEL ** -0.5)
    attn_wo = nrm(ks[18], (N_B_LAYERS, ATTN_DIM, D_MODEL), ATTN_DIM ** -0.5)
    final_norm = 1.0 + nrm(ks[19], (D_MODEL,), 0.05)
    return {"x": x, "mix_norm": mix_norm, "mlp_norm": mlp_norm, "mlp_w1": mlp_w1, "mlp_w2": mlp_w2,
            "ssm_log_dt": ssm_log_dt, "ssm_a_re": ssm_a_re, "ssm_a_im": ssm_a_im,
            "ssm_b_re": ssm_b_re, "ssm_b_im": ssm_b_im, "ssm_c_re": ssm_c_re, "ssm_c_im": ssm_c_im,
            "ssm_d": ssm_d, "ssm_w_glu": ssm_w_glu, "kv_norm": kv_norm, "w_kvf": w_kvf, "b_f": b_f,
            "attn_wq": attn_wq, "attn_wo": attn_wo, "final_norm": final_norm}

def second_block(x, mix_norm, mlp_norm, mlp_w1, mlp_w2, ssm_log_dt, ssm_a_re, ssm_a_im,
              ssm_b_re, ssm_b_im, ssm_c_re, ssm_c_im, ssm_d, ssm_w_glu, kv_norm, w_kvf, b_f,
              attn_wq, attn_wo, final_norm):
    h = x
    k = v = cum_log_f = None
    for i in range(DEPTH_2):
        hn = rmsnorm_2(h, mix_norm[i])
        if i < N_A_LAYERS:
            h = h + s5_mixer(hn, ssm_log_dt[i], ssm_a_re[i], ssm_a_im[i], ssm_b_re[i], ssm_b_im[i],
                             ssm_c_re[i], ssm_c_im[i], ssm_d[i], ssm_w_glu[i])
        else:
            j = i - N_A_LAYERS
            h = h + fox_attention(hn, attn_wq[j], attn_wo[j], k, v, cum_log_f)
        h = h + sqrelu_mlp(rmsnorm_2(h, mlp_norm[i]), mlp_w1[i], mlp_w2[i])
        if i == N_A_LAYERS - 1:
            k, v, cum_log_f = shared_kv(h, kv_norm, w_kvf, b_f)
    return rmsnorm_2(h, final_norm)


def setup_inputs(seed=0):
    out = dict(first_inputs(seed))
    for name, value in second_inputs(seed + 1).items():
        if name != "x":
            out[name + "_2"] = value
    return out


def reference(
    x, mem, positions, norm_mix_g, w_in, w_out, conv_b_w, conv_b_b, ln_b_g, ln_b_b,
    norm_cross_g, norm_mem_g, w_q_cross, w_k_cross, w_v_cross, w_o_cross, norm_ffn_g, w_gate,
    w_up, ffn_conv_w, ffn_conv_b, w_down, norm_final_g, mix_norm_2, mlp_norm_2, mlp_w1_2,
    mlp_w2_2, ssm_log_dt_2, ssm_a_re_2, ssm_a_im_2, ssm_b_re_2, ssm_b_im_2, ssm_c_re_2,
    ssm_c_im_2, ssm_d_2, ssm_w_glu_2, kv_norm_2, w_kvf_2, b_f_2, attn_wq_2, attn_wo_2,
    final_norm_2,
):
    x = first_block(
        x, mem, positions, norm_mix_g, w_in, w_out, conv_b_w, conv_b_b, ln_b_g, ln_b_b,
        norm_cross_g, norm_mem_g, w_q_cross, w_k_cross, w_v_cross, w_o_cross, norm_ffn_g,
        w_gate, w_up, ffn_conv_w, ffn_conv_b, w_down, norm_final_g,
    )
    return second_block(
        x, mix_norm_2, mlp_norm_2, mlp_w1_2, mlp_w2_2, ssm_log_dt_2, ssm_a_re_2, ssm_a_im_2,
        ssm_b_re_2, ssm_b_im_2, ssm_c_re_2, ssm_c_im_2, ssm_d_2, ssm_w_glu_2, kv_norm_2,
        w_kvf_2, b_f_2, attn_wq_2, attn_wo_2, final_norm_2,
    )


_drawn_inputs = setup_inputs


def setup_inputs(seed=0):
    import zlib

    import numpy as np

    out = dict(_drawn_inputs(seed))
    spreads = {}
    factors = {'norm_mix_g': 3.052,
     'conv_b_b': 2.751,
     'ln_b_g': 4.911,
     'ln_b_b': 5.279,
     'norm_cross_g': 8.0,
     'norm_mem_g': 8.0,
     'norm_ffn_g': 3.635,
     'ffn_conv_b': 5.258,
     'ssm_a_re_2': 8.0,
     'ssm_b_re_2': 3.432,
     'ssm_b_im_2': 3.433,
     'ssm_c_re_2': 3.363,
     'ssm_c_im_2': 3.439}
    for name, (base, spread) in spreads.items():
        noise = np.random.default_rng([zlib.crc32(name.encode()), seed]).standard_normal(out[name].shape)
        drawn = base * np.exp(spread * noise) if base else spread * noise
        out[name] = __import__('jax').numpy.asarray(drawn.astype(out[name].dtype))
    for name, factor in factors.items():
        out[name] = (out[name] * factor).astype(out[name].dtype)
    return out
```

```python
from contextlib import ExitStack

import numpy as np
import concourse.bass as bass
from concourse import mybir

F32 = mybir.dt.float32
F32R = mybir.dt.float32r
I32 = mybir.dt.int32
ALU = mybir.AluOpType
ACT = mybir.ActivationFunctionType
AX = mybir.AxisListType.X

P = 128
T = 512
TB = T // P
D = 1024
KC = D // P
NMEM = 256
MB = NMEM // P
IDXH = 4
TOPK = 128
CONVW = 31
PAD = CONVW - 1
BCH = 4
DFF = 2816
FC = DFF // P
EPS = 1e-6
THETA = 500000.0
ROT = 16
NHEAD = 16
NCST = 4 * P + 1 + 2 * NHEAD
BIG = float(2.0 ** 100)
FAR = -1.0e30
TAKEN = -3.0e38
MAGIC = 12582912.0
PI_BELOW = 3.1415925
TWO_PI = (6.28125, 0.0019350051879882812, 6.283185307179586 - 6.28125 - 0.0019350051879882812)
LN2 = (0.693359375, float(np.log(2.0)) - 0.693359375)

FFN_GROUPS = [(g, min(8, FC - g)) for g in range(0, FC, 8)]
ORDER = [("glu", 8), ("in", 8), ("memk", 8), ("memv", 8), ("out", 8), ("qc", 8), ("oc", 8)]
for _g, _n in FFN_GROUPS:
    ORDER += [(f"ffn{_g}", 2 * _n), (f"down{_g}", 8)]
GROUPS = 4 * D // P // 8
_MLP = [[(f"{_n}{_l}{_g}", 8) for _g in range(GROUPS) for _n in ("up", "dn")] for _l in range(2)]
ORDER += [("s5glu", 16)] + _MLP[0] + [("kv", 16), ("wq", 8), ("wo", 8)] + _MLP[1]
START = {}
NUNITS = 0
for _name, _c in ORDER:
    START[_name] = NUNITS
    NUNITS += _c
COUNT = dict(ORDER)

VECTORS = [("norm_mix_g", 8, 0), ("norm_cross_g", 8, 0), ("norm_mem_g", 8, 0), ("norm_ffn_g", 8, 0),
           ("norm_final_g", 8, 0), ("mix_norm_2", 16, 0), ("mlp_norm_2", 16, 0), ("kv_norm_2", 8, 0),
           ("final_norm_2", 8, 0), ("ssm_d_2", 8, 0), ("conv_b_b", 4, 0), ("ln_b_g", 4, 0), ("ln_b_b", 4, 0),
           ("conv_b_w", 124, 1), ("ffn_conv_w", 66, 2), ("ffn_conv_b", 22, 2)]
ROWS = [0, 0, 0]
COLUMN = {}
for _name, _c, _t in VECTORS:
    COLUMN[_name] = (_t, ROWS[_t])
    ROWS[_t] += _c

NORMS = [("mix", 8), ("ln", 4), ("cross", 8), ("ffn", 8), ("final", 8), ("s5", 8), ("mlp0", 8), ("kv", 8), ("mlp1", 8),
         ("last", 8)]
NORM = {name: n for n, (name, _) in enumerate(NORMS)}
SQUARES = {name: sum(c for _, c in NORMS[:n]) for n, (name, _) in enumerate(NORMS)}
NOPERAND = {"mix": 0, "cross": 8, "ffn": 16, "mlp0": 24, "kv": 32, "wq": 40, "mlp1": 48}
HIDDEN = {"ffn": 0, "s5": FC, "mlp0": FC + KC, "mlp1": FC + KC + 8 * GROUPS}
TILES = {"sparse": 0, "cross": 32, "fox": 48}
PAIRS = {"sparse": 0, "cross": 4, "fox": 12}
HALVES = {"sparse": 1, "cross": 9, "fox": 17}


def constants():
    c = np.zeros((P, NCST), np.float32)
    c[:, 0:P] = np.eye(P)
    for m in range(P):
        if m % 64 < ROT // 2:
            c[m + ROT // 2, P + m] = -1.0
        elif m % 64 < ROT:
            c[m - ROT // 2, P + m] = 1.0
    q, k = np.meshgrid(np.arange(P), np.arange(P), indexing="ij")
    c[:, 2 * P:3 * P] = np.where(k > q, -BIG, 0.0)
    c[:, 3 * P:4 * P] = 1.0
    f = (np.float32(THETA) ** (-np.arange(0, ROT, 2, dtype=np.float32) / np.float32(ROT))).astype(np.float32)
    for m in range(P):
        if m % 64 < ROT:
            c[m, 4 * P] = f[m % (ROT // 2)]
    for h in range(NHEAD):
        c[h:64:32, 4 * P + 1 + h] = 1.0
        c[64 + h::32, 4 * P + 1 + NHEAD + h] = 1.0
    return c


def build_program(nc, A, out):
    ctx = ExitStack()
    with ctx:
        first = (nc.sbuf_base + 127) // 128 * 128

        def at(name, shape, dt, offset):
            return nc.alloc_sbuf_tensor_at(name, shape, dt, offset=first + offset)

        def bank(name):
            return ctx.enter_context(nc.psum_tensor(name, [P, 512], F32))

        def sem(name):
            return ctx.enter_context(nc.semaphore(name))

        X = at("X", [P, KC, T], F32, 0)
        PH = at("PH", [P, KC, T], F32R, 16384)
        PL = at("PL", [P, KC, T], F32R, 32768)
        QH = at("QH", [P, KC, T], F32R, 49152)
        QL = at("QL", [P, KC, T], F32R, 65536)
        RAW = at("RAW", [P, 2, KC, P], F32, 81920)
        WH = at("WH", [P, 2, KC, P], F32R, 90112)
        WL = at("WL", [P, 2, KC, P], F32R, 98304)
        QT = at("QT", [P, KC, T], F32, 106496)
        KT = at("KT", [P, KC, T], F32, 122880)
        VT = at("VT", [P, KC, T], F32, 139264)
        PTH = at("PTH", [P, TB, T], F32R, 155648)
        PTL = at("PTL", [P, TB, T], F32R, 163840)
        E = at("E", [P, 2, T], F32, 172032)
        QSH = at("QSH", [P, T], F32R, 176128)
        QSL = at("QSL", [P, T], F32R, 178176)
        KSH = at("KSH", [P, T], F32R, 180224)
        KSL = at("KSL", [P, T], F32R, 182272)
        VS = at("VS", [P, T], F32, 184320)
        VSH = at("VSH", [P, TB, 2, P], F32R, 186368)
        VSL = at("VSL", [P, TB, 2, P], F32R, 190464)
        CST = at("CST", [P, NCST], F32, 194560)
        IDR = at("IDR", [P, P], F32R, 196768)
        TRIR = at("TRIR", [P, P], F32R, 197280)
        RS = at("RS", [P, T], F32, 197792)
        SSQ = at("SSQ", [P, T], F32, 199840)
        SQ = at("SQ", [P, 2, T], F32, 201888)
        DIAG = at("DIAG", [P, T], F32, 205984)
        VEC = at("VEC", [P, 3, P], F32, 208032)
        V4 = at("V4", [P, 4], F32, 209568)
        SD4 = at("SD4", [P, 4], F32, 209600)
        R4 = at("R4", [P, 4], F32, 209632)
        WI = at("WI", [P, TB, 4], F32, 209664)
        M8 = at("M8", [P, 3, 8], F32, 209728)
        NMX = at("NMX", [P, 2, 1], F32, 209824)
        SUM = at("SUM", [P, 2, 1], F32, 209856)
        REC = at("REC", [P, 2, 1], F32, 209888)
        XROW = at("XROW", [P, TB, D], F32, 106496)
        MROW = at("MROW", [P, MB, D], F32, 122880)
        VROW = at("VROW", [P, 3, P], F32, 155648)
        POSI = at("POSI", [P, T], I32, 163840)
        MSQ = at("MSQ", [P, D], F32, 172032)
        DS = at("DS", [P, KC, T], F32, 106496)
        KM = at("KM", [P, KC, NMEM], F32, 122880)
        VM = at("VM", [P, KC, NMEM], F32, 131072)
        U = at("U", [P, BCH, PAD + T], F32, 139264)
        COS = at("COS", [P, T], F32, 147968)
        SIN = at("SIN", [P, T], F32, 150016)
        SC = at("SC", [P, 3, T], F32, 16384)
        SEL = at("SEL", [P, TB, T], F32R, 22528)
        KD = at("KD", [P, 2, T], F32, 30720)
        CV = at("CV", [P, BCH, T], F32, 34816)
        G = at("G", [P, 2 + T], F32, 155648)
        H1 = at("H1", [P, T], F32, 157760)
        H2 = at("H2", [P, T], F32, 159808)
        JP = 32
        BB = at("BB", [P, 2, JP, 16], F32, 139264)
        CC = at("CC", [P, 2, JP, 16], F32, 143360)
        PW = at("PW", [P, 2, 9, JP], F32, 147456)
        UT = at("UT", [P, 2, JP], F32, 149760)
        RHO8 = at("RHO8", [P, JP], F32, 150016)
        LAM = at("LAM", [P, 3, JP], F32, 150144)
        SW = at("SW", [P, 10, JP], F32, 150528)
        S5ROW = at("S5ROW", [JP, 3, P], F32, 151808)
        POW2 = at("POW2", [P, JP], I32, 153600)
        DTROW = at("DTROW", [JP, 2], F32, 153344)
        ET = at("ET", [P, 2, JP, 64], F32, 122880)
        U5 = at("U5", [P, KC, T], F32, 106496)
        CROW = at("CROW", [P, 2, KC, 2, 64], F32, 16384)
        BRAW = at("BRAW", [P, 2, JP, 16], F32, 24576)
        BT = at("BT", [P, 2, JP, 16], F32, 28672)
        W1T = at("W1T", [P, 8, 2, 4, 2, 16], F32, 16384)
        W1 = at("W1", [P, 16, P], F32, 24576)
        KB = at("KB", [P, 2, 8, P], F32, 32768)
        SPV = at("SPV", [P, 2, 4, 64], F32, 40960)
        VR = at("VR", [P, 2, 4, 64], F32, 43008)
        WR = at("WR", [P, 2, 4, 64], F32, 45056)
        CL = at("CL", [P, 2, 2, 9, 4, 2, 16], F32, 155648)
        GT = at("GT", [P, 2, 9, 4, 16], F32, 174080)
        RHOT = at("RHOT", [P, 4, 64], F32, 178688)
        RT = at("RT", [P, 2, 4, 64], F32, 179712)
        YC = at("YC", [P, 2, T], F32, 181760)
        UC = at("UC", [P, 2, T], F32, 185856)
        CQH = at("CQH", [P, 2, T], F32R, 176128)
        CQL = at("CQL", [P, 2, T], F32R, 180224)
        CVS = at("CVS", [P, 2, NMEM], F32, 184320)
        CKH = at("CKH", [P, 2, NMEM], F32R, 186368)
        CKL = at("CKL", [P, 2, NMEM], F32R, 188416)
        CVH = at("CVH", [P, MB, 2 * P], F32R, 190464)
        CVL = at("CVL", [P, MB, 2 * P], F32R, 192512)
        MH = QH[:, 0:4, :].rearrange("p a (b n) -> p (a b) n", n=NMEM)
        ML = QL[:, 0:4, :].rearrange("p a (b n) -> p (a b) n", n=NMEM)
        FWR = at("FWR", [P, KC, P], F32, 163840)
        FWH = at("FWH", [P, KC, P], F32R, 167936)
        FWL = at("FWL", [P, KC, P], F32R, 176128)
        FZ = at("FZ", [P, T], F32, 172032)
        F = at("F", [P, T], F32, 174080)
        BF = at("BF", [P, 1], F32, 209888)
        LQ = at("LQ", [P, 2, T], F32R, 49152)
        RK = at("RK", [P, 2, T], F32R, 53248)
        LF = at("LF", [P, T], F32R, 61440)
        RF = at("RF", [P, T], F32R, 63488)
        FH = at("FH", [P, T], F32R, 57344)
        FL = at("FL", [P, T], F32R, 59392)
        YROW = at("YROW", [P, TB, D], F32, 106496)
        HOT = CST[:, 4 * P + 1:NCST]
        IDENT, ROTM, TRI, ONES = (CST[:, i * P:(i + 1) * P] for i in range(4))
        FREQ = CST[:, 4 * P:4 * P + 1]
        TA, TB_ = E[:, 0, :], E[:, 1, :]

        def column(name, i):
            name, first = name if isinstance(name, tuple) else (name, 0)
            t, base = COLUMN[name][0], COLUMN[name][1] + first
            return VEC[:, t, bass.ds(base + i, 1)]

        ACC = [bank("ACC0"), bank("ACC1")]
        ST = bank("ST")
        FOUR = ctx.enter_context(nc.psum_tensor("FOUR", [P, 4, 512], F32))
        S = [FOUR[:, 0, :], FOUR[:, 1, :]]
        TR = [FOUR[:, 2, :], FOUR[:, 3, :]]
        O = bank("O")

        w_landed = [sem("w_landed0"), sem("w_landed1")]
        w_hi = sem("w_hi")
        w_lo = sem("w_lo")
        unit_done = sem("unit_done")
        unit_out = sem("unit_out")
        cst_in = sem("cst_in")
        vec_in = sem("vec_in")
        x_in = sem("x_in")
        mem_in = sem("mem_in")
        cst_r = sem("cst_r")
        vec_t = sem("vec_t")
        vec_c = sem("vec_c")
        x_t = sem("x_t")
        x_ready = sem("x_ready")
        op_hi = sem("op_hi")
        op_lo = sem("op_lo")
        sq_ready = sem("sq_ready")
        sq_used = sem("sq_used")
        st_sum, st_var, st_std, st_diag, st_bc, st_rs = (
            sem(n) for n in ("st_sum", "st_var", "st_std", "st_diag", "st_bc", "st_rs"))
        mem_sq, mem_var, mem_std, mem_scaled, mem_t, mem_hi, mem_lo = (
            sem(n) for n in ("mem_sq", "mem_var", "mem_std", "mem_scaled", "mem_t", "mem_hi", "mem_lo"))
        pos_in, ang, angc, tables = sem("pos_in"), sem("ang"), sem("angc"), sem("tables")
        u_zero, gate_raw, gate_sig = sem("u_zero"), sem("gate_raw"), sem("gate_sig")
        rot_done, rot_used, rope_cos, rope_done = (
            sem(n) for n in ("rot_done", "rot_used", "rope_cos", "rope_done"))
        kd_in = [sem("kd_in0"), sem("kd_in1")]
        wi_t, wi_in, v_t, pad_zero, v_hi, v_lo = (sem(n) for n in ("wi_t", "wi_in", "v_t", "pad_zero", "v_hi", "v_lo"))
        index_mm, index_relu, index_sum, index_masked, sel_ready = (
            sem(n) for n in ("index_mm", "index_relu", "index_sum", "index_masked", "sel_ready"))
        conv_done, mean_sum, centred, ln_scaled, silu_done, branch_hi, branch_lo = (
            sem(n) for n in ("conv_done", "mean_sum", "centred", "ln_scaled", "silu_done", "branch_hi", "branch_lo"))
        g_zero, gate_conv, gate_act, hid_ready, hid_hi, hid_lo = (
            sem(n) for n in ("g_zero", "gate_conv", "gate_act", "hid_ready", "hid_hi", "hid_lo"))
        row_in, c_in, b_in, row_t, row_out, c_t, c_out = (
            sem(n) for n in ("s5_row_in", "s5_c_in", "s5_b_in", "s5_row_t", "s5_row_out", "s5_c_t", "s5_c_out"))
        angle_ready, sin_cos, den_inv, params = (
            sem(n) for n in ("angle_ready", "sin_cos", "den_inv", "s5_params"))
        zeroed, gen_ready, w1_t, w1_in, k_mm, kb_in, l_mm, l_used, sp_ready, y_mm, y_out, gelu_done, rho_ready = (
            sem(n) for n in ("s5_zeroed", "gen_ready", "w1_t", "w1_in", "k_mm", "kb_in", "l_mm", "l_used", "sp_ready",
                             "y_mm", "y_out", "gelu_done", "rho_ready"))
        normed_x, u5_ready, uc_ready = sem("normed_x"), sem("u5_ready"), sem("uc_ready")
        glu_out = sem("glu_out")
        fw_zero, fw_in, fw_hi, fw_lo, f_mm, f_abs, f_exp, f_ln, f_sum, f_ready, hot = (
            sem(n) for n in ("fw_zero", "fw_in", "fw_hi", "fw_lo", "f_mm", "f_abs", "f_exp", "f_ln", "f_sum", "f_ready",
                             "hot"))
        y_normed, y_t, y_even, y_odd, stored = (sem(n) for n in ("y_normed", "y_t", "y_even", "y_odd", "stored"))
        q_hi = sem("q_hi")
        q_lo = sem("q_lo")
        s_ready = sem("s_ready")
        mx_ready = sem("mx_ready")
        e_done = sem("e_done")
        e_scaled = sem("e_scaled")
        t_ready = sem("t_ready")
        pt_hi = sem("pt_hi")
        pt_lo = sem("pt_lo")
        pv_done = sem("pv_done")
        cvs_in, k_lo = sem("cvs_in"), sem("k_lo")
        o_hi, o_lo = sem("o_hi"), sem("o_lo")

        def weights(name):
            return A[name].rearrange("l (c p) n -> (l c) p n", p=P).rearrange("c p n -> p c n")

        w_in, w_out = weights("w_in"), weights("w_out")
        w_k, w_v = weights("w_k_cross"), weights("w_v_cross")
        w_qc, w_oc = weights("w_q_cross"), weights("w_o_cross")
        w_gate, w_up, w_down = weights("w_gate"), weights("w_up"), weights("w_down")
        w_glu, w_q, w_o = weights("ssm_w_glu_2"), weights("attn_wq_2"), weights("attn_wo_2")
        w_kvf = A["w_kvf_2"].rearrange("(c p) n -> p c n", p=P)
        w_up2 = [A["mlp_w1_2"][l].rearrange("(c p) n -> p c n", p=P) for l in range(2)]
        w_down2 = [A["mlp_w2_2"][l].rearrange("(c p) n -> p c n", p=P) for l in range(2)]
        IN_COLS = [896, 640, 768, 512, 0, 128, 256, 384]
        GA, GG = 964, 1476

        def unit_at(name, i, s, g=0):
            return START[name] + 2 * i + s

        block = ctx.enter_context(nc.Block())

        @block.sync
        def _(sp):
            def load(u, s, src):
                if not isinstance(u, int) or u >= 2:
                    sp.wait_ge(w_lo, u - 1)
                sp.dma_start(RAW[:, s, 0:src.shape[1], :], src).then_inc(w_landed[s], 16)

            sp.dma_start(CST[:], A["constants"]).then_inc(cst_in, 16)
            sp.dma_start(XROW[:], A["x"][0].rearrange("(b p) d -> p b d", p=P)).then_inc(x_in, 16)
            sp.dma_start(MROW[:], A["mem"][0].rearrange("(b p) d -> p b d", p=P)).then_inc(mem_in, 16)
            for s in range(2):
                load(s, s, w_in[:, :, (GA, GG)[s]:(GA, GG)[s] + P])
            with sp.Fori(1, 4) as i:
                for s in range(2):
                    load(unit_at("glu", i, s), s, w_in[:, :, bass.ds(i * P + (GA, GG)[s], P)])
            for j, c in enumerate(IN_COLS):
                load(START["in"] + j, j % 2, w_in[:, :, c:c + P])
            for name, w in (("memk", w_k), ("memv", w_v), ("out", w_out), ("qc", w_qc), ("oc", w_oc)):
                with sp.Fori(0, 4) as i:
                    for s in range(2):
                        load(unit_at(name, i, s), s, w[:, :, bass.ds(i * 2 * P + s * P, P)])
                if name == "qc":
                    sp.wait_ge(conv_done, BCH)
                    for j, x in enumerate(("ssm_a_re_2", "ssm_a_im_2")):
                        sp.dma_start(S5ROW[:, j, :], A[x][0].rearrange("(j g) p -> j (g p)", g=2)).then_inc(row_in, 16)
                    sp.dma_start(DTROW[:], A["ssm_log_dt_2"][0].rearrange("(j g) -> j g", g=2)).then_inc(row_in, 16)
                    sp.wait_ge(unit_done, START["oc"])
                    for ri, x in enumerate(("ssm_b_re_2", "ssm_b_im_2")):
                        sp.dma_start(BRAW[:, ri], A[x][0].rearrange("(j g) p c -> (g p) j c", g=2)).then_inc(b_in, 16)
                    for ri, x in enumerate(("ssm_c_re_2", "ssm_c_im_2")):
                        rows = A[x][0].rearrange("(k g) c p -> (g c) k p", k=KC)
                        for twice in range(2):
                            sp.dma_start(CROW[:, ri, :, twice, :], rows).then_inc(c_in, 16)
            for g, n in FFN_GROUPS:
                with sp.Fori(0, n) as i:
                    for s, w in enumerate((w_gate, w_up)):
                        load(unit_at(f"ffn{g}", i, s), s, w[:, :, bass.ds(i * P + g * P, P)])
                with sp.Fori(0, 4) as i:
                    for s in range(2):
                        load(unit_at(f"down{g}", i, s), s, w_down[:, g:g + n, bass.ds(i * 2 * P + s * P, P)])
            def loads(name, n, w, rows=slice(0, KC), first=0):
                with sp.Fori(0, n // 2) as i:
                    for s in range(2):
                        load(unit_at(name, i, s), s, w[:, rows, bass.ds(i * 2 * P + (s * P + first), P)])

            def mlp(l):
                for g in range(GROUPS):
                    loads(f"up{l}{g}", 8, w_up2[l], first=g * KC * P)
                    loads(f"dn{l}{g}", 8, w_down2[l], slice(g * KC, (g + 1) * KC))

            with sp.Fori(0, 8) as i:
                for s in range(2):
                    load(unit_at("s5glu", i, s), s, w_glu[:, :, bass.ds(i * P + s * D, P)])
            mlp(0)
            sp.wait_ge(fw_zero, 1)
            for j in range(4):
                sp.dma_start(FWR[:, :, 32 * j:32 * j + NHEAD], w_kvf[:, :, 2 * D:2 * D + NHEAD]).then_inc(fw_in, 16)
                sp.dma_start(BF[32 * j:32 * j + NHEAD, :], A["b_f_2"].rearrange("(h o) -> h o", o=1)).then_inc(fw_in, 16)
            loads("kv", 16, w_kvf)
            loads("wq", 8, w_q)
            loads("wo", 8, w_o)
            mlp(1)
            for c in range(KC):
                sp.wait_ge((y_even, y_odd)[c % 2], c // 2 + 1)
                sp.dma_start(out[0].rearrange("(b p) d -> p b d", p=P)[:, :, c * P:(c + 1) * P],
                             YROW[:, :, c * P:(c + 1) * P]).then_inc(stored, 16)
            sp.wait_ge(stored, 16 * KC)

        @block.scalar
        def _(act):
            def round_weights(u, s):
                act.wait_ge(w_landed[s], (u - s) * 8 + 16)
                if not isinstance(u, int) or u >= 2:
                    act.wait_ge(unit_done, u - 1)
                act.activation(WH[:, s], RAW[:, s], ACT.Copy).then_inc(w_hi, 1)

            def prepare(norm, c, gain, hi, s, ready):
                square_free(norm, c)
                act.wait_ge(*ready)
                act.activation(hi, X[:, bass.ds(c, 1), :], ACT.Copy, scale=column(gain, c)).then_inc(op_hi, 1)
                act.activation(SQ[:, s, :], X[:, bass.ds(c, 1), :], ACT.Square).then_inc(sq_ready, 1)

            def square_free(norm, c):
                if not isinstance(c, int) or SQUARES[norm] + c >= 2:
                    act.wait_ge(sq_used, SQUARES[norm] + c - 1)

            def square(norm, c, x, s):
                square_free(norm, c)
                act.activation(SQ[:, s, :], x[:, bass.ds(c, 1), :], ACT.Square).then_inc(sq_ready, 1)

            def standard_deviation(norm):
                act.wait_ge(st_var, NORM[norm] + 1)
                act.activation(SD4[:], V4[:], ACT.Sqrt).then_inc(st_std, 1)

            act.dma_start(POSI[:], A["positions"].to_broadcast([P, T])).then_inc(pos_in, 16)
            for name, rows, t in VECTORS:
                r = COLUMN[name][1]
                flat = A[name] if len(A[name].shape) == 1 else A[name].rearrange(
                    "a b -> (a b)") if len(A[name].shape) == 2 else A[name].rearrange("a b c -> (a b c)")
                act.dma_start(VROW[r:r + rows, t, :], flat.rearrange("(r p) -> r p", p=P)).then_inc(vec_in, 16)
            act.wait_ge(cst_in, 16)
            act.activation(IDR[:], IDENT, ACT.Copy).then_inc(cst_r, 1)
            act.activation(TRIR[:], TRI, ACT.Copy).then_inc(cst_r, 1)
            round_weights(0, 0)
            act.wait_ge(mem_in, 16)
            for b in range(MB):
                act.activation(MSQ[:], MROW[:, b, :], ACT.Square, accum_out=V4[:, b:b + 1]).then_inc(mem_sq, 1)
                act.drain()
            act.wait_ge(mem_var, 1)
            act.activation(SD4[:, 0:MB], V4[:, 0:MB], ACT.Sqrt).then_inc(mem_std, 1)
            act.wait_ge(vec_c, 1)
            for c in range(KC):
                prepare("mix", c, "norm_mix_g", PH[:, c, :], c % 2, (x_ready, c + 1))
            for c in range(KC):
                act.wait_ge(mem_t, c + 1)
                act.activation(MH[:, c, :], S[c % 2][:, 0:NMEM], ACT.Copy, scale=column("norm_mem_g", c))\
                   .then_inc(mem_hi, 1)
            act.wait_ge(ang, 1)
            act.activation(SIN[:], SIN[:], ACT.Sin).then_inc(tables, 1)
            act.activation(COS[:], COS[:], ACT.Sin).then_inc(tables, 1)

            def glu(i):
                for s in range(2):
                    round_weights(unit_at("glu", i, s) + 1, 1 - s)
                    if s == 0 and isinstance(i, int):
                        standard_deviation("mix")
                act.wait_ge(gate_raw, i + 1)
                act.activation(TB_, TB_, ACT.Sigmoid).then_inc(gate_sig, 1)

            glu(0)
            with act.Fori(1, 4) as i:
                glu(i)
            for u in range(START["in"], START["memk"]):
                round_weights(u + 1, (u + 1) % 2)
            for j, slot in ((0, 1), (1, 4)):
                act.wait_ge(rope_done, slot)
                act.dma_start(KD[64:P, j, :], KD[0:64, j, :]).then_inc(kd_in[j], 16)
            act.wait_ge(v_t, 1)
            act.wait_ge(pad_zero, 2)
            for half in range(2):
                act.activation(VSH[:, :, half, half * 64:half * 64 + 64],
                               S[0][:, 0:TB * 64].rearrange("p (b f) -> p b f", b=TB), ACT.Copy).then_inc(v_hi, 1)
            act.wait_ge(kd_in[1], 16)
            act.activation(KSH[:], KD[:, 1, :], ACT.Copy).then_inc(v_hi, 1)
            act.wait_ge(rope_done, 8)
            for n in range(3 * IDXH):
                nk = (n // IDXH + 2) * P
                act.wait_ge(index_mm, n + 1)
                if n >= 2:
                    act.wait_ge(index_sum, n - 1)
                act.activation(E[:, n % 2, 0:nk], S[n % 2][:, 0:nk], ACT.Relu).then_inc(index_relu, 1)
            for name, to in (("memk", KM), ("memv", VM)):
                with act.Fori(0, 4) as i:
                    for s in range(2):
                        u = unit_at(name, i, s)
                        round_weights(u + 1, 1 - s)
                        act.wait_ge(unit_done, u + 1)
                        act.activation(to[:, bass.ds(2 * i + s, 1), :], ACC[s][:, 0:NMEM], ACT.Copy)\
                           .then_inc(unit_out, 1)

            def exponentials(n, t, nk):
                act.wait_ge(mx_ready, n + 1)
                act.wait_ge(t_ready, n + 1)
                act.activation(E[:, t % 2, 0:nk], S[t % 2][:, 0:nk], ACT.Exp, bias=NMX[:, t % 2, :],
                               accum_out=SUM[:, t % 2, :]).then_inc(e_done, 1)

            def turned_high(n, t, qb, kb, free=None):
                act.wait_ge(t_ready, n + 3)
                if free is not None:
                    act.wait_ge(pv_done, free)
                act.activation(PTH[:, 0:kb, qb * P:(qb + 1) * P],
                               TR[t % 2][:, 0:kb * P].rearrange("p (k q) -> p k q", q=P), ACT.Copy).then_inc(pt_hi, 1)

            def attend(kind, c):
                n = TILES[kind] + 8 * c
                for t in range(8):
                    exponentials(n + t, t, (t % 4 + 1) * P)
                    if t:
                        turned_high(n + t - 1, t - 1, (t - 1) % 4, (t - 1) % 4 + 1,
                                    HALVES[kind] + 2 * c + (t - 1) // 4 if (t - 1) % 4 == 0 else None)
                turned_high(n + 7, 7, 3, 4)

            def high_out(bank_, to, k):
                act.wait_ge(pv_done, k)
                act.activation(to, bank_[:], ACT.Copy).then_inc(o_hi, 1)

            def hidden(ready, k, to, value, hi=QH):
                act.wait_ge(ready, value)
                act.activation(hi[:, bass.ds(k, 1), :], to, ACT.Copy).then_inc(hid_hi, 1)

            act.sem_inc(e_done, 2)
            with act.Fori(0, 4) as c:
                act.activation(QSH[:], DS[:, bass.ds(c + 4, 1), :], ACT.Copy).then_inc(q_hi, 1)
                attend("sparse", c)
                high_out(O, QH[:, bass.ds(c, 1), :], HALVES["sparse"] + 2 * c + 2)
            for c in range(BCH):
                act.wait_ge(centred, c + 1)
                square("ln", c, CV, c % 2)
            standard_deviation("ln")
            for c in range(BCH):
                act.wait_ge(ln_scaled, c + 1)
                act.activation(CV[:, c, :], CV[:, c, :], ACT.Silu, bias=column("ln_b_b", c),
                               scale=column("ln_b_g", c)).then_inc(silu_done, 1)
                act.wait_ge(silu_done, c + 1)
                act.activation(QH[:, 4 + c, :], CV[:, c, :], ACT.Copy).then_inc(branch_hi, 1)

            def residual(name, norm, gain, hi, i, g=None):
                for s in range(2):
                    u = START[name] + 2 * i + s
                    c = 2 * i + s
                    round_weights(u + 1, 1 - s)
                    prepare(norm, c, gain, hi[:, bass.ds(c, 1), :], s, (unit_out, u + 1))

            residual("out", "cross", "norm_cross_g", PH, 0)
            with act.Fori(1, 4) as i:
                residual("out", "cross", "norm_cross_g", PH, i)

            def plain(name, i, norm=None):
                for s in range(2):
                    round_weights(unit_at(name, i, s) + 1, 1 - s)
                    if s == 0 and norm:
                        standard_deviation(norm)

            plain("qc", 0, "cross")
            with act.Fori(1, 4) as i:
                plain("qc", i)
            act.wait_ge(angle_ready, 1)
            act.activation(SW[:, 4, :], SW[:, 1, :], ACT.Sin)
            act.activation(SW[:, 6, :], SW[:, 9, :], ACT.Sin).then_inc(sin_cos, 1)
            with act.Fori(0, 4) as h:
                n = TILES["cross"] + 4 * h
                act.activation(CQH[:], QT[:, bass.ds(2 * h, 2), :], ACT.Copy).then_inc(q_hi, 1)
                act.activation(CKH[:], KM[:, bass.ds(2 * h, 2), :], ACT.Copy).then_inc(q_hi, 1)
                act.wait_ge(v_t, h + 2)
                act.activation(CVH[:], O[:].rearrange("p (b f) -> p b f", b=MB), ACT.Copy).then_inc(v_hi, 1)
                for t in range(4):
                    exponentials(n + t, t, NMEM)
                    if t:
                        turned_high(n + t - 1, t - 1, t - 1, MB, HALVES["cross"] + 2 * h if t == 1 else None)
                turned_high(n + 3, 3, 3, MB)
                for m in range(2):
                    high_out((O, ST)[m], QH[:, bass.ds(2 * h + m, 1), :], HALVES["cross"] + 2 * h + m + 1)
            residual("oc", "ffn", "norm_ffn_g", PH, 0)
            with act.Fori(1, 4) as i:
                residual("oc", "ffn", "norm_ffn_g", PH, i)
            for g, n in FFN_GROUPS:
                def ffn(i):
                    for s in range(2):
                        round_weights(unit_at(f"ffn{g}", i, s) + 1, 1 - s)
                        if s == 0 and isinstance(i, int):
                            standard_deviation("ffn")
                    act.wait_ge(gate_conv, g + i + 1)
                    act.activation(H1[:], H1[:], ACT.Silu).then_inc(gate_act, 1)
                    hidden(hid_ready, i, H2[:], g + i + 1)

                if g == 0:
                    ffn(0)
                with act.Fori(g == 0, n) as i:
                    ffn(i)
                with act.Fori(0, 4) as i:
                    for s in range(2):
                        u = unit_at(f"down{g}", i, s)
                        round_weights(u + 1, 1 - s)
                        if g == FFN_GROUPS[-1][0]:
                            act.wait_ge(unit_out, u + 1)
                            square("final", 2 * i + s, X, s)
            standard_deviation("final")
            for c in range(KC):
                act.wait_ge(normed_x, c + 1)
                square("s5", c, X, c % 2)
            standard_deviation("s5")

            def mixer_input(c, b):
                act.wait_ge(u5_ready, c + 1)
                if not isinstance(c, int) or c >= 2:
                    act.wait_ge(y_mm, c - 1)
                act.activation(UC[:, b, :], U5[:, bass.ds(c, 1), :], ACT.Copy).then_inc(uc_ready, 1)

            def mixer(c, b, more):
                if more:
                    for k in range(4):
                        act.wait_ge(w1_t, 4 * c + 4 + k + 1)
                        if k == 0:
                            act.wait_ge(l_mm, c + 1)
                        act.activation(W1[:, 4 * k:4 * k + 4, :], ACC[k % 2][:].rearrange("p (a b) -> p a b", b=P),
                                       ACT.Copy).then_inc(w1_in, 1)
                act.wait_ge(y_out, c + 1)
                act.activation(YC[:, b, :], YC[:, b, :], ACT.Gelu_apprx_tanh).then_inc(gelu_done, 1)
                hidden(gelu_done, c, YC[:, b, :], c + 1)
                if not isinstance(c, int):
                    mixer_input(c + 2, b)

            for c in range(2):
                mixer_input(c, c)
            for k in range(4):
                act.wait_ge(w1_t, k + 1)
                act.activation(W1[:, 4 * k:4 * k + 4, :], ACC[k % 2][:].rearrange("p (a b) -> p a b", b=P),
                               ACT.Copy).then_inc(w1_in, 1)
            with act.Fori(0, 3) as i:
                for b in range(2):
                    mixer(2 * i + b, b, True)
            mixer(6, 0, True)
            mixer(7, 1, False)

            with act.Fori(0, 4) as i:
                for b in range(2):
                    c = 2 * i + b
                    for s in range(2):
                        round_weights(unit_at("s5glu", c, s) + 1, 1 - s)
                    act.wait_ge(unit_done, unit_at("s5glu", c, 1) + 1)
                    act.activation(TB_, ACC[1][:], ACT.Sigmoid).then_inc(gate_sig, 1)
                    prepare("mlp0", c, "mlp_norm_2", PH[:, bass.ds(c, 1), :], b, (glu_out, c + 1))

            def mlp(l, hi, following):
                norm = f"mlp{l}"
                for g in range(GROUPS):
                    def up(i):
                        for s in range(2):
                            round_weights(unit_at(f"up{l}{g}", i, s) + 1, 1 - s)
                            if s == 0 and isinstance(i, int):
                                standard_deviation(norm)
                            hidden(hid_ready, 2 * i + s, (H1, H2)[s][:], HIDDEN[norm] - KC + g * KC + 2 * i + s + 1, hi)

                    if g == 0:
                        up(0)
                    with act.Fori(g == 0, 4) as i:
                        up(i)
                    if g < GROUPS - 1:
                        with act.Fori(0, 4) as i:
                            for s in range(2):
                                round_weights(unit_at(f"dn{l}{g}", i, s) + 1, 1 - s)
                following()

            def mlp0_end():
                with act.Fori(0, 4) as i:
                    residual(f"dn0{GROUPS - 1}", "kv", "kv_norm_2", PH, i)

            def mlp1_end():
                def down(i, last):
                    for s in range(2):
                        u = unit_at(f"dn1{GROUPS - 1}", i, s)
                        if s == 0 or not last:
                            round_weights(u + 1, 1 - s)
                        act.wait_ge(unit_out, u + 1)
                        square("last", 2 * i + s, X, s)

                with act.Fori(0, 3) as i:
                    down(i, False)
                down(3, True)

            mlp(0, QH, mlp0_end)
            act.wait_ge(fw_in, 128)
            act.activation(FWH[:], FWR[:], ACT.Copy).then_inc(fw_hi, 1)

            def kv(i, b):
                c = 2 * i + b
                for s in range(2):
                    round_weights(unit_at("kv", c, s) + 1, 1 - s)
                    if s == 0 and isinstance(c, int) and c == 0:
                        standard_deviation("kv")
                if b == 0 and isinstance(i, int):
                    act.wait_ge(unit_done, START["kv"])
                act.activation(QH[:, bass.ds(c, 1), :], X[:, bass.ds(c, 1), :], ACT.Copy,
                               scale=column(("mix_norm_2", KC), c)).then_inc(op_hi, 1)

            kv(0, 0)
            kv(0, 1)
            with act.Fori(1, 4) as i:
                for b in range(2):
                    kv(i, b)
            act.wait_ge(f_abs, 1)
            act.activation(F[:], F[:], ACT.Exp, scale=-1.0).then_inc(f_exp, 1)
            act.wait_ge(f_exp, 1)
            act.activation(F[:], F[:], ACT.Ln, bias=ONES[:, 0:1]).then_inc(f_ln, 1)
            with act.Fori(0, 4) as i:
                plain("wq", i)
            act.wait_ge(unit_done, START["wo"])
            act.wait_ge(f_sum, 1)
            act.activation(FH[:], F[:], ACT.Copy).then_inc(f_ready, 1)
            act.wait_ge(f_ready, 1)
            act.activation(RF[0:32, :], FH[0:32, :].bitcast(F32), ACT.Copy, scale=-1.0)
            act.activation(LF[64:96, :], FH[64:96, :].bitcast(F32), ACT.Copy)
            act.drain().then_inc(f_ready, 1)
            with act.Fori(0, 8) as c:
                act.activation(QSH[:], QT[:, bass.ds(c, 1), :], ACT.Copy).then_inc(q_hi, 1)
                act.activation(KSH[:], KT[:, bass.ds(c, 1), :], ACT.Copy).then_inc(q_hi, 1)
                act.wait_ge(v_t, 6 + c)
                for half in range(2):
                    act.activation(VSH[:, :, half, half * 64:half * 64 + 64],
                                   O[:].rearrange("p (b h f) -> p b h f", b=TB, h=2)[:, :, half, :], ACT.Copy)\
                       .then_inc(v_hi, 1)
                attend("fox", c)
                high_out(O, PH[:, bass.ds(c, 1), :], HALVES["fox"] + 2 * c + 2)
            with act.Fori(0, 4) as i:
                residual("wo", "mlp1", ("mlp_norm_2", KC), QH, i)
            mlp(1, PH, mlp1_end)
            standard_deviation("last")
            for c in range(0, KC, 2):
                act.wait_ge(y_t, c + 1)
                act.activation(YROW[:, :, c * P:(c + 1) * P], TR[0][:].rearrange("p (b f) -> p b f", f=P), ACT.Copy)\
                   .then_inc(y_even, 1)

        @block.gpsimd
        def _(pool):
            def remainder(u, s):
                pool.wait_ge(w_hi, u + 1)
                pool.tensor_tensor(WL[:, s], RAW[:, s], WH[:, s], ALU.subtract).then_inc(w_lo, 1)

            def add_square(norm, c, s):
                pool.wait_ge(sq_ready, SQUARES[norm] + c + 1)
                if isinstance(c, int) and c == 0:
                    if NORM[norm]:
                        pool.wait_ge(st_sum, NORM[norm])
                    pool.tensor_copy(SSQ[:], SQ[:, s, :]).then_inc(sq_used, 1)
                else:
                    pool.tensor_tensor(SSQ[:], SSQ[:], SQ[:, s, :], ALU.add).then_inc(sq_used, 1)
                pool.drain()

            pool.memset(U[:, :, 0:PAD], 0.0).then_inc(u_zero, 1)
            pool.memset(VSH[:].bitcast(F32), 0.0).then_inc(pad_zero, 1)
            pool.memset(VSL[:].bitcast(F32), 0.0).then_inc(pad_zero, 1)
            remainder(0, 0)
            for c in range(KC):
                add_square("mix", c, c % 2)
            with pool.Fori(0, 4) as i:
                for s in range(2):
                    remainder(unit_at("glu", i, s) + 1, 1 - s)
            for j in range(8):
                remainder(START["in"] + j + 1, (j + 1) % 2)
            for j in range(8):
                rows = P if j not in (0, 3) else 64
                pool.wait_ge(rot_done, j + 1)
                pool.tensor_tensor(DS[0:rows, j, :], DS[0:rows, j, :], COS[0:rows, :], ALU.mult).then_inc(rope_cos, 1)
            pool.wait_ge(v_hi, 3)
            pool.tensor_tensor(KSL[:], KD[:, 1, :], KSH[:], ALU.subtract).then_inc(k_lo, 1)
            for qb in range(1, TB):
                diagonal = SC[:, qb - 1, qb * P:(qb + 1) * P]
                pool.wait_ge(index_sum, IDXH * qb)
                pool.affine_select(out=diagonal, in_=diagonal, compare_op=ALU.is_ge, fill=FAR, base=0,
                                   pattern=[[-1, P]], channel_multiplier=1).then_inc(index_masked, 1)
            for name in ("memk", "memv"):
                with pool.Fori(0, 4) as i:
                    for s in range(2):
                        remainder(unit_at(name, i, s) + 1, 1 - s)
            with pool.Fori(0, 4) as c:
                pool.wait_ge(q_hi, c + 1)
                pool.tensor_tensor(QSL[:], DS[:, bass.ds(c + 4, 1), :], QSH[:], ALU.subtract).then_inc(q_lo, 1)
            for c in range(BCH):
                add_square("ln", c, c % 2)
            for c in range(BCH):
                pool.wait_ge(branch_hi, c + 1)
                pool.tensor_tensor(QL[:, 4 + c, :], CV[:, c, :], QH[:, 4 + c, :], ALU.subtract).then_inc(branch_lo, 1)

            def residual(name, norm, i, last=False):
                for s in range(2):
                    if not last or s == 0:
                        remainder(START[name] + 2 * i + s + 1, 1 - s)
                    add_square(norm, 2 * i + s, s)

            residual("out", "cross", 0)
            with pool.Fori(1, 4) as i:
                residual("out", "cross", i)
            with pool.Fori(0, 4) as i:
                for s in range(2):
                    remainder(unit_at("qc", i, s) + 1, 1 - s)
            pool.wait_ge(row_in, 48)
            pool.tensor_copy(S5ROW[:, 2, :].rearrange("j (g p) -> j g p", g=2),
                             DTROW[:, :, None].to_broadcast([JP, 2, 64])).then_inc(row_out, 1)
            with pool.Fori(0, 4) as h:
                k = 4 + 2 * h
                pool.wait_ge(q_hi, k + 1)
                pool.tensor_tensor(CQL[:], QT[:, bass.ds(2 * h, 2), :], CQH[:], ALU.subtract).then_inc(q_lo, 1)
                pool.wait_ge(q_hi, k + 2)
                pool.tensor_tensor(CKL[:], KM[:, bass.ds(2 * h, 2), :], CKH[:], ALU.subtract).then_inc(q_lo, 1)
                pool.wait_ge(v_t, h + 1)
                pool.tensor_copy(CVS[:], VM[:, bass.ds(2 * h, 2), :]).then_inc(cvs_in, 1)
            def mul(out, a, b):
                pool.tensor_tensor(out, a, b, ALU.mult)

            def wide(x):
                return x[:, :, None].to_broadcast([P, JP, 16])

            LBR, LBI = PW[:, 0, 1, :], PW[:, 1, 1, :]
            t = [SW[:, k, :] for k in range(10)]
            pool.wait_ge(sin_cos, 1)
            mul(LBR, t[2], t[6])
            mul(LBI, t[2], t[4])
            pool.tensor_copy(UT[:, 0, :], t[6])
            pool.tensor_copy(UT[:, 1, :], t[4])
            pool.memset(PW[:, 0, 0, :], 1.0)
            pool.memset(PW[:, 1, 0, :], 0.0)
            for k in range(1, 8):
                pool.drain()
                mul(t[0], PW[:, 0, k, :], LBR)
                mul(t[1], PW[:, 1, k, :], LBI)
                mul(t[2], PW[:, 0, k, :], LBI)
                mul(t[3], PW[:, 1, k, :], LBR)
                pool.drain()
                pool.tensor_tensor(PW[:, 0, k + 1, :], t[0], t[1], ALU.subtract)
                pool.tensor_tensor(PW[:, 1, k + 1, :], t[2], t[3], ALU.add)
            for k in range(3):
                pool.drain()
                mul(t[0], UT[:, 0, :], UT[:, 0, :])
                mul(t[1], UT[:, 1, :], UT[:, 1, :])
                mul(t[2], UT[:, 0, :], UT[:, 1, :])
                pool.drain()
                pool.tensor_tensor(UT[:, 0, :], t[0], t[1], ALU.subtract)
                pool.tensor_scalar(UT[:, 1, :], t[2], 2.0, None, ALU.mult)
            pool.wait_ge(den_inv, 1)
            pool.tensor_scalar(t[4], LBR, -1.0, None, ALU.add)
            pool.drain()
            mul(t[0], t[4], LAM[:, 0, :])
            mul(t[1], LBI, LAM[:, 1, :])
            mul(t[2], LBI, LAM[:, 0, :])
            mul(t[3], t[4], LAM[:, 1, :])
            pool.drain()
            pool.tensor_tensor(t[5], t[0], t[1], ALU.add)
            pool.tensor_tensor(t[6], t[2], t[3], ALU.subtract)
            pool.drain()
            mul(t[5], t[5], t[8])
            mul(t[6], t[6], t[8])
            pool.drain()
            pool.wait_ge(b_in, 32)
            for ri, (x, y, op) in enumerate(((t[5], t[6], ALU.subtract), (t[6], t[5], ALU.add))):
                mul(BT[:, 0], wide(x), BRAW[:, 0])
                mul(BT[:, 1], wide(y), BRAW[:, 1])
                pool.drain()
                pool.tensor_tensor(BB[:, ri], BT[:, 0], BT[:, 1], op)
                pool.drain()
            pool.nop().then_inc(params, 1)
            residual("oc", "ffn", 0)
            with pool.Fori(1, 4) as i:
                residual("oc", "ffn", i)
            pool.memset(G[:, 0:2], 0.0).then_inc(g_zero, 1)
            for g, n in FFN_GROUPS:
                with pool.Fori(0, n) as i:
                    for s in range(2):
                        remainder(unit_at(f"ffn{g}", i, s) + 1, 1 - s)
                if g != FFN_GROUPS[-1][0]:
                    with pool.Fori(0, 4) as i:
                        for s in range(2):
                            remainder(unit_at(f"down{g}", i, s) + 1, 1 - s)
            residual(f"down{g}", "final", 0)
            with pool.Fori(1, 4) as i:
                residual(f"down{g}", "final", i)
            for x in (W1T, KB, CL, SPV, RHOT):
                pool.memset(x[:], 0.0)
            pool.drain()
            pool.nop().then_inc(zeroed, 1)
            for c in range(KC):
                add_square("s5", c, c % 2)

            def generate(c, b):
                four = bass.ds(4 * c, 4)
                if not isinstance(c, int) or c:
                    pool.wait_ge(k_mm, c)
                for n, x, ri_ops in ((8, BB, (ALU.subtract, ALU.add)), (9, CC, (ALU.add, ALU.subtract))):
                    if n == 9 and (not isinstance(c, int) or c >= 2):
                        pool.wait_ge(y_mm, c - 1)
                    for ri in range(2):
                        for j in range(2):
                            a = PW[:, j if ri == 0 else 1 - j, 0:n, four][:, :, :, None].to_broadcast([P, n, 4, 16])
                            d = x[:, j, four, :][:, None, :, :].to_broadcast([P, n, 4, 16])
                            pool.tensor_tensor(GT[:, j, 0:n], a, d, ALU.mult)
                        pool.drain()
                        for g in range(2):
                            rows = slice(64 * g, 64 * g + 64)
                            o = W1T[rows, :, ri, :, g, :] if n == 8 else CL[rows, b, ri, :, :, g, :]
                            j = n == 9 and ri == 1
                            pool.tensor_tensor(o, GT[rows, int(j), 0:n], GT[rows, 1 - j, 0:n], ri_ops[ri])
                        pool.drain()
                pool.nop().then_inc(gen_ready, 1)

            generate(0, 0)
            generate(1, 1)
            with pool.Fori(1, 4) as i:
                for b in range(2):
                    generate(2 * i + b, b)

            def glu(i):
                for b in range(2):
                    c = 2 * i + b
                    for s in range(2):
                        remainder(unit_at("s5glu", c, s) + 1, 1 - s)
                    add_square("mlp0", c, b)

            glu(0)
            with pool.Fori(1, 4) as i:
                glu(i)
            pool.memset(FWR[:], 0.0)
            pool.memset(BF[:], 0.0)
            pool.memset(VSH[:].bitcast(F32), 0.0)
            pool.memset(VSL[:].bitcast(F32), 0.0)
            pool.drain().then_inc(fw_zero, 1)

            def mlp(l, norm):
                def remainders(name):
                    with pool.Fori(0, 4) as i:
                        for s in range(2):
                            remainder(unit_at(name, i, s) + 1, 1 - s)

                for g in range(GROUPS):
                    remainders(f"up{l}{g}")
                    if g < GROUPS - 1:
                        remainders(f"dn{l}{g}")
                name = f"dn{l}{GROUPS - 1}"
                residual(name, norm, 0)
                with pool.Fori(1, 3) as i:
                    residual(name, norm, i)
                residual(name, norm, 3, last=l == 1)

            mlp(0, "kv")
            pool.wait_ge(fw_hi, 1)
            pool.tensor_tensor(FWL[:], FWR[:], FWH[:], ALU.subtract).then_inc(fw_lo, 1)
            with pool.Fori(0, 8) as i:
                for s in range(2):
                    remainder(unit_at("kv", i, s) + 1, 1 - s)
            with pool.Fori(0, 4) as i:
                for s in range(2):
                    remainder(unit_at("wq", i, s) + 1, 1 - s)
            pool.wait_ge(f_ready, 3)
            with pool.Fori(0, 8) as c:
                k = 12 + 2 * c
                pool.wait_ge(q_hi, k + 1)
                pool.tensor_tensor(QSL[:], QT[:, bass.ds(c, 1), :], QSH[:], ALU.subtract).then_inc(q_lo, 1)
                pool.wait_ge(q_hi, k + 2)
                pool.tensor_tensor(KSL[:], KT[:, bass.ds(c, 1), :], KSH[:], ALU.subtract).then_inc(q_lo, 1)
                pool.wait_ge(v_t, 5 + c)
                pool.tensor_copy(VS[:], VT[:, bass.ds(c, 1), :]).then_inc(cvs_in, 1)
                for half in range(2):
                    for j, (to, fixed) in enumerate(((LQ, LF), (RK, RF))):
                        head = HOT[:, bass.ds(2 * c + half + NHEAD * j, 1)]
                        ins = pool.tensor_tensor(to[:, half, :], fixed[:], head.to_broadcast([P, T]), ALU.add)
                ins.then_inc(hot, 1)
            residual("wo", "mlp1", 0)
            with pool.Fori(1, 4) as i:
                residual("wo", "mlp1", i)
            mlp(1, "last")

        @block.tensor
        def _(pe):
            def unit(u, s, xh, xl, n=T, kc=KC, chunks=None):
                pe.wait_ge(w_hi, u + 1)
                if not isinstance(u, int) or u >= 2:
                    pe.wait_ge(unit_out, u - 1)
                for k in range(kc):
                    if chunks:
                        pe.wait_ge(chunks[0], chunks[1] + k + 1)
                    pe.matmul(ACC[s][:, 0:n], WH[:, s, k, :], xh[:, k, :], start=(k == 0), stop=False)
                    pe.matmul(ACC[s][:, 0:n], WH[:, s, k, :], xl[:, k, :], start=False, stop=False)
                pe.wait_ge(w_lo, u + 1)
                for k in range(kc):
                    mm = pe.matmul(ACC[s][:, 0:n], WL[:, s, k, :], xh[:, k, :], start=False, stop=(k == kc - 1))
                mm.then_inc(unit_done, 1)

            def column_sums(norm):
                pe.wait_ge(sq_used, SQUARES[norm] + dict(NORMS)[norm])
                if NORM[norm]:
                    pe.wait_ge(st_rs, NORM[norm])
                for b in range(TB):
                    mm = pe.matmul(ST[:, b:b + 1], SSQ[:, b * P:(b + 1) * P], ONES[:, 0:1], start=True, stop=True)
                mm.then_inc(st_sum, 1)

            def spread_scales(norm):
                pe.wait_ge(st_diag, NORM[norm] + 1)
                pe.matmul(ST[:], ONES, DIAG[:], start=True, stop=True).then_inc(st_bc, 1)

            pe.wait_ge(cst_in, 16)
            pe.wait_ge(x_in, 16)
            for c in range(KC):
                if c >= 2:
                    pe.wait_ge(x_ready, c - 1)
                for b in range(TB):
                    mm = pe.transpose(TR[c % 2][:, b * P:(b + 1) * P], XROW[:, b, c * P:(c + 1) * P], IDENT)
                mm.then_inc(x_t, 1)
                if c == 0:
                    pe.wait_ge(vec_in, 16 * len(VECTORS))
                    for t in range(3):
                        mm = pe.transpose(ST[:, t * P:t * P + ROWS[t]], VROW[0:ROWS[t], t, :], IDENT[0:ROWS[t], 0:ROWS[t]])
                    mm.then_inc(vec_t, 1)
            pe.wait_ge(mem_scaled, MB)
            for c in range(KC):
                if c >= 2:
                    pe.wait_ge(mem_lo, c - 1)
                for b in range(MB):
                    mm = pe.transpose(S[c % 2][:, b * P:(b + 1) * P], MROW[:, b, c * P:(c + 1) * P], IDENT)
                mm.then_inc(mem_t, 1)
            unit(0, 0, PH, PL, chunks=(op_lo, NOPERAND["mix"]))
            column_sums("mix")
            unit(1, 1, PH, PL)
            spread_scales("mix")
            with pe.Fori(1, 4) as i:
                for s in range(2):
                    unit(unit_at("glu", i, s), s, PH, PL)
            with pe.Fori(0, 4) as i:
                for s in range(2):
                    unit(unit_at("in", i, s), s, PH, PL)
            for j in range(8):
                rows = P if j not in (0, 3) else 64
                pe.wait_ge(unit_out, START["in"] + j + 1)
                if j >= 2:
                    pe.wait_ge(rot_used, j - 1)
                pe.matmul(TR[j % 2][0:rows, :], ROTM[0:rows, 0:rows], DS[0:rows, j, :], start=True, stop=True)\
                  .then_inc(rot_done, 1)
            for b in range(TB):
                mm = pe.transpose(O[:, b * 4:b * 4 + 4], DS[64:68, 0, b * P:(b + 1) * P], IDENT[64:68, 64:68])
            mm.then_inc(wi_t, 1)
            for b in range(TB):
                mm = pe.transpose(S[0][:, b * 64:(b + 1) * 64], DS[64:P, 3, b * P:(b + 1) * P], IDENT[64:P, 64:P])
            mm.then_inc(v_t, 1)
            pe.wait_ge(kd_in[0], 16)
            pe.wait_ge(rope_done, 3)
            pe.wait_ge(v_lo, 2)
            for n in range(3 * IDXH):
                qb, h = n // IDXH + 1, n % IDXH
                rows = slice(h % 2 * 64, h % 2 * 64 + 64)
                if n >= 2:
                    pe.wait_ge(index_relu, n - 1)
                pe.matmul(S[n % 2][:, 0:(qb + 1) * P], DS[rows, 1 + h // 2, qb * P:(qb + 1) * P],
                          KD[rows, 0, 0:(qb + 1) * P], start=True, stop=True).then_inc(index_mm, 1)
            pe.wait_ge(mem_lo, KC)
            for name in ("memk", "memv"):
                with pe.Fori(0, 4) as i:
                    for s in range(2):
                        unit(unit_at(name, i, s), s, MH, ML, n=NMEM)

            def three(out, ah, al, bh, bl, first, last):
                pe.matmul(out, ah, bh, start=first, stop=False)
                pe.matmul(out, ah, bl, start=False, stop=False)
                return pe.matmul(out, al, bh, start=False, stop=last)

            def scores(kind, n, t):
                half, qb = t // 4, t % 4
                nk = (qb + 1) * P
                rows, q = slice(half * 64, half * 64 + 64), slice(qb * P, nk)
                pe.wait_ge(e_done, n + 1)
                three(S[t % 2][:, 0:nk], QSH[rows, q], QSL[rows, q], KSH[rows, 0:nk], KSL[rows, 0:nk], True, False)
                if kind == "sparse":
                    mm = pe.matmul(S[t % 2][:, 0:nk], IDR[:], SEL[:, qb, 0:nk], start=False, stop=True)
                else:
                    pe.matmul(S[t % 2][:, 0:nk], LQ[:, half, q], RK[:, half, 0:nk], start=False, stop=False)
                    mm = pe.matmul(S[t % 2][:, q], IDR[:], TRIR[:], start=False, stop=True)
                mm.then_inc(s_ready, 1)

            def turn(n, t, kb):
                pe.wait_ge(e_scaled, n + 1)
                pe.wait_ge(pt_lo, n + 1)
                for k in range(kb):
                    mm = pe.transpose(TR[t % 2][:, k * P:(k + 1) * P], E[:, t % 2, k * P:(k + 1) * P], IDENT)
                mm.then_inc(t_ready, 1)

            def values(kind, c, n, half):
                pe.wait_ge(pt_lo, n + 4 * half + 6)
                if kind == "fox" and half == 0:
                    pe.wait_ge(v_lo, 6 + 2 * c + 2)
                for k in range(TB):
                    mm = three(O[:, k * P:T], VSH[:, k, half, :], VSL[:, k, half, :], PTH[:, k, k * P:T],
                               PTL[:, k, k * P:T], half == 0 and k == 0, half == 1 and k == TB - 1)
                mm.then_inc(pv_done, 1)

            def attend(kind, c):
                n = TILES[kind] + 8 * c
                for t in range(8):
                    scores(kind, n + t, t)
                    if t == 5:
                        values(kind, c, n, 0)
                    if t:
                        turn(n + t - 1, t - 1, (t - 1) % 4 + 1)
                turn(n + 7, 7, 4)
                values(kind, c, n, 1)

            pe.sem_inc(t_ready, 2)
            pe.sem_inc(pv_done, 1)
            pe.wait_ge(sel_ready, TB)
            pe.wait_ge(k_lo, 1)
            with pe.Fori(0, 4) as c:
                pe.wait_ge(q_lo, c + 1)
                attend("sparse", c)
            pe.wait_ge(conv_done, BCH)
            for c in range(BCH):
                mm = pe.matmul(S[0][:], ONES, CV[:, c, :], start=(c == 0), stop=(c == BCH - 1))
            mm.then_inc(mean_sum, 1)
            column_sums("ln")
            spread_scales("ln")
            pe.wait_ge(o_lo, PAIRS["sparse"] + 4)
            pe.wait_ge(branch_lo, BCH)
            with pe.Fori(0, 4) as i:
                for s in range(2):
                    unit(unit_at("out", i, s), s, QH, QL)

            def normed(name, norm, xh, xl, pairs):
                unit(START[name], 0, xh, xl, chunks=(op_lo, NOPERAND[norm]))
                column_sums(norm)
                unit(START[name] + 1, 1, xh, xl)
                spread_scales(norm)
                with pe.Fori(1, pairs) as i:
                    for s in range(2):
                        unit(unit_at(name, i, s), s, xh, xl)

            normed("qc", "cross", PH, PL, 4)
            pe.wait_ge(row_out, 1)
            for j in range(3):
                mm = pe.transpose(O[:, j * JP:(j + 1) * JP], S5ROW[:, j, :], IDENT[0:JP, 0:JP])
            mm.then_inc(row_t, 1)
            pe.wait_ge(c_in, 64)
            for j in range(4):
                ri, first = j // 2, j % 2 * 4
                if j >= 2:
                    pe.wait_ge(c_out, j - 1)
                for k in range(4):
                    mm = pe.transpose(TR[j % 2][:, k * P:(k + 1) * P],
                                      CROW[:, ri, first + k, :, :].rearrange("p a b -> p (a b)"), IDENT)
                mm.then_inc(c_t, 1)
            pe.wait_ge(c_out, 4)
            with pe.Fori(0, 4) as h:
                n = TILES["cross"] + 4 * h
                pe.wait_ge(cvs_in, h + 1)
                pe.wait_ge(o_lo, PAIRS["cross"] + 2 * h)
                for m in range(2):
                    for b in range(MB):
                        mm = pe.transpose(O[:, b * 2 * P + m * P:b * 2 * P + (m + 1) * P], CVS[:, m, b * P:(b + 1) * P],
                                          IDENT)
                mm.then_inc(v_t, 1)
                pe.wait_ge(q_lo, 4 + 2 * h + 2)
                for t in range(4):
                    q = slice(t * P, (t + 1) * P)
                    pe.wait_ge(e_done, n + t + 1)
                    for k in range(2):
                        mm = three(S[t % 2][:, 0:NMEM], CQH[:, k, q], CQL[:, k, q], CKH[:, k, :], CKL[:, k, :],
                                   k == 0, k == 1)
                    mm.then_inc(s_ready, 1)
                    if t:
                        turn(n + t - 1, t - 1, MB)
                turn(n + 3, 3, MB)
                pe.wait_ge(pt_lo, n + 6)
                pe.wait_ge(v_lo, h + 3)
                for m in range(2):
                    for k in range(MB):
                        mm = three((O, ST)[m][:], CVH[:, k, m * P:(m + 1) * P], CVL[:, k, m * P:(m + 1) * P],
                                   PTH[:, k, :], PTL[:, k, :], k == 0, k == MB - 1)
                    mm.then_inc(pv_done, 1)
            pe.wait_ge(o_lo, PAIRS["cross"] + 8)
            with pe.Fori(0, 4) as i:
                for s in range(2):
                    unit(unit_at("oc", i, s), s, QH, QL)
            for g, n in FFN_GROUPS:
                if g == 0:
                    normed("ffn0", "ffn", PH, PL, n)
                else:
                    with pe.Fori(0, n) as i:
                        for s in range(2):
                            unit(unit_at(f"ffn{g}", i, s), s, PH, PL)
                pe.wait_ge(hid_lo, g + n)
                with pe.Fori(0, 4) as i:
                    for s in range(2):
                        unit(unit_at(f"down{g}", i, s), s, QH, QL, kc=n)
            column_sums("final")
            spread_scales("final")
            column_sums("s5")
            spread_scales("s5")

            def turn_b(c):
                pe.wait_ge(gen_ready, c + 1)
                for k in range(4):
                    if k >= 2:
                        pe.wait_ge(w1_in, 4 * c + k - 1)
                    for m in range(4):
                        mm = pe.transpose(ACC[k % 2][:, m * P:(m + 1) * P],
                                          W1T[:, 2 * k + m // 2, m % 2].rearrange("p a b c -> p (a b c)"), IDENT)
                    mm.then_inc(w1_t, 1)

            def kernel_lags(c, b):
                if not isinstance(c, int) or c:
                    pe.wait_ge(kb_in, c)
                for j in range(4):
                    for ri in range(2):
                        mm = pe.matmul(O[32 * j:32 * j + 32, 0:256].rearrange("p (k c) -> p k c", k=8),
                                       W1T[:, 0, ri, j].rearrange("p a b -> p (a b)"),
                                       CL[:, b, ri, 0:8, j].rearrange("p k a b -> p k (a b)"),
                                       start=(ri == 0), stop=(ri == 1))
                mm.then_inc(k_mm, 1)

            UCv = UC[:].rearrange("p b (m i) -> p b m i", i=8)

            def mixer(c, b, more):
                pe.wait_ge(w1_in, 4 * c + 4)
                pe.wait_ge(uc_ready, c + 1)
                if not isinstance(c, int) or c:
                    pe.wait_ge(l_used, c)
                for i in range(8):
                    for ri in range(2):
                        for j in range(4):
                            rows = slice(32 * j, 32 * j + 32)
                            mm = pe.matmul(FOUR[:, j, ri * 64:ri * 64 + 64], W1[rows, 2 * (7 - i) + ri, :],
                                           UCv[rows, b, :, i], start=(i == 0 and ri == 0), stop=(i == 7),
                                           skip_group_check=True)
                mm.then_inc(l_mm, 1)
                if more:
                    turn_b(c + 1)
                    kernel_lags(c + 1, 1 - b)
                pe.wait_ge(kb_in, c + 1)
                if not isinstance(c, int) or c:
                    pe.wait_ge(y_out, c)
                Y = ST[:].rearrange("p (m i) -> p m i", i=8)
                for lag in range(8):
                    pe.matmul(Y[:, :, lag:8], KB[:, b, lag, :], UCv[:, b, :, 0:8 - lag],
                              start=(lag == 0), stop=False, skip_group_check=True)
                pe.wait_ge(sp_ready, c + 1)
                for i in range(8):
                    for ri in range(2):
                        for j in range(4):
                            mm = pe.matmul(Y[32 * j:32 * j + 32, :, i],
                                           CL[:, b, ri, i + 1, j].rearrange("p a b -> p (a b)"), SPV[:, ri, j, :],
                                           start=False, stop=(ri == 1 and i == 7), skip_group_check=True)
                mm.then_inc(y_mm, 1)

            turn_b(0)
            kernel_lags(0, 0)
            mixer(0, 0, True)
            mixer(1, 1, True)
            with pe.Fori(1, 3) as i:
                for b in range(2):
                    mixer(2 * i + b, b, True)
            mixer(6, 0, True)
            mixer(7, 1, False)

            def units(name, first, last, xh, xl):
                with pe.Fori(first, last) as i:
                    for s in range(2):
                        unit(unit_at(name, i, s), s, xh, xl)

            def first_pair(name, xh, xl, chunks):
                unit(START[name], 0, xh, xl, chunks=chunks)
                unit(START[name] + 1, 1, xh, xl)

            def mlp(l, x, h):
                for g in range(GROUPS):
                    if g == 0:
                        normed(f"up{l}{g}", f"mlp{l}", *x, 4)
                    else:
                        units(f"up{l}{g}", 0, 4, *x)
                    first_pair(f"dn{l}{g}", *h, (hid_lo, HIDDEN[f"mlp{l}"] + g * KC))
                    units(f"dn{l}{g}", 1, 4, *h)

            first_pair("s5glu", QH, QL, (hid_lo, HIDDEN["s5"]))
            units("s5glu", 1, 8, QH, QL)
            mlp(0, (PH, PL), (QH, QL))
            normed("kv", "kv", PH, PL, 8)
            pe.wait_ge(fw_lo, 1)
            for k in range(KC):
                mm = three(O[:], FWH[:, k, :], FWL[:, k, :], PH[:, k, :], PL[:, k, :], k == 0, k == KC - 1)
            mm.then_inc(f_mm, 1)
            pe.wait_ge(op_lo, NOPERAND["wq"] + KC)
            units("wq", 0, 4, QH, QL)
            pe.wait_ge(f_ready, 3)
            with pe.Fori(0, 8) as c:
                pe.wait_ge(cvs_in, 5 + c)
                pe.wait_ge(o_lo, PAIRS["fox"] + c)
                for b in range(TB):
                    mm = pe.transpose(O[:, b * P:(b + 1) * P], VS[:, b * P:(b + 1) * P], IDENT)
                mm.then_inc(v_t, 1)
                pe.wait_ge(q_lo, 14 + 2 * c)
                pe.wait_ge(hot, c + 1)
                attend("fox", c)
            pe.wait_ge(o_lo, PAIRS["fox"] + 8)
            units("wo", 0, 4, PH, PL)
            mlp(1, (QH, QL), (PH, PL))
            column_sums("last")
            spread_scales("last")
            for c in range(KC):
                pe.wait_ge(y_normed, c + 1)
                if c >= 2:
                    pe.wait_ge((y_even, y_odd)[c % 2], c // 2)
                for b in range(TB):
                    mm = pe.transpose(TR[c % 2][:, b * P:(b + 1) * P], X[:, c, b * P:(b + 1) * P], IDENT)
                mm.then_inc(y_t, 1)

        @block.vector
        def _(dve):
            def low(norm, c, gain, hi, lo):
                dve.wait_ge(op_hi, NOPERAND[norm] + c + 1)
                dve.scalar_tensor_tensor(lo, X[:, bass.ds(c, 1), :], column(gain, c), hi, ALU.mult, ALU.subtract)\
                   .then_inc(op_lo, 1)

            def newton(r, v, y):
                dve.tensor_tensor(y, r, r, ALU.mult)
                dve.drain()
                dve.scalar_tensor_tensor(y, y, -0.5, v, ALU.mult, ALU.mult)
                dve.drain()
                dve.scalar_tensor_tensor(r, y, 1.5, r, ALU.add, ALU.mult)
                dve.drain()

            def scales(norm, n):
                k = NORM[norm] + 1
                dve.wait_ge(st_sum, k)
                dve.tensor_scalar(V4[:], ST[:, 0:TB], 1.0 / n, EPS, ALU.mult, ALU.add).then_inc(st_var, 1)
                dve.wait_ge(st_std, k)
                dve.reciprocal(R4[:], SD4[:])
                dve.drain()
                newton(R4[:], V4[:], SD4[:])
                dve.tensor_tensor(DIAG[:].rearrange("p (b t) -> p b t", b=TB),
                                  IDENT[:, None, :].to_broadcast([P, TB, P]),
                                  R4[:, :, None].to_broadcast([P, TB, P]), ALU.mult).then_inc(st_diag, 1)
                dve.wait_ge(st_bc, k)
                dve.tensor_copy(RS[:], ST[:]).then_inc(st_rs, 1)
                dve.drain()

            dve.wait_ge(mem_sq, MB)
            dve.tensor_scalar(V4[:, 0:MB], V4[:, 0:MB], 1.0 / D, EPS, ALU.mult, ALU.add).then_inc(mem_var, 1)
            for c in range(KC):
                dve.wait_ge(x_t, c + 1)
                dve.tensor_copy(X[:, c, :], TR[c % 2][:]).then_inc(x_ready, 1)
                if c == 0:
                    dve.wait_ge(vec_t, 1)
                    for t in range(3):
                        last = dve.tensor_copy(VEC[:, t, 0:ROWS[t]], ST[:, t * P:t * P + ROWS[t]])
                    last.then_inc(vec_c, 1)
                    dve.drain()
                    dve.wait_ge(mem_std, 1)
                    dve.reciprocal(R4[:, 0:MB], SD4[:, 0:MB])
                    dve.drain()
                    newton(R4[:, 0:MB], V4[:, 0:MB], SD4[:, 0:MB])
                    for b in range(MB):
                        dve.tensor_scalar(MROW[:, b, :], MROW[:, b, :], R4[:, b:b + 1], None, ALU.mult)\
                           .then_inc(mem_scaled, 1)
                if c >= 1:
                    low("mix", c - 1, "norm_mix_g", PH[:, c - 1, :], PL[:, c - 1, :])
            low("mix", KC - 1, "norm_mix_g", PH[:, KC - 1, :], PL[:, KC - 1, :])
            for c in range(KC):
                dve.wait_ge(mem_hi, c + 1)
                dve.scalar_tensor_tensor(ML[:, c, :], S[c % 2][:, 0:NMEM], column("norm_mem_g", c), MH[:, c, :],
                                         ALU.mult, ALU.subtract).then_inc(mem_lo, 1)
            dve.wait_ge(pos_in, 16)
            dve.tensor_copy(COS[:], POSI[:])
            dve.drain()
            dve.tensor_scalar(SIN[:], COS[:], FREQ, None, ALU.mult)
            dve.drain()
            dve.tensor_scalar(COS[:], SIN[:], 1.0 / (2.0 * np.pi), MAGIC, ALU.mult, ALU.add)
            dve.drain()
            dve.tensor_scalar(COS[:], COS[:], -MAGIC, None, ALU.add)
            for part in TWO_PI:
                dve.drain()
                dve.scalar_tensor_tensor(SIN[:], COS[:], -part, SIN[:], ALU.mult, ALU.add)
            dve.drain()
            dve.tensor_scalar(SIN[:], SIN[:], PI_BELOW, -PI_BELOW, ALU.min, ALU.max)
            dve.drain()
            dve.scalar_tensor_tensor(COS[:], SIN[:], -1.0, SIN[:], ALU.mult, ALU.max)
            dve.drain()
            dve.tensor_scalar(COS[:], COS[:], -1.0, float(np.pi / 2), ALU.mult, ALU.add).then_inc(ang, 1)
            scales("mix", D)
            dve.wait_ge(u_zero, 1)

            def glu(i):
                u = unit_at("glu", i, 0)
                if not isinstance(i, int):
                    dve.wait_ge(gate_sig, i)
                dve.wait_ge(unit_done, u + 1)
                dve.tensor_tensor(TA, ACC[0][:], RS[:], ALU.mult).then_inc(unit_out, 1)
                dve.wait_ge(unit_done, u + 2)
                dve.tensor_tensor(TB_, ACC[1][:], RS[:], ALU.mult).then_inc(unit_out, 1)
                dve.drain().then_inc(gate_raw, 1)
                dve.wait_ge(gate_sig, i + 1)
                dve.tensor_tensor(U[:, bass.ds(i, 1), PAD:PAD + T], TA, TB_, ALU.mult)
                dve.drain()

            glu(0)
            with dve.Fori(1, 4) as i:
                glu(i)
            SCALE = [1.0, 0.125, 0.125, 1.0, 0.125, 0.125, 0.125, 0.125]
            for j in range(8):
                u = START["in"] + j
                dve.wait_ge(unit_done, u + 1)
                dve.scalar_tensor_tensor(DS[:, j, :], ACC[j % 2][:], SCALE[j], RS[:], ALU.mult, ALU.mult)\
                   .then_inc(unit_out, 1)
            for j in range(8):
                rows = P if j not in (0, 3) else 64
                to = KD[0:64, j // 3, :] if j in (0, 3) else DS[:, j, :]
                dve.wait_ge(rot_done, j + 1)
                dve.tensor_tensor(E[0:rows, j % 2, :], TR[j % 2][0:rows, :], SIN[0:rows, :], ALU.mult)\
                   .then_inc(rot_used, 1)
                dve.drain()
                dve.wait_ge(rope_cos, j + 1)
                dve.tensor_tensor(to, DS[0:rows, j, :], E[0:rows, j % 2, :], ALU.add).then_inc(rope_done, 1)
            dve.wait_ge(wi_t, 1)
            dve.tensor_scalar(WI[:].rearrange("p b h -> p (b h)"), O[:, 0:TB * 4], 0.5, None, ALU.mult)
            for half in range(2):
                cols = slice(half * 64, half * 64 + 64)
                dve.wait_ge(v_hi, 2)
                dve.tensor_tensor(VSL[:, :, half, cols], S[0][:, 0:TB * 64].rearrange("p (b f) -> p b f", b=TB),
                                  VSH[:, :, half, cols], ALU.subtract).then_inc(v_lo, 1)
            for n in range(3 * IDXH):
                qb, h = n // IDXH + 1, n % IDXH
                nk = (qb + 1) * P
                dve.drain()
                dve.wait_ge(index_relu, n + 1)
                if h == 0:
                    ins = dve.tensor_scalar(SC[:, qb - 1, 0:nk], E[:, n % 2, 0:nk], WI[:, qb, h:h + 1], None, ALU.mult)
                else:
                    ins = dve.scalar_tensor_tensor(SC[:, qb - 1, 0:nk], E[:, n % 2, 0:nk], WI[:, qb, h:h + 1],
                                                   SC[:, qb - 1, 0:nk], ALU.mult, ALU.add)
                ins.then_inc(index_sum, 1)
            dve.tensor_copy(SEL[:, 0, 0:P], TRI).then_inc(sel_ready, 1)
            dve.wait_ge(index_masked, 3)
            with dve.Fori(0, TOPK // 8) as r:
                for b in range(3):
                    dve.max(M8[:, b, :], SC[:, b, 0:(b + 2) * P])
                dve.drain()
                for b in range(3):
                    dve.match_replace(SC[:, b, 0:(b + 2) * P], M8[:, b, :], SC[:, b, 0:(b + 2) * P], TAKEN)
                dve.drain()
            for b in range(3):
                dve.tensor_scalar(SEL[:, b + 1, 0:(b + 2) * P], SC[:, b, 0:(b + 2) * P], TAKEN, -BIG,
                                  ALU.not_equal, ALU.mult).then_inc(sel_ready, 1)
            with dve.Fori(0, BCH) as c:
                def tap(k):
                    return U[:, bass.ds(c, 1), k:k + T]

                dve.tensor_scalar(CV[:, bass.ds(c, 1), :], tap(0), column("conv_b_w", c), column("conv_b_b", c),
                                  ALU.mult, ALU.add)
                for k in range(1, CONVW):
                    dve.drain()
                    ins = dve.scalar_tensor_tensor(CV[:, bass.ds(c, 1), :], tap(k), column("conv_b_w", BCH * k + c),
                                                   CV[:, bass.ds(c, 1), :], ALU.mult, ALU.add)
                ins.then_inc(conv_done, 1)

            def negative_max(n, t, nk):
                dve.wait_ge(s_ready, n + 1)
                dve.wait_ge(e_done, n + 1)
                dve.tensor_reduce(NMX[:, t % 2, :], S[t % 2][:, 0:nk], AX, ALU.max, negate=True).then_inc(mx_ready, 1)

            def divide(n, t, nk):
                dve.wait_ge(e_done, n + 3)
                dve.reciprocal(REC[:, t % 2, :], SUM[:, t % 2, :])
                dve.drain()
                dve.tensor_scalar(E[:, t % 2, 0:nk], E[:, t % 2, 0:nk], REC[:, t % 2, :], None, ALU.mult)\
                   .then_inc(e_scaled, 1)

            def turned_low(n, t, qb, kb):
                to = (slice(None), slice(0, kb), slice(qb * P, (qb + 1) * P))
                dve.wait_ge(pt_hi, n + 1)
                dve.tensor_tensor(PTL[to], TR[t % 2][:, 0:kb * P].rearrange("p (k q) -> p k q", q=P), PTH[to],
                                  ALU.subtract).then_inc(pt_lo, 1)

            def attend(kind, c):
                n = TILES[kind] + 8 * c
                for t in range(8):
                    negative_max(n + t, t, (t % 4 + 1) * P)
                    if t:
                        divide(n + t - 1, t - 1, ((t - 1) % 4 + 1) * P)
                    if t > 1:
                        turned_low(n + t - 2, t - 2, (t - 2) % 4, (t - 2) % 4 + 1)
                divide(n + 7, 7, 4 * P)
                turned_low(n + 6, 6, 2, 3)
                turned_low(n + 7, 7, 3, 4)

            def low_out(bank_, lo, hi, k):
                dve.wait_ge(o_hi, k + 1)
                dve.tensor_tensor(lo, bank_[:], hi, ALU.subtract).then_inc(o_lo, 1)

            dve.sem_inc(pt_lo, 2)
            with dve.Fori(0, 4) as c:
                attend("sparse", c)
                low_out(O, QL[:, bass.ds(c, 1), :], QH[:, bass.ds(c, 1), :], PAIRS["sparse"] + c)
            dve.wait_ge(mean_sum, 1)
            for c in range(BCH):
                dve.scalar_tensor_tensor(CV[:, c, :], S[0][:], -1.0 / (BCH * P), CV[:, c, :], ALU.mult, ALU.add)\
                   .then_inc(centred, 1)
            scales("ln", BCH * P)
            for c in range(BCH):
                dve.tensor_tensor(CV[:, c, :], CV[:, c, :], RS[:], ALU.mult).then_inc(ln_scaled, 1)

            def residual(name, norm, gain, hi, lo, i):
                for s in range(2):
                    c = 2 * i + s
                    x = X[:, bass.ds(c, 1), :]
                    dve.wait_ge(unit_done, START[name] + c + 1)
                    dve.tensor_tensor(x, x, ACC[s][:], ALU.add).then_inc(unit_out, 1)
                    low(norm, c, gain, hi[:, bass.ds(c, 1), :], lo[:, bass.ds(c, 1), :])

            with dve.Fori(0, 4) as i:
                residual("out", "cross", "norm_cross_g", PH, PL, i)
            scales("cross", D)

            def scaled(name, i, to, k=1.0):
                for s in range(2):
                    u = unit_at(name, i, s)
                    dve.wait_ge(unit_done, u + 1)
                    dve.scalar_tensor_tensor(to[:, bass.ds(2 * i + s, 1), :], ACC[s][:], k, RS[:], ALU.mult, ALU.mult)\
                       .then_inc(unit_out, 1)

            with dve.Fori(0, 4) as i:
                scaled("qc", i, QT, 1.0 / 16)
            dve.wait_ge(row_t, 1)
            dve.tensor_copy(LAM[:].rearrange("p a b -> p (a b)"), O[:, 0:3 * JP])
            for j in range(4):
                dve.wait_ge(c_t, j + 1)
                for g in range(2):
                    rows = slice(64 * g, 64 * g + 64)
                    src = TR[j % 2][rows, :].rearrange("p (j g c) -> p j g c", g=2, c=16)[:, :, g, :]
                    ins = dve.tensor_scalar(CC[rows, j // 2, j % 2 * 16:j % 2 * 16 + 16, :], src, (1.0, -1.0)[j // 2],
                                            None, ALU.mult)
                ins.then_inc(c_out, 1)
            w = [SW[:, k, :] for k in range(10)]

            def exponential(out, x, n, r, q):
                dve.drain()
                dve.tensor_scalar(n, x, float(1.0 / np.log(2.0)), MAGIC, ALU.mult, ALU.add)
                dve.drain()
                dve.tensor_scalar(n, n, -MAGIC, -126.0, ALU.add, ALU.max)
                dve.drain()
                dve.scalar_tensor_tensor(r, n, -LN2[0], x, ALU.mult, ALU.add)
                dve.drain()
                dve.scalar_tensor_tensor(r, n, -LN2[1], r, ALU.mult, ALU.add)
                dve.tensor_scalar(POW2[:], n, 127.0, float(2 ** 23), ALU.add, ALU.mult)
                dve.drain()
                dve.tensor_scalar(q, r, 1.0 / 5040, None, ALU.mult)
                for k in (720.0, 120.0, 24.0, 6.0, 2.0, 1.0):
                    dve.drain()
                    dve.scalar_tensor_tensor(q, q, 1.0 / k, r, ALU.add, ALU.mult)
                dve.drain()
                dve.scalar_tensor_tensor(out, q, 1.0, POW2[:].bitcast(F32), ALU.add, ALU.mult)
                dve.drain()

            exponential(LAM[:, 2, :], LAM[:, 2, :], w[3], w[4], w[5])
            dve.tensor_tensor(w[0], LAM[:, 0, :], LAM[:, 2, :], ALU.mult)
            dve.tensor_tensor(w[1], LAM[:, 1, :], LAM[:, 2, :], ALU.mult)
            dve.tensor_tensor(w[7], LAM[:, 0, :], LAM[:, 0, :], ALU.mult)
            dve.tensor_tensor(w[8], LAM[:, 1, :], LAM[:, 1, :], ALU.mult)
            dve.drain()
            dve.tensor_tensor(w[7], w[7], w[8], ALU.add)
            dve.tensor_scalar(w[3], w[1], 1.0 / (2.0 * np.pi), MAGIC, ALU.mult, ALU.add)
            dve.drain()
            dve.reciprocal(w[8], w[7]).then_inc(den_inv, 1)
            dve.tensor_scalar(w[3], w[3], -MAGIC, None, ALU.add)
            for part in TWO_PI:
                dve.drain()
                dve.scalar_tensor_tensor(w[1], w[3], -part, w[1], ALU.mult, ALU.add)
            dve.drain()
            dve.tensor_scalar(w[1], w[1], PI_BELOW, -PI_BELOW, ALU.min, ALU.max)
            dve.drain()
            dve.scalar_tensor_tensor(w[9], w[1], -1.0, w[1], ALU.mult, ALU.max)
            exponential(w[2], w[0], w[3], w[4], w[5])
            dve.tensor_scalar(w[9], w[9], -1.0, float(np.pi / 2), ALU.mult, ALU.add)
            dve.tensor_tensor(w[3], w[2], w[2], ALU.mult)
            dve.drain()
            dve.tensor_tensor(w[5], w[3], w[3], ALU.mult)
            dve.drain()
            dve.tensor_tensor(RHO8[:], w[5], w[5], ALU.mult)
            dve.drain().then_inc(angle_ready, 1)
            with dve.Fori(0, 4) as h:
                n = TILES["cross"] + 4 * h
                dve.wait_ge(v_hi, h + 4)
                dve.tensor_tensor(CVL[:], O[:].rearrange("p (b f) -> p b f", b=MB), CVH[:], ALU.subtract)\
                   .then_inc(v_lo, 1)
                for t in range(4):
                    negative_max(n + t, t, NMEM)
                    if t:
                        divide(n + t - 1, t - 1, NMEM)
                    if t > 1:
                        turned_low(n + t - 2, t - 2, t - 2, MB)
                divide(n + 3, 3, NMEM)
                turned_low(n + 2, 2, 2, MB)
                turned_low(n + 3, 3, 3, MB)
                for m in range(2):
                    chunk = bass.ds(2 * h + m, 1)
                    low_out((O, ST)[m], QL[:, chunk, :], QH[:, chunk, :], PAIRS["cross"] + 2 * h + m)
            with dve.Fori(0, 4) as i:
                residual("oc", "ffn", "norm_ffn_g", PH, PL, i)
            def turn_table(k):
                if k == 0:
                    dve.wait_ge(params, 1)
                    dve.memset(ET[:, 0, :, 0], 1.0)
                    dve.memset(ET[:, 1, :, 0], 0.0)
                    dve.drain()
                n = 2 ** k
                TMP = at(f"TMP{k}", [P, 2, JP, n], F32, 155648 + 6208)
                for ri in range(2):
                    for j in range(2):
                        u = UT[:, j if ri == 0 else 1 - j, :, None].to_broadcast([P, JP, n])
                        dve.tensor_tensor(TMP[:, j], ET[:, j, :, 0:n], u, ALU.mult)
                    dve.drain()
                    dve.tensor_tensor(ET[:, ri, :, n:2 * n], TMP[:, 0], TMP[:, 1], (ALU.subtract, ALU.add)[ri])
                    dve.drain()
                if k < 5:
                    t = [SW[:, j, :] for j in range(3)]
                    dve.tensor_tensor(t[0], UT[:, 0, :], UT[:, 0, :], ALU.mult)
                    dve.tensor_tensor(t[1], UT[:, 1, :], UT[:, 1, :], ALU.mult)
                    dve.tensor_tensor(t[2], UT[:, 0, :], UT[:, 1, :], ALU.mult)
                    dve.drain()
                    dve.tensor_tensor(UT[:, 0, :], t[0], t[1], ALU.subtract)
                    dve.tensor_scalar(UT[:, 1, :], t[2], 2.0, None, ALU.mult)
                    dve.drain()

            def hidden_low(k, x, value, hi=QH, lo=QL):
                dve.wait_ge(hid_hi, value)
                dve.tensor_tensor(lo[:, bass.ds(k, 1), :], x, hi[:, bass.ds(k, 1), :], ALU.subtract).then_inc(hid_lo, 1)

            scales("ffn", D)
            dve.wait_ge(g_zero, 1)
            for g, n in FFN_GROUPS:
                turn_table(g // 4)
                with dve.Fori(0, n) as i:
                    u = unit_at(f"ffn{g}", i, 0)
                    f = i + g
                    dve.wait_ge(unit_done, u + 1)
                    dve.tensor_tensor(G[:, 2:2 + T], ACC[0][:], RS[:], ALU.mult).then_inc(unit_out, 1)
                    dve.drain()
                    dve.tensor_scalar(H1[:], G[:, 0:T], column("ffn_conv_w", f), column("ffn_conv_b", f), ALU.mult, ALU.add)
                    dve.drain()
                    dve.scalar_tensor_tensor(H1[:], G[:, 1:1 + T], column("ffn_conv_w", f + FC), H1[:], ALU.mult, ALU.add)
                    dve.drain()
                    dve.scalar_tensor_tensor(H1[:], G[:, 2:2 + T], column("ffn_conv_w", f + 2 * FC), H1[:], ALU.mult, ALU.add)\
                       .then_inc(gate_conv, 1)
                    dve.wait_ge(unit_done, u + 2)
                    dve.tensor_tensor(H2[:], ACC[1][:], RS[:], ALU.mult).then_inc(unit_out, 1)
                    dve.drain()
                    dve.wait_ge(gate_act, f + 1)
                    dve.tensor_tensor(H2[:], H2[:], H1[:], ALU.mult).then_inc(hid_ready, 1)
                    hidden_low(i, H2[:], f + 1)
                turn_table(g // 4 + 1)
                with dve.Fori(0, 4) as i:
                    for s in range(2):
                        x = X[:, bass.ds(2 * i + s, 1), :]
                        dve.wait_ge(unit_done, unit_at(f"down{g}", i, s) + 1)
                        dve.tensor_tensor(x, x, ACC[s][:], ALU.add).then_inc(unit_out, 1)
                dve.drain()
            scales("final", D)
            for c in range(KC):
                dve.scalar_tensor_tensor(X[:, c, :], X[:, c, :], column("norm_final_g", c), RS[:], ALU.mult, ALU.mult)\
                   .then_inc(normed_x, 1)
            scales("s5", D)
            for c in range(KC):
                dve.scalar_tensor_tensor(U5[:, c, :], X[:, c, :], column("mix_norm_2", c), RS[:], ALU.mult, ALU.mult)\
                   .then_inc(u5_ready, 1)

            def kernel_in(c, b):
                dve.wait_ge(k_mm, c + 1)
                if not isinstance(c, int) or c >= 2:
                    dve.wait_ge(y_mm, c - 1)
                for j in range(4):
                    rows = slice(32 * j, 32 * j + 32)
                    ins = dve.tensor_copy(KB[rows, b, :, 32 * j:32 * j + 32],
                                          O[rows, 0:256].rearrange("p (k c) -> p k c", k=8))
                ins.then_inc(kb_in, 1)

            def mixer(c, b, more):
                four = bass.ds(4 * c, 4)
                cos, sin = ET[:, 0, four, :], ET[:, 1, four, :]
                dve.wait_ge(l_mm, c + 1)
                for ri, (x, y, op) in enumerate(((0, 1, ALU.add), (1, 0, ALU.subtract))):
                    dve.tensor_tensor(RT[:, 0], FOUR[:, :, x * 64:x * 64 + 64], cos, ALU.mult)
                    ins = dve.tensor_tensor(RT[:, 1], FOUR[:, :, y * 64:y * 64 + 64], sin, ALU.mult)
                    if ri:
                        ins.then_inc(l_used, 1)
                    dve.drain()
                    dve.tensor_tensor(VR[:, ri], RT[:, 0], RT[:, 1], op)
                    dve.drain()
                dve.tensor_copy(RHOT[:, :, 1:64], RHO8[:, four, None].to_broadcast([P, 4, 63]))
                dve.drain()
                for ri in range(2):
                    dve.tensor_tensor_scan(WR[:, ri].rearrange("p a b -> p (a b)"), RHOT[:].rearrange("p a b -> p (a b)"),
                                           VR[:, ri].rearrange("p a b -> p (a b)"), 0.0, ALU.mult, ALU.add)
                dve.drain()
                if not isinstance(c, int) or c:
                    dve.wait_ge(y_mm, c)
                cos, sin = ET[:, 0, four, 0:63], ET[:, 1, four, 0:63]
                for ri, (x, y, op) in enumerate(((0, 1, ALU.subtract), (1, 0, ALU.add))):
                    dve.tensor_tensor(RT[:, 0, :, 0:63], WR[:, x, :, 0:63], cos, ALU.mult)
                    dve.tensor_tensor(RT[:, 1, :, 0:63], WR[:, y, :, 0:63], sin, ALU.mult)
                    dve.drain()
                    dve.tensor_tensor(SPV[:, ri, :, 1:64], RT[:, 0, :, 0:63], RT[:, 1, :, 0:63], op)
                    dve.drain()
                dve.nop().then_inc(sp_ready, 1)
                if more:
                    kernel_in(c + 1, 1 - b)
                dve.wait_ge(y_mm, c + 1)
                if not isinstance(c, int) or c >= 2:
                    dve.wait_ge(hid_hi, HIDDEN["s5"] + c - 1)
                dve.scalar_tensor_tensor(YC[:, b, :], U5[:, bass.ds(c, 1), :], column("ssm_d_2", c), ST[:],
                                         ALU.mult, ALU.add).then_inc(y_out, 1)
                hidden_low(c, YC[:, b, :], HIDDEN["s5"] + c + 1)

            dve.wait_ge(zeroed, 1)
            kernel_in(0, 0)
            mixer(0, 0, True)
            mixer(1, 1, True)
            with dve.Fori(1, 3) as i:
                for b in range(2):
                    mixer(2 * i + b, b, True)
            mixer(6, 0, True)
            mixer(7, 1, False)
            dve.drain()
            with dve.Fori(0, 8) as c:
                u = unit_at("s5glu", c, 0)
                x = X[:, bass.ds(c, 1), :]
                dve.wait_ge(unit_done, u + 1)
                dve.tensor_copy(TA, ACC[0][:]).then_inc(unit_out, 1)
                dve.drain()
                dve.wait_ge(gate_sig, 4 + c + 1)
                dve.tensor_tensor(TA, TA, TB_, ALU.mult).then_inc(unit_out, 1)
                dve.drain()
                dve.tensor_tensor(x, x, TA, ALU.add).then_inc(glu_out, 1)
                low("mlp0", c, "mlp_norm_2", PH[:, bass.ds(c, 1), :], PL[:, bass.ds(c, 1), :])

            def mlp(l, hi, lo):
                norm = f"mlp{l}"
                for g in range(GROUPS):
                    with dve.Fori(0, 4) as i:
                        for s in range(2):
                            k = 2 * i + s
                            h = (H1, H2)[s]
                            dve.wait_ge(unit_done, unit_at(f"up{l}{g}", i, s) + 1)
                            dve.tensor_tensor(h[:], ACC[s][:], RS[:], ALU.mult).then_inc(unit_out, 1)
                            dve.drain()
                            dve.scalar_tensor_tensor(h[:], h[:], 0.0, h[:], ALU.max, ALU.mult).then_inc(hid_ready, 1)
                            dve.drain()
                            hidden_low(k, h[:], HIDDEN[norm] + g * KC + k + 1, hi, lo)
                    if g < GROUPS - 1:
                        with dve.Fori(0, 4) as i:
                            for s in range(2):
                                x = X[:, bass.ds(2 * i + s, 1), :]
                                dve.wait_ge(unit_done, unit_at(f"dn{l}{g}", i, s) + 1)
                                dve.tensor_tensor(x, x, ACC[s][:], ALU.add).then_inc(unit_out, 1)
                        dve.drain()

            scales("mlp0", D)
            mlp(0, QH, QL)
            with dve.Fori(0, 4) as i:
                residual(f"dn0{GROUPS - 1}", "kv", "kv_norm_2", PH, PL, i)
            scales("kv", D)
            for j, to in enumerate((KT, VT)):
                with dve.Fori(0, 4) as i:
                    for s in range(2):
                        c = 2 * i + s
                        dve.wait_ge(unit_done, START["kv"] + j * 8 + c + 1)
                        dve.tensor_tensor(to[:, bass.ds(c, 1), :], ACC[s][:], RS[:], ALU.mult).then_inc(unit_out, 1)
                    c = i + 4 * j
                    low("wq", c, ("mix_norm_2", KC), QH[:, bass.ds(c, 1), :], QL[:, bass.ds(c, 1), :])
            dve.wait_ge(f_mm, 1)
            dve.tensor_tensor(FZ[:], O[:], RS[:], ALU.mult)
            dve.drain()
            dve.tensor_scalar(FZ[:], FZ[:], BF[:], None, ALU.add)
            dve.drain()
            dve.scalar_tensor_tensor(F[:], FZ[:], -1.0, FZ[:], ALU.mult, ALU.max).then_inc(f_abs, 1)
            dve.wait_ge(f_ln, 1)
            dve.scalar_tensor_tensor(FZ[:], FZ[:], 0.0, F[:], ALU.min, ALU.subtract)
            dve.drain()
            dve.tensor_tensor_scan(F[:], ONES[:, 0:1].to_broadcast([P, T]), FZ[:], 0.0, ALU.mult, ALU.add)\
               .then_inc(f_sum, 1)
            with dve.Fori(0, 4) as i:
                scaled("wq", i, QT, 0.125)
            dve.wait_ge(f_ready, 1)
            dve.tensor_tensor(FL[:], F[:], FH[:], ALU.subtract)
            dve.drain()
            dve.memset(LF[0:64, :].bitcast(F32), 0.0)
            dve.memset(RF[64:P, :].bitcast(F32), 0.0)
            dve.tensor_scalar(RF[32:64, :], FL[32:64, :].bitcast(F32), -1.0, None, ALU.mult)
            dve.tensor_copy(LF[96:P, :], FL[96:P, :].bitcast(F32))
            dve.wait_ge(f_ready, 2)
            dve.drain().then_inc(f_ready, 1)
            with dve.Fori(0, 8) as c:
                for half in range(2):
                    dve.wait_ge(v_hi, 9 + 2 * c)
                    cols = slice(half * 64, half * 64 + 64)
                    dve.tensor_tensor(VSL[:, :, half, cols],
                                      O[:].rearrange("p (b h f) -> p b h f", b=TB, h=2)[:, :, half, :],
                                      VSH[:, :, half, cols], ALU.subtract).then_inc(v_lo, 1)
                attend("fox", c)
                low_out(O, PL[:, bass.ds(c, 1), :], PH[:, bass.ds(c, 1), :], PAIRS["fox"] + c)
            with dve.Fori(0, 4) as i:
                residual("wo", "mlp1", ("mlp_norm_2", KC), QH, QL, i)
            scales("mlp1", D)
            mlp(1, PH, PL)
            with dve.Fori(0, 4) as i:
                for s in range(2):
                    x = X[:, bass.ds(2 * i + s, 1), :]
                    dve.wait_ge(unit_done, unit_at(f"dn1{GROUPS - 1}", i, s) + 1)
                    dve.tensor_tensor(x, x, ACC[s][:], ALU.add).then_inc(unit_out, 1)
            scales("last", D)
            for c in range(KC):
                dve.scalar_tensor_tensor(X[:, c, :], X[:, c, :], column("final_norm_2", c), RS[:], ALU.mult, ALU.mult)\
                   .then_inc(y_normed, 1)
            for c in range(1, KC, 2):
                dve.wait_ge(y_t, c + 1)
                dve.tensor_copy(YROW[:, :, c * P:(c + 1) * P], TR[1][:].rearrange("p (b f) -> p b f", f=P))\
                   .then_inc(y_odd, 1)


_INS = ["x", "mem", "positions", "norm_mix_g", "w_in", "w_out", "conv_b_w", "conv_b_b", "ln_b_g", "ln_b_b",
        "norm_cross_g", "norm_mem_g", "w_q_cross", "w_k_cross", "w_v_cross", "w_o_cross", "norm_ffn_g", "w_gate",
        "w_up", "ffn_conv_w", "ffn_conv_b", "w_down", "norm_final_g", "mix_norm_2", "mlp_norm_2", "mlp_w1_2",
        "mlp_w2_2", "ssm_log_dt_2", "ssm_a_re_2", "ssm_a_im_2", "ssm_b_re_2", "ssm_b_im_2", "ssm_c_re_2",
        "ssm_c_im_2", "ssm_d_2", "ssm_w_glu_2", "kv_norm_2", "w_kvf_2", "b_f_2", "attn_wq_2", "attn_wo_2",
        "final_norm_2", "constants"]
_OUTS = [((1, 512, 1024), "float32")]


def kernel(**inputs):
    import concourse.bacc as bacc
    from concourse.bass_utils import run_bass_kernel_spmd

    nc = bacc.Bacc("TRN2", target_bir_lowering=False, num_devices=1)
    inputs = dict(inputs, constants=constants())
    arrays, args = {}, {}
    for name in _INS:
        a = np.ascontiguousarray(inputs[name])
        arrays[f"in_{name}_dram"] = a
        args[name] = nc.dram_tensor(f"in_{name}_dram", a.shape, mybir.dt.from_np(a.dtype), kind="ExternalInput").ap()
    shape, dtype = _OUTS[0]
    out = nc.dram_tensor("out_0_dram", shape, mybir.dt.from_np(np.dtype(dtype)), kind="ExternalOutput").ap()
    build_program(nc, args, out)
    r = run_bass_kernel_spmd(nc, [arrays], core_ids=[0])
    return r.results[0]["out_0_dram"]
```

```python
from contextlib import ExitStack

import numpy as np
import concourse.bass as bass
from concourse import mybir

F32 = mybir.dt.float32
F32R = mybir.dt.float32r
I32 = mybir.dt.int32
ALU = mybir.AluOpType
ACT = mybir.ActivationFunctionType
AX = mybir.AxisListType.X

P = 128
T = 512
TB = T // P
D = 1024
KC = D // P
NMEM = 256
MB = NMEM // P
IDXH = 4
TOPK = 128
CONVW = 31
PAD = CONVW - 1
BCH = 4
DFF = 2816
FC = DFF // P
EPS = 1e-6
THETA = 500000.0
ROT = 16
NHEAD = 16
NCST = 4 * P + 1 + 2 * NHEAD
BIG = float(2.0 ** 100)
FAR = -1.0e30
TAKEN = -3.0e38
MAGIC = 12582912.0
PI_BELOW = 3.1415925
TWO_PI = (6.28125, 0.0019350051879882812, 6.283185307179586 - 6.28125 - 0.0019350051879882812)
LN2 = (0.693359375, float(np.log(2.0)) - 0.693359375)

FFN_GROUPS = [(g, min(8, FC - g)) for g in range(0, FC, 8)]
ORDER = [("glu", 8), ("in", 8), ("memk", 8), ("memv", 8), ("out", 8), ("qc", 8), ("oc", 8)]
for _g, _n in FFN_GROUPS:
    ORDER += [(f"ffn{_g}", 2 * _n), (f"down{_g}", 8)]
GROUPS = 4 * D // P // 8
_MLP = [[(f"{_n}{_l}{_g}", 8) for _g in range(GROUPS) for _n in ("up", "dn")] for _l in range(2)]
ORDER += [("s5glu", 16)] + _MLP[0] + [("kv", 16), ("wq", 8), ("wo", 8)] + _MLP[1]
START = {}
NUNITS = 0
for _name, _c in ORDER:
    START[_name] = NUNITS
    NUNITS += _c
COUNT = dict(ORDER)

VECTORS = [("norm_mix_g", 8, 0), ("norm_cross_g", 8, 0), ("norm_mem_g", 8, 0), ("norm_ffn_g", 8, 0),
           ("norm_final_g", 8, 0), ("mix_norm_2", 16, 0), ("mlp_norm_2", 16, 0), ("kv_norm_2", 8, 0),
           ("final_norm_2", 8, 0), ("ssm_d_2", 8, 0), ("conv_b_b", 4, 0), ("ln_b_g", 4, 0), ("ln_b_b", 4, 0),
           ("conv_b_w", 124, 1), ("ffn_conv_w", 66, 2), ("ffn_conv_b", 22, 2)]
ROWS = [0, 0, 0]
COLUMN = {}
for _name, _c, _t in VECTORS:
    COLUMN[_name] = (_t, ROWS[_t])
    ROWS[_t] += _c

NORMS = [("mix", 8), ("ln", 4), ("cross", 8), ("ffn", 8), ("final", 8), ("s5", 8), ("mlp0", 8), ("kv", 8), ("mlp1", 8),
         ("last", 8)]
NORM = {name: n for n, (name, _) in enumerate(NORMS)}
SQUARES = {name: sum(c for _, c in NORMS[:n]) for n, (name, _) in enumerate(NORMS)}
NOPERAND = {"mix": 0, "cross": 8, "ffn": 16, "mlp0": 24, "kv": 32, "wq": 40, "mlp1": 48}
HIDDEN = {"ffn": 0, "s5": FC, "mlp0": FC + KC, "mlp1": FC + KC + 8 * GROUPS}
TILES = {"sparse": 0, "cross": 32, "fox": 48}
PAIRS = {"sparse": 0, "cross": 4, "fox": 12}
STAGED = {"sparse": 0, "cross": 4, "fox": 8}
HALVES = {"sparse": 1, "cross": 9, "fox": 17}


def constants():
    c = np.zeros((P, NCST), np.float32)
    c[:, 0:P] = np.eye(P)
    for m in range(P):
        if m % 64 < ROT // 2:
            c[m + ROT // 2, P + m] = -1.0
        elif m % 64 < ROT:
            c[m - ROT // 2, P + m] = 1.0
    q, k = np.meshgrid(np.arange(P), np.arange(P), indexing="ij")
    c[:, 2 * P:3 * P] = np.where(k > q, -BIG, 0.0)
    c[:, 3 * P:4 * P] = 1.0
    f = (np.float32(THETA) ** (-np.arange(0, ROT, 2, dtype=np.float32) / np.float32(ROT))).astype(np.float32)
    for m in range(P):
        if m % 64 < ROT:
            c[m, 4 * P] = f[m % (ROT // 2)]
    for h in range(NHEAD):
        c[h:64:32, 4 * P + 1 + h] = 1.0
        c[64 + h::32, 4 * P + 1 + NHEAD + h] = 1.0
    return c


def build_program(nc, A, out):
    ctx = ExitStack()
    with ctx:
        first = (nc.sbuf_base + 127) // 128 * 128

        def at(name, shape, dt, offset):
            return nc.alloc_sbuf_tensor_at(name, shape, dt, offset=first + offset)

        def bank(name):
            return ctx.enter_context(nc.psum_tensor(name, [P, 512], F32))

        def sem(name):
            return ctx.enter_context(nc.semaphore(name))

        X = at("X", [P, KC, T], F32, 0)
        PH = at("PH", [P, KC, T], F32R, 16384)
        PL = at("PL", [P, KC, T], F32R, 32768)
        QH = at("QH", [P, KC, T], F32R, 49152)
        QL = at("QL", [P, KC, T], F32R, 65536)
        RAW = at("RAW", [P, 2, KC, P], F32, 81920)
        WH = at("WH", [P, 2, KC, P], F32R, 90112)
        WL = at("WL", [P, 2, KC, P], F32R, 98304)
        QT = at("QT", [P, KC, T], F32, 106496)
        KT = at("KT", [P, KC, T], F32, 122880)
        VT = at("VT", [P, KC, T], F32, 139264)
        PTH = at("PTH", [P, TB, T], F32R, 155648)
        PTL = at("PTL", [P, TB, T], F32R, 163840)
        E = at("E", [P, 2, T], F32, 172032)
        QSH = [at("QSH", [P, T], F32R, 176128), at("QSH1", [P, T], F32R, 65536)]
        QSL = [at("QSL", [P, T], F32R, 178176), at("QSL1", [P, T], F32R, 67584)]
        KSH = [at("KSH", [P, T], F32R, 180224), at("KSH1", [P, T], F32R, 69632)]
        KSL = [at("KSL", [P, T], F32R, 182272), at("KSL1", [P, T], F32R, 71680)]
        VS = at("VS", [P, T], F32, 184320)
        VSH = [at("VSH", [P, TB, 2, P], F32R, 186368), at("VSH1", [P, TB, 2, P], F32R, 73728)]
        VSL = [at("VSL", [P, TB, 2, P], F32R, 190464), at("VSL1", [P, TB, 2, P], F32R, 77824)]
        AQH = [QSH[0], at("AQH1", [P, T], F32R, 43008)]
        AQL = [QSL[0], at("AQL1", [P, T], F32R, 45056)]
        CST = at("CST", [P, NCST], F32, 194560)
        IDR = at("IDR", [P, P], F32R, 196768)
        TRIR = at("TRIR", [P, P], F32R, 197280)
        RS = at("RS", [P, T], F32, 197792)
        SSQ = at("SSQ", [P, T], F32, 199840)
        SQ = at("SQ", [P, 2, T], F32, 201888)
        DIAG = at("DIAG", [P, T], F32, 205984)
        VEC = at("VEC", [P, 3, P], F32, 208032)
        V4 = at("V4", [P, 4], F32, 209568)
        SD4 = at("SD4", [P, 4], F32, 209600)
        R4 = at("R4", [P, 4], F32, 209632)
        WI = at("WI", [P, TB, 4], F32, 209664)
        M8 = at("M8", [P, 3, 8], F32, 209728)
        NMX = at("NMX", [P, 4, 1], F32, 209824)
        SUM = at("SUM", [P, 4, 1], F32, 209856)
        REC = at("REC", [P, 4, 1], F32, 209888)
        XROW = at("XROW", [P, TB, D], F32, 106496)
        MROW = at("MROW", [P, MB, D], F32, 122880)
        VROW = at("VROW", [P, 3, P], F32, 155648)
        POSI = at("POSI", [P, T], I32, 163840)
        MSQ = at("MSQ", [P, D], F32, 172032)
        DS = at("DS", [P, KC, T], F32, 106496)
        KM = at("KM", [P, KC, NMEM], F32, 122880)
        VM = at("VM", [P, KC, NMEM], F32, 131072)
        U = at("U", [P, BCH, PAD + T], F32, 139264)
        COS = at("COS", [P, T], F32, 147968)
        SIN = at("SIN", [P, T], F32, 150016)
        SC = at("SC", [P, 3, T], F32, 16384)
        SEL = at("SEL", [P, TB, T], F32R, 22528)
        KD = at("KD", [P, 2, T], F32, 30720)
        CV = at("CV", [P, BCH, T], F32, 34816)
        G = at("G", [P, 2 + T], F32, 155648)
        H1 = at("H1", [P, T], F32, 157760)
        H2 = at("H2", [P, T], F32, 159808)
        JP = 32
        BB = at("BB", [P, 2, JP, 16], F32, 139264)
        CC = at("CC", [P, 2, JP, 16], F32, 143360)
        PW = at("PW", [P, 2, 9, JP], F32, 147456)
        UT = at("UT", [P, 2, JP], F32, 149760)
        RHO8 = at("RHO8", [P, JP], F32, 150016)
        LAM = at("LAM", [P, 3, JP], F32, 150144)
        SW = at("SW", [P, 10, JP], F32, 150528)
        S5ROW = at("S5ROW", [JP, 3, P], F32, 151808)
        POW2 = at("POW2", [P, JP], I32, 153600)
        DTROW = at("DTROW", [JP, 2], F32, 153344)
        ET = at("ET", [P, 2, JP, 64], F32, 122880)
        U5 = at("U5", [P, KC, T], F32, 106496)
        CROW = at("CROW", [P, 2, KC, 2, 64], F32, 16384)
        BRAW = at("BRAW", [P, 2, JP, 16], F32, 24576)
        BT = at("BT", [P, 2, JP, 16], F32, 28672)
        W1T = at("W1T", [P, 8, 2, 4, 2, 16], F32, 16384)
        W1 = at("W1", [P, 16, P], F32, 24576)
        KB = at("KB", [P, 2, 8, P], F32, 32768)
        SPV = at("SPV", [P, 2, 4, 64], F32, 40960)
        VR = at("VR", [P, 2, 4, 64], F32, 43008)
        WR = at("WR", [P, 2, 4, 64], F32, 45056)
        CL = at("CL", [P, 2, 2, 9, 4, 2, 16], F32, 155648)
        GT = at("GT", [P, 2, 9, 4, 16], F32, 174080)
        RHOT = at("RHOT", [P, 4, 64], F32, 178688)
        RT = at("RT", [P, 2, 4, 64], F32, 179712)
        YC = at("YC", [P, 2, T], F32, 181760)
        UC = at("UC", [P, 2, T], F32, 185856)
        CQH = [at("CQH", [P, 2, T], F32R, 176128), at("CQH1", [P, 2, T], F32R, 32768)]
        CQL = [at("CQL", [P, 2, T], F32R, 180224), at("CQL1", [P, 2, T], F32R, 36864)]
        CVS = at("CVS", [P, 2, NMEM], F32, 184320)
        CKH = [at("CKH", [P, 2, NMEM], F32R, 186368), at("CKH1", [P, 2, NMEM], F32R, 40960)]
        CKL = [at("CKL", [P, 2, NMEM], F32R, 188416), at("CKL1", [P, 2, NMEM], F32R, 43008)]
        CVH = [at("CVH", [P, MB, 2 * P], F32R, 190464), at("CVH1", [P, MB, 2 * P], F32R, 45056)]
        CVL = [at("CVL", [P, MB, 2 * P], F32R, 192512), at("CVL1", [P, MB, 2 * P], F32R, 47104)]
        MH = QH[:, 0:4, :].rearrange("p a (b n) -> p (a b) n", n=NMEM)
        ML = QL[:, 0:4, :].rearrange("p a (b n) -> p (a b) n", n=NMEM)
        FWR = at("FWR", [P, KC, P], F32, 163840)
        FWH = at("FWH", [P, KC, P], F32R, 167936)
        FWL = at("FWL", [P, KC, P], F32R, 176128)
        FZ = at("FZ", [P, T], F32, 172032)
        F = at("F", [P, T], F32, 174080)
        BF = at("BF", [P, 1], F32, 209920)
        LQ = at("LQ", [P, 4, T], F32R, 49152)
        RK = at("RK", [P, 4, T], F32R, 57344)
        LF = at("LF", [P, T], F32R, 201888)
        RF = at("RF", [P, T], F32R, 203936)
        FH = at("FH", [P, T], F32R, 199840)
        FL = at("FL", [P, T], F32R, 205984)
        YROW = at("YROW", [P, TB, D], F32, 106496)
        HOT = CST[:, 4 * P + 1:NCST]
        IDENT, ROTM, TRI, ONES = (CST[:, i * P:(i + 1) * P] for i in range(4))
        FREQ = CST[:, 4 * P:4 * P + 1]
        ET4 = [E[:, 0, :], E[:, 1, :], at("E2", [P, T], F32, 199840)[:], at("E3", [P, T], F32, 205984)[:]]
        TA, TB_ = E[:, 0, :], E[:, 1, :]

        def column(name, i):
            name, first = name if isinstance(name, tuple) else (name, 0)
            t, base = COLUMN[name][0], COLUMN[name][1] + first
            return VEC[:, t, bass.ds(base + i, 1)]

        ACC = [bank("ACC0"), bank("ACC1")]
        ST = bank("ST")
        FOUR = ctx.enter_context(nc.psum_tensor("FOUR", [P, 4, 512], F32))
        S = [FOUR[:, 0, :], FOUR[:, 1, :]]
        TR = [FOUR[:, 2, :], FOUR[:, 3, :]]
        O = bank("O")
        SB = [FOUR[:, j, :] for j in range(4)]
        TT = ACC

        w_landed = [sem("w_landed0"), sem("w_landed1")]
        w_hi = sem("w_hi")
        w_lo = sem("w_lo")
        unit_done = sem("unit_done")
        unit_out = sem("unit_out")
        cst_in = sem("cst_in")
        vec_in = sem("vec_in")
        x_in = sem("x_in")
        mem_in = sem("mem_in")
        cst_r = sem("cst_r")
        vec_t = sem("vec_t")
        vec_c = sem("vec_c")
        x_t = sem("x_t")
        x_ready = sem("x_ready")
        op_hi = sem("op_hi")
        op_lo = sem("op_lo")
        sq_ready = sem("sq_ready")
        sq_used = sem("sq_used")
        st_sum, st_var, st_std, st_diag, st_bc, st_rs = (
            sem(n) for n in ("st_sum", "st_var", "st_std", "st_diag", "st_bc", "st_rs"))
        mem_sq, mem_var, mem_std, mem_scaled, mem_t, mem_hi, mem_lo = (
            sem(n) for n in ("mem_sq", "mem_var", "mem_std", "mem_scaled", "mem_t", "mem_hi", "mem_lo"))
        pos_in, ang, angc, tables = sem("pos_in"), sem("ang"), sem("angc"), sem("tables")
        u_zero, gate_raw, gate_sig = sem("u_zero"), sem("gate_raw"), sem("gate_sig")
        rot_done, rot_used, rope_cos, rope_done = (
            sem(n) for n in ("rot_done", "rot_used", "rope_cos", "rope_done"))
        kd_in = [sem("kd_in0"), sem("kd_in1")]
        wi_t, wi_in, v_t, pad_zero, v_hi, v_lo = (sem(n) for n in ("wi_t", "wi_in", "v_t", "pad_zero", "v_hi", "v_lo"))
        index_mm, index_relu, index_sum, index_masked, sel_ready = (
            sem(n) for n in ("index_mm", "index_relu", "index_sum", "index_masked", "sel_ready"))
        conv_done, mean_sum, centred, ln_scaled, silu_done, branch_hi, branch_lo = (
            sem(n) for n in ("conv_done", "mean_sum", "centred", "ln_scaled", "silu_done", "branch_hi", "branch_lo"))
        g_zero, gate_conv, gate_act, hid_ready, hid_hi, hid_lo = (
            sem(n) for n in ("g_zero", "gate_conv", "gate_act", "hid_ready", "hid_hi", "hid_lo"))
        row_in, c_in, b_in, row_t, row_out, c_t, c_out = (
            sem(n) for n in ("s5_row_in", "s5_c_in", "s5_b_in", "s5_row_t", "s5_row_out", "s5_c_t", "s5_c_out"))
        angle_ready, sin_cos, den_inv, params = (
            sem(n) for n in ("angle_ready", "sin_cos", "den_inv", "s5_params"))
        zeroed, gen_ready, w1_t, w1_in, k_mm, kb_in, l_mm, l_used, sp_ready, y_mm, y_out, gelu_done, rho_ready = (
            sem(n) for n in ("s5_zeroed", "gen_ready", "w1_t", "w1_in", "k_mm", "kb_in", "l_mm", "l_used", "sp_ready",
                             "y_mm", "y_out", "gelu_done", "rho_ready"))
        normed_x, u5_ready, uc_ready = sem("normed_x"), sem("u5_ready"), sem("uc_ready")
        glu_out = sem("glu_out")
        fw_zero, fw_in, fw_hi, fw_lo, f_mm, f_abs, f_exp, f_ln, f_sum, f_ready, hot = (
            sem(n) for n in ("fw_zero", "fw_in", "fw_hi", "fw_lo", "f_mm", "f_abs", "f_exp", "f_ln", "f_sum", "f_ready",
                             "hot"))
        y_normed, y_t, y_even, y_odd, stored = (sem(n) for n in ("y_normed", "y_t", "y_even", "y_odd", "stored"))
        q_hi = sem("q_hi")
        q_lo = sem("q_lo")
        s_ready = sem("s_ready")
        mx_ready = sem("mx_ready")
        e_done = sem("e_done")
        e_scaled = sem("e_scaled")
        t_ready = sem("t_ready")
        pt_hi = sem("pt_hi")
        pt_lo = sem("pt_lo")
        pv_done = sem("pv_done")
        cvs_in, k_lo = sem("cvs_in"), sem("k_lo")
        staged = sem("staged")
        o_hi, o_lo = sem("o_hi"), sem("o_lo")

        def weights(name):
            return A[name].rearrange("l (c p) n -> (l c) p n", p=P).rearrange("c p n -> p c n")

        w_in, w_out = weights("w_in"), weights("w_out")
        w_k, w_v = weights("w_k_cross"), weights("w_v_cross")
        w_qc, w_oc = weights("w_q_cross"), weights("w_o_cross")
        w_gate, w_up, w_down = weights("w_gate"), weights("w_up"), weights("w_down")
        w_glu, w_q, w_o = weights("ssm_w_glu_2"), weights("attn_wq_2"), weights("attn_wo_2")
        w_kvf = A["w_kvf_2"].rearrange("(c p) n -> p c n", p=P)
        w_up2 = [A["mlp_w1_2"][l].rearrange("(c p) n -> p c n", p=P) for l in range(2)]
        w_down2 = [A["mlp_w2_2"][l].rearrange("(c p) n -> p c n", p=P) for l in range(2)]
        IN_COLS = [896, 640, 768, 512, 0, 128, 256, 384]
        GA, GG = 964, 1476

        def groups(eng, n, group):
            group(0, 0, True, False)
            with eng.Fori(0, n // 2 - 1) as i:
                group(2 * i + 1, 1, False, False)
                group(2 * i + 2, 0, False, False)
            group(n - 1, 1, False, True)

        def keys(kind, t):
            return NMEM if kind == "cross" else (t % TB + 1) * P

        SLOTS = {"sparse": 4, "cross": 2, "fox": 4}
        AHEAD = {"sparse": 3, "cross": 2, "fox": 3}
        SIZE = {"sparse": 8, "cross": 4, "fox": 8}
        OUT = {"sparse": (QH, QL), "cross": (QH, QL), "fox": (PH, PL)}

        def unit_at(name, i, s, g=0):
            return START[name] + 2 * i + s

        block = ctx.enter_context(nc.Block())

        @block.sync
        def _(sp):
            def load(u, s, src):
                if not isinstance(u, int) or u >= 2:
                    sp.wait_ge(w_lo, u - 1)
                sp.dma_start(RAW[:, s, 0:src.shape[1], :], src).then_inc(w_landed[s], 16)

            sp.dma_start(CST[:], A["constants"]).then_inc(cst_in, 16)
            sp.dma_start(XROW[:], A["x"][0].rearrange("(b p) d -> p b d", p=P)).then_inc(x_in, 16)
            sp.dma_start(MROW[:], A["mem"][0].rearrange("(b p) d -> p b d", p=P)).then_inc(mem_in, 16)
            for s in range(2):
                load(s, s, w_in[:, :, (GA, GG)[s]:(GA, GG)[s] + P])
            with sp.Fori(1, 4) as i:
                for s in range(2):
                    load(unit_at("glu", i, s), s, w_in[:, :, bass.ds(i * P + (GA, GG)[s], P)])
            for j, c in enumerate(IN_COLS):
                load(START["in"] + j, j % 2, w_in[:, :, c:c + P])
            for name, w in (("memk", w_k), ("memv", w_v), ("out", w_out), ("qc", w_qc), ("oc", w_oc)):
                with sp.Fori(0, 4) as i:
                    for s in range(2):
                        load(unit_at(name, i, s), s, w[:, :, bass.ds(i * 2 * P + s * P, P)])
                if name == "qc":
                    sp.wait_ge(conv_done, BCH)
                    for j, x in enumerate(("ssm_a_re_2", "ssm_a_im_2")):
                        sp.dma_start(S5ROW[:, j, :], A[x][0].rearrange("(j g) p -> j (g p)", g=2)).then_inc(row_in, 16)
                    sp.dma_start(DTROW[:], A["ssm_log_dt_2"][0].rearrange("(j g) -> j g", g=2)).then_inc(row_in, 16)
                    sp.wait_ge(unit_done, START["oc"])
                    for ri, x in enumerate(("ssm_b_re_2", "ssm_b_im_2")):
                        sp.dma_start(BRAW[:, ri], A[x][0].rearrange("(j g) p c -> (g p) j c", g=2)).then_inc(b_in, 16)
                    for ri, x in enumerate(("ssm_c_re_2", "ssm_c_im_2")):
                        rows = A[x][0].rearrange("(k g) c p -> (g c) k p", k=KC)
                        for twice in range(2):
                            sp.dma_start(CROW[:, ri, :, twice, :], rows).then_inc(c_in, 16)
            for g, n in FFN_GROUPS:
                with sp.Fori(0, n) as i:
                    for s, w in enumerate((w_gate, w_up)):
                        load(unit_at(f"ffn{g}", i, s), s, w[:, :, bass.ds(i * P + g * P, P)])
                with sp.Fori(0, 4) as i:
                    for s in range(2):
                        load(unit_at(f"down{g}", i, s), s, w_down[:, g:g + n, bass.ds(i * 2 * P + s * P, P)])
            def loads(name, n, w, rows=slice(0, KC), first=0):
                with sp.Fori(0, n // 2) as i:
                    for s in range(2):
                        load(unit_at(name, i, s), s, w[:, rows, bass.ds(i * 2 * P + (s * P + first), P)])

            def mlp(l):
                for g in range(GROUPS):
                    loads(f"up{l}{g}", 8, w_up2[l], first=g * KC * P)
                    loads(f"dn{l}{g}", 8, w_down2[l], slice(g * KC, (g + 1) * KC))

            with sp.Fori(0, 8) as i:
                for s in range(2):
                    load(unit_at("s5glu", i, s), s, w_glu[:, :, bass.ds(i * P + s * D, P)])
            mlp(0)
            sp.wait_ge(fw_zero, 1)
            for j in range(4):
                sp.dma_start(FWR[:, :, 32 * j:32 * j + NHEAD], w_kvf[:, :, 2 * D:2 * D + NHEAD]).then_inc(fw_in, 16)
                sp.dma_start(BF[32 * j:32 * j + NHEAD, :], A["b_f_2"].rearrange("(h o) -> h o", o=1)).then_inc(fw_in, 16)
            loads("kv", 16, w_kvf)
            loads("wq", 8, w_q)
            loads("wo", 8, w_o)
            mlp(1)
            for c in range(KC):
                sp.wait_ge((y_even, y_odd)[c % 2], c // 2 + 1)
                sp.dma_start(out[0].rearrange("(b p) d -> p b d", p=P)[:, :, c * P:(c + 1) * P],
                             YROW[:, :, c * P:(c + 1) * P]).then_inc(stored, 16)
            sp.wait_ge(stored, 16 * KC)

        @block.scalar
        def _(act):
            def round_weights(u, s):
                act.wait_ge(w_landed[s], (u - s) * 8 + 16)
                if not isinstance(u, int) or u >= 2:
                    act.wait_ge(unit_done, u - 1)
                act.activation(WH[:, s], RAW[:, s], ACT.Copy).then_inc(w_hi, 1)

            def prepare(norm, c, gain, hi, s, ready):
                square_free(norm, c)
                act.wait_ge(*ready)
                act.activation(hi, X[:, bass.ds(c, 1), :], ACT.Copy, scale=column(gain, c)).then_inc(op_hi, 1)
                act.activation(SQ[:, s, :], X[:, bass.ds(c, 1), :], ACT.Square).then_inc(sq_ready, 1)

            def square_free(norm, c):
                if not isinstance(c, int) or SQUARES[norm] + c >= 2:
                    act.wait_ge(sq_used, SQUARES[norm] + c - 1)

            def square(norm, c, x, s):
                square_free(norm, c)
                act.activation(SQ[:, s, :], x[:, bass.ds(c, 1), :], ACT.Square).then_inc(sq_ready, 1)

            def standard_deviation(norm):
                act.wait_ge(st_var, NORM[norm] + 1)
                act.activation(SD4[:], V4[:], ACT.Sqrt).then_inc(st_std, 1)

            act.dma_start(POSI[:], A["positions"].to_broadcast([P, T])).then_inc(pos_in, 16)
            for name, rows, t in VECTORS:
                r = COLUMN[name][1]
                flat = A[name] if len(A[name].shape) == 1 else A[name].rearrange(
                    "a b -> (a b)") if len(A[name].shape) == 2 else A[name].rearrange("a b c -> (a b c)")
                act.dma_start(VROW[r:r + rows, t, :], flat.rearrange("(r p) -> r p", p=P)).then_inc(vec_in, 16)
            act.wait_ge(cst_in, 16)
            act.activation(IDR[:], IDENT, ACT.Copy).then_inc(cst_r, 1)
            act.activation(TRIR[:], TRI, ACT.Copy).then_inc(cst_r, 1)
            round_weights(0, 0)
            act.wait_ge(mem_in, 16)
            for b in range(MB):
                act.activation(MSQ[:], MROW[:, b, :], ACT.Square, accum_out=V4[:, b:b + 1]).then_inc(mem_sq, 1)
                act.drain()
            act.wait_ge(mem_var, 1)
            act.activation(SD4[:, 0:MB], V4[:, 0:MB], ACT.Sqrt).then_inc(mem_std, 1)
            act.wait_ge(vec_c, 1)
            for c in range(KC):
                prepare("mix", c, "norm_mix_g", PH[:, c, :], c % 2, (x_ready, c + 1))
            for c in range(KC):
                act.wait_ge(mem_t, c + 1)
                act.activation(MH[:, c, :], S[c % 2][:, 0:NMEM], ACT.Copy, scale=column("norm_mem_g", c))\
                   .then_inc(mem_hi, 1)
            act.wait_ge(ang, 1)
            act.activation(SIN[:], SIN[:], ACT.Sin).then_inc(tables, 1)
            act.activation(COS[:], COS[:], ACT.Sin).then_inc(tables, 1)

            def glu(i):
                for s in range(2):
                    round_weights(unit_at("glu", i, s) + 1, 1 - s)
                    if s == 0 and isinstance(i, int):
                        standard_deviation("mix")
                act.wait_ge(gate_raw, i + 1)
                act.activation(TB_, TB_, ACT.Sigmoid).then_inc(gate_sig, 1)

            glu(0)
            with act.Fori(1, 4) as i:
                glu(i)
            for u in range(START["in"], START["memk"]):
                round_weights(u + 1, (u + 1) % 2)
            for j, slot in ((0, 1), (1, 4)):
                act.wait_ge(rope_done, slot)
                act.dma_start(KD[64:P, j, :], KD[0:64, j, :]).then_inc(kd_in[j], 16)
            act.wait_ge(v_t, 1)
            act.wait_ge(pad_zero, 2)
            for half in range(2):
                act.activation(VSH[0][:, :, half, half * 64:half * 64 + 64],
                               S[0][:, 0:TB * 64].rearrange("p (b f) -> p b f", b=TB), ACT.Copy).then_inc(v_hi, 1)
            act.wait_ge(kd_in[1], 16)
            act.activation(KSH[0][:], KD[:, 1, :], ACT.Copy).then_inc(v_hi, 1)
            act.wait_ge(rope_done, 8)
            for n in range(3 * IDXH):
                nk = (n // IDXH + 2) * P
                act.wait_ge(index_mm, n + 1)
                if n >= 2:
                    act.wait_ge(index_sum, n - 1)
                act.activation(E[:, n % 2, 0:nk], S[n % 2][:, 0:nk], ACT.Relu).then_inc(index_relu, 1)
            for name, to in (("memk", KM), ("memv", VM)):
                with act.Fori(0, 4) as i:
                    for s in range(2):
                        u = unit_at(name, i, s)
                        round_weights(u + 1, 1 - s)
                        act.wait_ge(unit_done, u + 1)
                        act.activation(to[:, bass.ds(2 * i + s, 1), :], ACC[s][:, 0:NMEM], ACT.Copy)\
                           .then_inc(unit_out, 1)

            def exponentials(kind, n, t):
                nk, j = keys(kind, t % SIZE[kind]), t % SLOTS[kind]
                act.wait_ge(mx_ready, n + 1)
                act.wait_ge(t_ready, n + 5 - SLOTS[kind])
                act.activation(ET4[j][:, 0:nk], SB[j][:, 0:nk], ACT.Exp, bias=NMX[:, j, :],
                               accum_out=SUM[:, j, :]).then_inc(e_done, 1)

            def turned_high(kind, c, t):
                n, qb, kb = TILES[kind] + SIZE[kind] * c + t, t % TB, keys(kind, t) // P
                act.wait_ge(t_ready, n + 5)
                if qb == 0:
                    act.wait_ge(pv_done, HALVES[kind] + 2 * c + t // TB)
                act.activation(PTH[:, 0:kb, qb * P:(qb + 1) * P],
                               TT[t % 2][:, 0:kb * P].rearrange("p (k q) -> p k q", q=P), ACT.Copy).then_inc(pt_hi, 1)

            def out_high(kind, c):
                for m in range(1 + (kind == "cross")):
                    chunk = bass.ds(2 * c + m if kind == "cross" else c, 1)
                    high_out((O, ST)[m], OUT[kind][0][:, chunk, :],
                             HALVES[kind] + 2 * c + (m + 1 if kind == "cross" else 2))

            def values_high(kind, c, b):
                if kind == "cross":
                    act.wait_ge(v_t, c + 2)
                    act.activation(CVH[b][:], SB[3].rearrange("p (b f) -> p b f", b=MB), ACT.Copy).then_inc(v_hi, 1)
                if kind == "fox":
                    act.wait_ge(v_t, c + 6)
                    for half in range(2):
                        act.activation(VSH[b][:, :, half, half * 64:half * 64 + 64],
                                       ST[:].rearrange("p (b h f) -> p b h f", b=TB, h=2)[:, :, half, :], ACT.Copy)\
                           .then_inc(v_hi, 1)

            def heads_high(c, b):
                act.activation(CQH[b][:], QT[:, bass.ds(2 * c, 2), :], ACT.Copy).then_inc(q_hi, 1)
                act.activation(CKH[b][:], KM[:, bass.ds(2 * c, 2), :], ACT.Copy).then_inc(q_hi, 1)

            def attend(kind, n_groups):
                size, ahead = SIZE[kind], 2

                def group(c, b, first, last):
                    n = TILES[kind] + size * c
                    for t in range(size):
                        if not last or t + ahead < size:
                            exponentials(kind, n + t + ahead, t + ahead)
                        turned_high(kind, c, t)
                        if t == 0 and not first:
                            out_high(kind, c - 1)
                        if t == 1 and kind == "cross" and not last:
                            heads_high(c + 1, 1 - b)
                        if t == size - 2 and not last:
                            values_high(kind, c + 1, 1 - b)

                if kind == "cross":
                    heads_high(0, 0)
                values_high(kind, 0, 0)
                for t in range(ahead):
                    exponentials(kind, TILES[kind] + t, t)
                groups(act, n_groups, group)
                out_high(kind, n_groups - 1)

            def high_out(bank_, to, k):
                act.wait_ge(pv_done, k)
                act.activation(to, bank_[:], ACT.Copy).then_inc(o_hi, 1)

            def hidden(ready, k, to, value, hi=QH):
                act.wait_ge(ready, value)
                act.activation(hi[:, bass.ds(k, 1), :], to, ACT.Copy).then_inc(hid_hi, 1)

            act.sem_inc(e_done, 4)
            attend("sparse", 4)
            for c in range(BCH):
                act.wait_ge(centred, c + 1)
                square("ln", c, CV, c % 2)
            standard_deviation("ln")
            for c in range(BCH):
                act.wait_ge(ln_scaled, c + 1)
                act.activation(CV[:, c, :], CV[:, c, :], ACT.Silu, bias=column("ln_b_b", c),
                               scale=column("ln_b_g", c)).then_inc(silu_done, 1)
                act.wait_ge(silu_done, c + 1)
                act.activation(QH[:, 4 + c, :], CV[:, c, :], ACT.Copy).then_inc(branch_hi, 1)

            def residual(name, norm, gain, hi, i, g=None):
                for s in range(2):
                    u = START[name] + 2 * i + s
                    c = 2 * i + s
                    round_weights(u + 1, 1 - s)
                    prepare(norm, c, gain, hi[:, bass.ds(c, 1), :], s, (unit_out, u + 1))

            residual("out", "cross", "norm_cross_g", PH, 0)
            with act.Fori(1, 4) as i:
                residual("out", "cross", "norm_cross_g", PH, i)

            def plain(name, i, norm=None):
                for s in range(2):
                    round_weights(unit_at(name, i, s) + 1, 1 - s)
                    if s == 0 and norm:
                        standard_deviation(norm)

            plain("qc", 0, "cross")
            with act.Fori(1, 4) as i:
                plain("qc", i)
            act.wait_ge(angle_ready, 1)
            act.activation(SW[:, 4, :], SW[:, 1, :], ACT.Sin)
            act.activation(SW[:, 6, :], SW[:, 9, :], ACT.Sin).then_inc(sin_cos, 1)
            attend("cross", 4)
            residual("oc", "ffn", "norm_ffn_g", PH, 0)
            with act.Fori(1, 4) as i:
                residual("oc", "ffn", "norm_ffn_g", PH, i)
            for g, n in FFN_GROUPS:
                def ffn(i):
                    for s in range(2):
                        round_weights(unit_at(f"ffn{g}", i, s) + 1, 1 - s)
                        if s == 0 and isinstance(i, int):
                            standard_deviation("ffn")
                    act.wait_ge(gate_conv, g + i + 1)
                    act.activation(H1[:], H1[:], ACT.Silu).then_inc(gate_act, 1)
                    hidden(hid_ready, i, H2[:], g + i + 1)

                if g == 0:
                    ffn(0)
                with act.Fori(g == 0, n) as i:
                    ffn(i)
                with act.Fori(0, 4) as i:
                    for s in range(2):
                        u = unit_at(f"down{g}", i, s)
                        round_weights(u + 1, 1 - s)
                        if g == FFN_GROUPS[-1][0]:
                            act.wait_ge(unit_out, u + 1)
                            square("final", 2 * i + s, X, s)
            standard_deviation("final")
            for c in range(KC):
                act.wait_ge(normed_x, c + 1)
                square("s5", c, X, c % 2)
            standard_deviation("s5")

            def mixer_input(c, b):
                act.wait_ge(u5_ready, c + 1)
                if not isinstance(c, int) or c >= 2:
                    act.wait_ge(y_mm, c - 1)
                act.activation(UC[:, b, :], U5[:, bass.ds(c, 1), :], ACT.Copy).then_inc(uc_ready, 1)

            def mixer(c, b, more):
                if more:
                    for k in range(4):
                        act.wait_ge(w1_t, 4 * c + 4 + k + 1)
                        if k == 0:
                            act.wait_ge(l_mm, c + 1)
                        act.activation(W1[:, 4 * k:4 * k + 4, :], ACC[k % 2][:].rearrange("p (a b) -> p a b", b=P),
                                       ACT.Copy).then_inc(w1_in, 1)
                act.wait_ge(y_out, c + 1)
                act.activation(YC[:, b, :], YC[:, b, :], ACT.Gelu_apprx_tanh).then_inc(gelu_done, 1)
                hidden(gelu_done, c, YC[:, b, :], c + 1)
                if not isinstance(c, int):
                    mixer_input(c + 2, b)

            for c in range(2):
                mixer_input(c, c)
            for k in range(4):
                act.wait_ge(w1_t, k + 1)
                act.activation(W1[:, 4 * k:4 * k + 4, :], ACC[k % 2][:].rearrange("p (a b) -> p a b", b=P),
                               ACT.Copy).then_inc(w1_in, 1)
            with act.Fori(0, 3) as i:
                for b in range(2):
                    mixer(2 * i + b, b, True)
            mixer(6, 0, True)
            mixer(7, 1, False)

            with act.Fori(0, 4) as i:
                for b in range(2):
                    c = 2 * i + b
                    for s in range(2):
                        round_weights(unit_at("s5glu", c, s) + 1, 1 - s)
                    act.wait_ge(unit_done, unit_at("s5glu", c, 1) + 1)
                    act.activation(TB_, ACC[1][:], ACT.Sigmoid).then_inc(gate_sig, 1)
                    prepare("mlp0", c, "mlp_norm_2", PH[:, bass.ds(c, 1), :], b, (glu_out, c + 1))

            def mlp(l, hi, following):
                norm = f"mlp{l}"
                for g in range(GROUPS):
                    def up(i):
                        for s in range(2):
                            round_weights(unit_at(f"up{l}{g}", i, s) + 1, 1 - s)
                            if s == 0 and isinstance(i, int):
                                standard_deviation(norm)
                            hidden(hid_ready, 2 * i + s, (H1, H2)[s][:], HIDDEN[norm] - KC + g * KC + 2 * i + s + 1, hi)

                    if g == 0:
                        up(0)
                    with act.Fori(g == 0, 4) as i:
                        up(i)
                    if g < GROUPS - 1:
                        with act.Fori(0, 4) as i:
                            for s in range(2):
                                round_weights(unit_at(f"dn{l}{g}", i, s) + 1, 1 - s)
                following()

            def mlp0_end():
                with act.Fori(0, 4) as i:
                    residual(f"dn0{GROUPS - 1}", "kv", "kv_norm_2", PH, i)

            def mlp1_end():
                def down(i, last):
                    for s in range(2):
                        u = unit_at(f"dn1{GROUPS - 1}", i, s)
                        if s == 0 or not last:
                            round_weights(u + 1, 1 - s)
                        act.wait_ge(unit_out, u + 1)
                        square("last", 2 * i + s, X, s)

                with act.Fori(0, 3) as i:
                    down(i, False)
                down(3, True)

            mlp(0, QH, mlp0_end)
            act.wait_ge(fw_in, 128)
            act.activation(FWH[:], FWR[:], ACT.Copy).then_inc(fw_hi, 1)

            def kv(i, b):
                c = 2 * i + b
                for s in range(2):
                    round_weights(unit_at("kv", c, s) + 1, 1 - s)
                    if s == 0 and isinstance(c, int) and c == 0:
                        standard_deviation("kv")
                if b == 0 and isinstance(i, int):
                    act.wait_ge(unit_done, START["kv"])
                act.activation(QH[:, bass.ds(c, 1), :], X[:, bass.ds(c, 1), :], ACT.Copy,
                               scale=column(("mix_norm_2", KC), c)).then_inc(op_hi, 1)

            kv(0, 0)
            kv(0, 1)
            with act.Fori(1, 4) as i:
                for b in range(2):
                    kv(i, b)
            act.wait_ge(f_abs, 1)
            act.activation(F[:], F[:], ACT.Exp, scale=-1.0).then_inc(f_exp, 1)
            act.wait_ge(f_exp, 1)
            act.activation(F[:], F[:], ACT.Ln, bias=ONES[:, 0:1]).then_inc(f_ln, 1)
            with act.Fori(0, 4) as i:
                plain("wq", i)
            act.wait_ge(unit_done, START["wo"])
            act.wait_ge(f_sum, 1)
            act.activation(FH[:], F[:], ACT.Copy).then_inc(f_ready, 1)
            act.wait_ge(f_ready, 1)
            act.activation(RF[0:32, :], FH[0:32, :].bitcast(F32), ACT.Copy, scale=-1.0)
            act.activation(LF[64:96, :], FH[64:96, :].bitcast(F32), ACT.Copy)
            act.drain().then_inc(f_ready, 1)
            attend("fox", 8)
            with act.Fori(0, 4) as i:
                residual("wo", "mlp1", ("mlp_norm_2", KC), QH, i)
            mlp(1, PH, mlp1_end)
            standard_deviation("last")
            for c in range(0, KC, 2):
                act.wait_ge(y_t, c + 1)
                act.activation(YROW[:, :, c * P:(c + 1) * P], TR[0][:].rearrange("p (b f) -> p b f", f=P), ACT.Copy)\
                   .then_inc(y_even, 1)

        @block.gpsimd
        def _(pool):
            def remainder(u, s):
                pool.wait_ge(w_hi, u + 1)
                pool.tensor_tensor(WL[:, s], RAW[:, s], WH[:, s], ALU.subtract).then_inc(w_lo, 1)

            def add_square(norm, c, s):
                pool.wait_ge(sq_ready, SQUARES[norm] + c + 1)
                if isinstance(c, int) and c == 0:
                    if NORM[norm]:
                        pool.wait_ge(st_sum, NORM[norm])
                    pool.tensor_copy(SSQ[:], SQ[:, s, :]).then_inc(sq_used, 1)
                else:
                    pool.tensor_tensor(SSQ[:], SSQ[:], SQ[:, s, :], ALU.add).then_inc(sq_used, 1)
                pool.drain()

            pool.memset(U[:, :, 0:PAD], 0.0).then_inc(u_zero, 1)
            pool.memset(VSH[0][:].bitcast(F32), 0.0).then_inc(pad_zero, 1)
            pool.memset(VSL[0][:].bitcast(F32), 0.0).then_inc(pad_zero, 1)
            remainder(0, 0)
            for c in range(KC):
                add_square("mix", c, c % 2)
            with pool.Fori(0, 4) as i:
                for s in range(2):
                    remainder(unit_at("glu", i, s) + 1, 1 - s)
            for j in range(8):
                remainder(START["in"] + j + 1, (j + 1) % 2)
            for j in range(8):
                rows = P if j not in (0, 3) else 64
                pool.wait_ge(rot_done, j + 1)
                pool.tensor_tensor(DS[0:rows, j, :], DS[0:rows, j, :], COS[0:rows, :], ALU.mult).then_inc(rope_cos, 1)
            pool.wait_ge(v_hi, 3)
            pool.tensor_tensor(KSL[0][:], KD[:, 1, :], KSH[0][:], ALU.subtract).then_inc(k_lo, 1)
            for qb in range(1, TB):
                diagonal = SC[:, qb - 1, qb * P:(qb + 1) * P]
                pool.wait_ge(index_sum, IDXH * qb)
                pool.affine_select(out=diagonal, in_=diagonal, compare_op=ALU.is_ge, fill=FAR, base=0,
                                   pattern=[[-1, P]], channel_multiplier=1).then_inc(index_masked, 1)
            for name in ("memk", "memv"):
                with pool.Fori(0, 4) as i:
                    for s in range(2):
                        remainder(unit_at(name, i, s) + 1, 1 - s)
            def free(kind, c, first):
                if not first:
                    pool.wait_ge(e_done, TILES[kind] + SIZE[kind] * (c - 1) + 4)

            def queries(c, b, first, last):
                free("sparse", c, first)
                pool.tensor_copy(AQH[b][:], DS[:, bass.ds(c + 4, 1), :])
                pool.drain()
                pool.tensor_tensor(AQL[b][:], DS[:, bass.ds(c + 4, 1), :], AQH[b][:], ALU.subtract).then_inc(staged, 1)

            groups(pool, 4, queries)
            for c in range(BCH):
                add_square("ln", c, c % 2)
            for c in range(BCH):
                pool.wait_ge(branch_hi, c + 1)
                pool.tensor_tensor(QL[:, 4 + c, :], CV[:, c, :], QH[:, 4 + c, :], ALU.subtract).then_inc(branch_lo, 1)

            def residual(name, norm, i, last=False):
                for s in range(2):
                    if not last or s == 0:
                        remainder(START[name] + 2 * i + s + 1, 1 - s)
                    add_square(norm, 2 * i + s, s)

            residual("out", "cross", 0)
            with pool.Fori(1, 4) as i:
                residual("out", "cross", i)
            with pool.Fori(0, 4) as i:
                for s in range(2):
                    remainder(unit_at("qc", i, s) + 1, 1 - s)
            pool.wait_ge(row_in, 48)
            pool.tensor_copy(S5ROW[:, 2, :].rearrange("j (g p) -> j g p", g=2),
                             DTROW[:, :, None].to_broadcast([JP, 2, 64])).then_inc(row_out, 1)
            def heads_low(c, b, first, last):
                pool.wait_ge(q_hi, 2 * c + 1)
                pool.tensor_tensor(CQL[b][:], QT[:, bass.ds(2 * c, 2), :], CQH[b][:], ALU.subtract)
                pool.wait_ge(q_hi, 2 * c + 2)
                pool.tensor_tensor(CKL[b][:], KM[:, bass.ds(2 * c, 2), :], CKH[b][:], ALU.subtract).then_inc(staged, 1)
                pool.wait_ge(v_t, c + 1)
                pool.tensor_copy(CVS[:], VM[:, bass.ds(2 * c, 2), :]).then_inc(cvs_in, 1)

            groups(pool, 4, heads_low)
            def mul(out, a, b):
                pool.tensor_tensor(out, a, b, ALU.mult)

            def wide(x):
                return x[:, :, None].to_broadcast([P, JP, 16])

            LBR, LBI = PW[:, 0, 1, :], PW[:, 1, 1, :]
            t = [SW[:, k, :] for k in range(10)]
            pool.wait_ge(sin_cos, 1)
            mul(LBR, t[2], t[6])
            mul(LBI, t[2], t[4])
            pool.tensor_copy(UT[:, 0, :], t[6])
            pool.tensor_copy(UT[:, 1, :], t[4])
            pool.memset(PW[:, 0, 0, :], 1.0)
            pool.memset(PW[:, 1, 0, :], 0.0)
            for k in range(1, 8):
                pool.drain()
                mul(t[0], PW[:, 0, k, :], LBR)
                mul(t[1], PW[:, 1, k, :], LBI)
                mul(t[2], PW[:, 0, k, :], LBI)
                mul(t[3], PW[:, 1, k, :], LBR)
                pool.drain()
                pool.tensor_tensor(PW[:, 0, k + 1, :], t[0], t[1], ALU.subtract)
                pool.tensor_tensor(PW[:, 1, k + 1, :], t[2], t[3], ALU.add)
            for k in range(3):
                pool.drain()
                mul(t[0], UT[:, 0, :], UT[:, 0, :])
                mul(t[1], UT[:, 1, :], UT[:, 1, :])
                mul(t[2], UT[:, 0, :], UT[:, 1, :])
                pool.drain()
                pool.tensor_tensor(UT[:, 0, :], t[0], t[1], ALU.subtract)
                pool.tensor_scalar(UT[:, 1, :], t[2], 2.0, None, ALU.mult)
            pool.wait_ge(den_inv, 1)
            pool.tensor_scalar(t[4], LBR, -1.0, None, ALU.add)
            pool.drain()
            mul(t[0], t[4], LAM[:, 0, :])
            mul(t[1], LBI, LAM[:, 1, :])
            mul(t[2], LBI, LAM[:, 0, :])
            mul(t[3], t[4], LAM[:, 1, :])
            pool.drain()
            pool.tensor_tensor(t[5], t[0], t[1], ALU.add)
            pool.tensor_tensor(t[6], t[2], t[3], ALU.subtract)
            pool.drain()
            mul(t[5], t[5], t[8])
            mul(t[6], t[6], t[8])
            pool.drain()
            pool.wait_ge(b_in, 32)
            for ri, (x, y, op) in enumerate(((t[5], t[6], ALU.subtract), (t[6], t[5], ALU.add))):
                mul(BT[:, 0], wide(x), BRAW[:, 0])
                mul(BT[:, 1], wide(y), BRAW[:, 1])
                pool.drain()
                pool.tensor_tensor(BB[:, ri], BT[:, 0], BT[:, 1], op)
                pool.drain()
            pool.nop().then_inc(params, 1)
            residual("oc", "ffn", 0)
            with pool.Fori(1, 4) as i:
                residual("oc", "ffn", i)
            pool.memset(G[:, 0:2], 0.0).then_inc(g_zero, 1)
            for g, n in FFN_GROUPS:
                with pool.Fori(0, n) as i:
                    for s in range(2):
                        remainder(unit_at(f"ffn{g}", i, s) + 1, 1 - s)
                if g != FFN_GROUPS[-1][0]:
                    with pool.Fori(0, 4) as i:
                        for s in range(2):
                            remainder(unit_at(f"down{g}", i, s) + 1, 1 - s)
            residual(f"down{g}", "final", 0)
            with pool.Fori(1, 4) as i:
                residual(f"down{g}", "final", i)
            for x in (W1T, KB, CL, SPV, RHOT):
                pool.memset(x[:], 0.0)
            pool.drain()
            pool.nop().then_inc(zeroed, 1)
            for c in range(KC):
                add_square("s5", c, c % 2)

            def generate(c, b):
                four = bass.ds(4 * c, 4)
                if not isinstance(c, int) or c:
                    pool.wait_ge(k_mm, c)
                for n, x, ri_ops in ((8, BB, (ALU.subtract, ALU.add)), (9, CC, (ALU.add, ALU.subtract))):
                    if n == 9 and (not isinstance(c, int) or c >= 2):
                        pool.wait_ge(y_mm, c - 1)
                    for ri in range(2):
                        for j in range(2):
                            a = PW[:, j if ri == 0 else 1 - j, 0:n, four][:, :, :, None].to_broadcast([P, n, 4, 16])
                            d = x[:, j, four, :][:, None, :, :].to_broadcast([P, n, 4, 16])
                            pool.tensor_tensor(GT[:, j, 0:n], a, d, ALU.mult)
                        pool.drain()
                        for g in range(2):
                            rows = slice(64 * g, 64 * g + 64)
                            o = W1T[rows, :, ri, :, g, :] if n == 8 else CL[rows, b, ri, :, :, g, :]
                            j = n == 9 and ri == 1
                            pool.tensor_tensor(o, GT[rows, int(j), 0:n], GT[rows, 1 - j, 0:n], ri_ops[ri])
                        pool.drain()
                pool.nop().then_inc(gen_ready, 1)

            generate(0, 0)
            generate(1, 1)
            with pool.Fori(1, 4) as i:
                for b in range(2):
                    generate(2 * i + b, b)

            def glu(i):
                for b in range(2):
                    c = 2 * i + b
                    for s in range(2):
                        remainder(unit_at("s5glu", c, s) + 1, 1 - s)
                    add_square("mlp0", c, b)

            glu(0)
            with pool.Fori(1, 4) as i:
                glu(i)
            pool.memset(FWR[:], 0.0)
            pool.memset(BF[:], 0.0)
            pool.memset(VSH[0][:].bitcast(F32), 0.0)
            pool.memset(VSL[0][:].bitcast(F32), 0.0)
            pool.drain().then_inc(fw_zero, 1)

            def mlp(l, norm):
                def remainders(name):
                    with pool.Fori(0, 4) as i:
                        for s in range(2):
                            remainder(unit_at(name, i, s) + 1, 1 - s)

                for g in range(GROUPS):
                    remainders(f"up{l}{g}")
                    if g < GROUPS - 1:
                        remainders(f"dn{l}{g}")
                name = f"dn{l}{GROUPS - 1}"
                residual(name, norm, 0)
                with pool.Fori(1, 3) as i:
                    residual(name, norm, i)
                residual(name, norm, 3, last=l == 1)

            mlp(0, "kv")
            pool.wait_ge(fw_hi, 1)
            pool.tensor_tensor(FWL[:], FWR[:], FWH[:], ALU.subtract).then_inc(fw_lo, 1)
            with pool.Fori(0, 8) as i:
                for s in range(2):
                    remainder(unit_at("kv", i, s) + 1, 1 - s)
            with pool.Fori(0, 4) as i:
                for s in range(2):
                    remainder(unit_at("wq", i, s) + 1, 1 - s)
            def heads(c, b, first, last):
                free("fox", c, first)
                pool.tensor_copy(QSH[b][:], QT[:, bass.ds(c, 1), :])
                pool.tensor_copy(KSH[b][:], KT[:, bass.ds(c, 1), :])
                pool.drain()
                pool.tensor_tensor(QSL[b][:], QT[:, bass.ds(c, 1), :], QSH[b][:], ALU.subtract)
                pool.tensor_tensor(KSL[b][:], KT[:, bass.ds(c, 1), :], KSH[b][:], ALU.subtract)
                for half in range(2):
                    for j, (to, fixed) in enumerate(((LQ, LF), (RK, RF))):
                        head = HOT[:, bass.ds(2 * c + half + NHEAD * j, 1)]
                        pool.tensor_tensor(to[:, 2 * b + half, :], fixed[:], head.to_broadcast([P, T]), ALU.add)
                    pool.drain().then_inc(staged, 1)
                    if half == 0:
                        pool.wait_ge(v_t, 5 + c)
                        pool.tensor_copy(VS[:], VT[:, bass.ds(c, 1), :]).then_inc(cvs_in, 1)

            pool.wait_ge(f_ready, 2)
            pool.memset(VSH[1][:].bitcast(F32), 0.0)
            pool.memset(VSL[1][:].bitcast(F32), 0.0)
            pool.drain().then_inc(pad_zero, 1)
            pool.wait_ge(f_ready, 3)
            groups(pool, 8, heads)
            residual("wo", "mlp1", 0)
            with pool.Fori(1, 4) as i:
                residual("wo", "mlp1", i)
            mlp(1, "last")

        @block.tensor
        def _(pe):
            def unit(u, s, xh, xl, n=T, kc=KC, chunks=None):
                pe.wait_ge(w_hi, u + 1)
                if not isinstance(u, int) or u >= 2:
                    pe.wait_ge(unit_out, u - 1)
                for k in range(kc):
                    if chunks:
                        pe.wait_ge(chunks[0], chunks[1] + k + 1)
                    pe.matmul(ACC[s][:, 0:n], WH[:, s, k, :], xh[:, k, :], start=(k == 0), stop=False)
                    pe.matmul(ACC[s][:, 0:n], WH[:, s, k, :], xl[:, k, :], start=False, stop=False)
                pe.wait_ge(w_lo, u + 1)
                for k in range(kc):
                    mm = pe.matmul(ACC[s][:, 0:n], WL[:, s, k, :], xh[:, k, :], start=False, stop=(k == kc - 1))
                mm.then_inc(unit_done, 1)

            def column_sums(norm):
                pe.wait_ge(sq_used, SQUARES[norm] + dict(NORMS)[norm])
                if NORM[norm]:
                    pe.wait_ge(st_rs, NORM[norm])
                for b in range(TB):
                    mm = pe.matmul(ST[:, b:b + 1], SSQ[:, b * P:(b + 1) * P], ONES[:, 0:1], start=True, stop=True)
                mm.then_inc(st_sum, 1)

            def spread_scales(norm):
                pe.wait_ge(st_diag, NORM[norm] + 1)
                pe.matmul(ST[:], ONES, DIAG[:], start=True, stop=True).then_inc(st_bc, 1)

            pe.wait_ge(cst_in, 16)
            pe.wait_ge(x_in, 16)
            for c in range(KC):
                if c >= 2:
                    pe.wait_ge(x_ready, c - 1)
                for b in range(TB):
                    mm = pe.transpose(TR[c % 2][:, b * P:(b + 1) * P], XROW[:, b, c * P:(c + 1) * P], IDENT)
                mm.then_inc(x_t, 1)
                if c == 0:
                    pe.wait_ge(vec_in, 16 * len(VECTORS))
                    for t in range(3):
                        mm = pe.transpose(ST[:, t * P:t * P + ROWS[t]], VROW[0:ROWS[t], t, :], IDENT[0:ROWS[t], 0:ROWS[t]])
                    mm.then_inc(vec_t, 1)
            pe.wait_ge(mem_scaled, MB)
            for c in range(KC):
                if c >= 2:
                    pe.wait_ge(mem_lo, c - 1)
                for b in range(MB):
                    mm = pe.transpose(S[c % 2][:, b * P:(b + 1) * P], MROW[:, b, c * P:(c + 1) * P], IDENT)
                mm.then_inc(mem_t, 1)
            unit(0, 0, PH, PL, chunks=(op_lo, NOPERAND["mix"]))
            column_sums("mix")
            unit(1, 1, PH, PL)
            spread_scales("mix")
            with pe.Fori(1, 4) as i:
                for s in range(2):
                    unit(unit_at("glu", i, s), s, PH, PL)
            with pe.Fori(0, 4) as i:
                for s in range(2):
                    unit(unit_at("in", i, s), s, PH, PL)
            for j in range(8):
                rows = P if j not in (0, 3) else 64
                pe.wait_ge(unit_out, START["in"] + j + 1)
                if j >= 2:
                    pe.wait_ge(rot_used, j - 1)
                pe.matmul(TR[j % 2][0:rows, :], ROTM[0:rows, 0:rows], DS[0:rows, j, :], start=True, stop=True)\
                  .then_inc(rot_done, 1)
            for b in range(TB):
                mm = pe.transpose(O[:, b * 4:b * 4 + 4], DS[64:68, 0, b * P:(b + 1) * P], IDENT[64:68, 64:68])
            mm.then_inc(wi_t, 1)
            for b in range(TB):
                mm = pe.transpose(S[0][:, b * 64:(b + 1) * 64], DS[64:P, 3, b * P:(b + 1) * P], IDENT[64:P, 64:P])
            mm.then_inc(v_t, 1)
            pe.wait_ge(kd_in[0], 16)
            pe.wait_ge(rope_done, 3)
            pe.wait_ge(v_lo, 2)
            for n in range(3 * IDXH):
                qb, h = n // IDXH + 1, n % IDXH
                rows = slice(h % 2 * 64, h % 2 * 64 + 64)
                if n >= 2:
                    pe.wait_ge(index_relu, n - 1)
                pe.matmul(S[n % 2][:, 0:(qb + 1) * P], DS[rows, 1 + h // 2, qb * P:(qb + 1) * P],
                          KD[rows, 0, 0:(qb + 1) * P], start=True, stop=True).then_inc(index_mm, 1)
            pe.wait_ge(mem_lo, KC)
            for name in ("memk", "memv"):
                with pe.Fori(0, 4) as i:
                    for s in range(2):
                        unit(unit_at(name, i, s), s, MH, ML, n=NMEM)

            def three(out, ah, al, bh, bl, first, last):
                pe.matmul(out, ah, bh, start=first, stop=False)
                pe.matmul(out, ah, bl, start=False, stop=False)
                return pe.matmul(out, al, bh, start=False, stop=last)

            def scores(kind, c, b, t):
                n = TILES[kind] + SIZE[kind] * c + t
                half, qb, nk = t // TB, t % TB, keys(kind, t)
                s = SB[t % SLOTS[kind]]
                q = slice(qb * P, (qb + 1) * P)
                if kind == "fox" and t % TB == 0:
                    pe.wait_ge(staged, STAGED[kind] + 2 * c + t // TB + 1)
                elif t == 0:
                    pe.wait_ge(staged, STAGED[kind] + c + 1)
                pe.wait_ge(e_done, n + 5 - SLOTS[kind])
                if kind == "cross":
                    for k in range(2):
                        mm = three(s[:, 0:nk], CQH[b][:, k, q], CQL[b][:, k, q], CKH[b][:, k, :], CKL[b][:, k, :], k == 0, k == 1)
                else:
                    rows = slice(half * 64, half * 64 + 64)
                    qh, ql, kh, kl = ((AQH[b], AQL[b], KSH[0], KSL[0]) if kind == "sparse" else
                                      (QSH[b], QSL[b], KSH[b], KSL[b]))
                    three(s[:, 0:nk], qh[rows, q], ql[rows, q], kh[rows, 0:nk], kl[rows, 0:nk], True, False)
                    if kind == "sparse":
                        mm = pe.matmul(s[:, 0:nk], IDR[:], SEL[:, qb, 0:nk], start=False, stop=True)
                    else:
                        pe.matmul(s[:, 0:nk], LQ[:, 2 * b + half, q], RK[:, 2 * b + half, 0:nk], start=False, stop=False)
                        mm = pe.matmul(s[:, q], IDR[:], TRIR[:], start=False, stop=True)
                mm.then_inc(s_ready, 1)

            def turn(kind, c, t):
                n = TILES[kind] + SIZE[kind] * c + t
                pe.wait_ge(e_scaled, n + 1)
                pe.wait_ge(pt_lo, n + 1)
                for k in range(keys(kind, t) // P):
                    mm = pe.transpose(TT[t % 2][:, k * P:(k + 1) * P], ET4[t % SLOTS[kind]][:, k * P:(k + 1) * P], IDENT)
                mm.then_inc(t_ready, 1)

            def values(kind, c, b, half):
                pe.wait_ge(pt_lo, TILES[kind] + SIZE[kind] * c + 4 * half + 6)
                if kind == "cross":
                    pe.wait_ge(v_lo, c + 3)
                    pe.wait_ge(o_lo, PAIRS["cross"] + 2 * c)
                    for m in range(2):
                        for k in range(MB):
                            mm = three((O, ST)[m][:], CVH[b][:, k, m * P:(m + 1) * P], CVL[b][:, k, m * P:(m + 1) * P],
                                       PTH[:, k, :], PTL[:, k, :], k == 0, k == MB - 1)
                        mm.then_inc(pv_done, 1)
                    return
                if kind == "fox" and half == 0:
                    pe.wait_ge(v_lo, 6 + 2 * c + 2)
                if half == 0 and not (kind == "sparse" and isinstance(c, int) and c == 0):
                    pe.wait_ge(o_lo, PAIRS[kind] + c)
                vh, vl = (VSH[0], VSL[0]) if kind == "sparse" else (VSH[b], VSL[b])
                for k in range(TB):
                    mm = three(O[:, k * P:T], vh[:, k, half, :], vl[:, k, half, :], PTH[:, k, k * P:T],
                               PTL[:, k, k * P:T], half == 0 and k == 0, half == 1 and k == TB - 1)
                mm.then_inc(pv_done, 1)

            def turn_values(kind, c, first):
                if kind == "cross":
                    pe.wait_ge(cvs_in, c + 1)
                    if not first:
                        pe.wait_ge(v_lo, c + 2)
                    for m in range(2):
                        for k in range(MB):
                            mm = pe.transpose(SB[3][:, k * 2 * P + m * P:k * 2 * P + (m + 1) * P],
                                              CVS[:, m, k * P:(k + 1) * P], IDENT)
                    mm.then_inc(v_t, 1)
                if kind == "fox":
                    pe.wait_ge(cvs_in, c + 5)
                    if not first:
                        pe.wait_ge(v_lo, 6 + 2 * c)
                    for k in range(TB):
                        mm = pe.transpose(ST[:, k * P:(k + 1) * P], VS[:, k * P:(k + 1) * P], IDENT)
                    mm.then_inc(v_t, 1)

            def attend(kind, n_groups):
                size, ahead = SIZE[kind], AHEAD[kind]
                halves = size // TB

                def group(c, b, first, last):
                    for t in range(size):
                        if t + ahead < size:
                            scores(kind, c, b, t + ahead)
                        elif not last:
                            scores(kind, c + 1, 1 - b, t + ahead - size)
                        turn(kind, c, t)
                        if t == 0 and not first:
                            values(kind, c - 1, 1 - b, halves - 1)
                        if t == TB:
                            values(kind, c, b, 0)
                        if t == size // 2 and not last:
                            turn_values(kind, c + 1, False)

                turn_values(kind, 0, True)
                for t in range(ahead):
                    scores(kind, 0, 0, t)
                groups(pe, n_groups, group)
                values(kind, n_groups - 1, 1, halves - 1)

            pe.sem_inc(t_ready, 4)
            pe.sem_inc(pv_done, 1)
            pe.wait_ge(sel_ready, TB)
            pe.wait_ge(k_lo, 1)
            attend("sparse", 4)
            pe.wait_ge(conv_done, BCH)
            for c in range(BCH):
                mm = pe.matmul(S[0][:], ONES, CV[:, c, :], start=(c == 0), stop=(c == BCH - 1))
            mm.then_inc(mean_sum, 1)
            column_sums("ln")
            spread_scales("ln")
            pe.wait_ge(o_lo, PAIRS["sparse"] + 4)
            pe.wait_ge(branch_lo, BCH)
            with pe.Fori(0, 4) as i:
                for s in range(2):
                    unit(unit_at("out", i, s), s, QH, QL)

            def normed(name, norm, xh, xl, pairs):
                unit(START[name], 0, xh, xl, chunks=(op_lo, NOPERAND[norm]))
                column_sums(norm)
                unit(START[name] + 1, 1, xh, xl)
                spread_scales(norm)
                with pe.Fori(1, pairs) as i:
                    for s in range(2):
                        unit(unit_at(name, i, s), s, xh, xl)

            normed("qc", "cross", PH, PL, 4)
            pe.wait_ge(row_out, 1)
            for j in range(3):
                mm = pe.transpose(O[:, j * JP:(j + 1) * JP], S5ROW[:, j, :], IDENT[0:JP, 0:JP])
            mm.then_inc(row_t, 1)
            pe.wait_ge(c_in, 64)
            for j in range(4):
                ri, first = j // 2, j % 2 * 4
                if j >= 2:
                    pe.wait_ge(c_out, j - 1)
                for k in range(4):
                    mm = pe.transpose(TR[j % 2][:, k * P:(k + 1) * P],
                                      CROW[:, ri, first + k, :, :].rearrange("p a b -> p (a b)"), IDENT)
                mm.then_inc(c_t, 1)
            pe.wait_ge(c_out, 4)
            attend("cross", 4)
            pe.wait_ge(o_lo, PAIRS["cross"] + 8)
            with pe.Fori(0, 4) as i:
                for s in range(2):
                    unit(unit_at("oc", i, s), s, QH, QL)
            for g, n in FFN_GROUPS:
                if g == 0:
                    normed("ffn0", "ffn", PH, PL, n)
                else:
                    with pe.Fori(0, n) as i:
                        for s in range(2):
                            unit(unit_at(f"ffn{g}", i, s), s, PH, PL)
                pe.wait_ge(hid_lo, g + n)
                with pe.Fori(0, 4) as i:
                    for s in range(2):
                        unit(unit_at(f"down{g}", i, s), s, QH, QL, kc=n)
            column_sums("final")
            spread_scales("final")
            column_sums("s5")
            spread_scales("s5")

            def turn_b(c):
                pe.wait_ge(gen_ready, c + 1)
                for k in range(4):
                    if k >= 2:
                        pe.wait_ge(w1_in, 4 * c + k - 1)
                    for m in range(4):
                        mm = pe.transpose(ACC[k % 2][:, m * P:(m + 1) * P],
                                          W1T[:, 2 * k + m // 2, m % 2].rearrange("p a b c -> p (a b c)"), IDENT)
                    mm.then_inc(w1_t, 1)

            def kernel_lags(c, b):
                if not isinstance(c, int) or c:
                    pe.wait_ge(kb_in, c)
                for j in range(4):
                    for ri in range(2):
                        mm = pe.matmul(O[32 * j:32 * j + 32, 0:256].rearrange("p (k c) -> p k c", k=8),
                                       W1T[:, 0, ri, j].rearrange("p a b -> p (a b)"),
                                       CL[:, b, ri, 0:8, j].rearrange("p k a b -> p k (a b)"),
                                       start=(ri == 0), stop=(ri == 1))
                mm.then_inc(k_mm, 1)

            UCv = UC[:].rearrange("p b (m i) -> p b m i", i=8)

            def mixer(c, b, more):
                pe.wait_ge(w1_in, 4 * c + 4)
                pe.wait_ge(uc_ready, c + 1)
                if not isinstance(c, int) or c:
                    pe.wait_ge(l_used, c)
                for i in range(8):
                    for ri in range(2):
                        for j in range(4):
                            rows = slice(32 * j, 32 * j + 32)
                            mm = pe.matmul(FOUR[:, j, ri * 64:ri * 64 + 64], W1[rows, 2 * (7 - i) + ri, :],
                                           UCv[rows, b, :, i], start=(i == 0 and ri == 0), stop=(i == 7),
                                           skip_group_check=True)
                mm.then_inc(l_mm, 1)
                if more:
                    turn_b(c + 1)
                    kernel_lags(c + 1, 1 - b)
                pe.wait_ge(kb_in, c + 1)
                if not isinstance(c, int) or c:
                    pe.wait_ge(y_out, c)
                Y = ST[:].rearrange("p (m i) -> p m i", i=8)
                for lag in range(8):
                    pe.matmul(Y[:, :, lag:8], KB[:, b, lag, :], UCv[:, b, :, 0:8 - lag],
                              start=(lag == 0), stop=False, skip_group_check=True)
                pe.wait_ge(sp_ready, c + 1)
                for i in range(8):
                    for ri in range(2):
                        for j in range(4):
                            mm = pe.matmul(Y[32 * j:32 * j + 32, :, i],
                                           CL[:, b, ri, i + 1, j].rearrange("p a b -> p (a b)"), SPV[:, ri, j, :],
                                           start=False, stop=(ri == 1 and i == 7), skip_group_check=True)
                mm.then_inc(y_mm, 1)

            turn_b(0)
            kernel_lags(0, 0)
            mixer(0, 0, True)
            mixer(1, 1, True)
            with pe.Fori(1, 3) as i:
                for b in range(2):
                    mixer(2 * i + b, b, True)
            mixer(6, 0, True)
            mixer(7, 1, False)

            def units(name, first, last, xh, xl):
                with pe.Fori(first, last) as i:
                    for s in range(2):
                        unit(unit_at(name, i, s), s, xh, xl)

            def first_pair(name, xh, xl, chunks):
                unit(START[name], 0, xh, xl, chunks=chunks)
                unit(START[name] + 1, 1, xh, xl)

            def mlp(l, x, h):
                for g in range(GROUPS):
                    if g == 0:
                        normed(f"up{l}{g}", f"mlp{l}", *x, 4)
                    else:
                        units(f"up{l}{g}", 0, 4, *x)
                    first_pair(f"dn{l}{g}", *h, (hid_lo, HIDDEN[f"mlp{l}"] + g * KC))
                    units(f"dn{l}{g}", 1, 4, *h)

            first_pair("s5glu", QH, QL, (hid_lo, HIDDEN["s5"]))
            units("s5glu", 1, 8, QH, QL)
            mlp(0, (PH, PL), (QH, QL))
            normed("kv", "kv", PH, PL, 8)
            pe.wait_ge(fw_lo, 1)
            for k in range(KC):
                mm = three(O[:], FWH[:, k, :], FWL[:, k, :], PH[:, k, :], PL[:, k, :], k == 0, k == KC - 1)
            mm.then_inc(f_mm, 1)
            pe.wait_ge(op_lo, NOPERAND["wq"] + KC)
            units("wq", 0, 4, QH, QL)
            pe.wait_ge(f_ready, 3)
            attend("fox", 8)
            pe.wait_ge(o_lo, PAIRS["fox"] + 8)
            units("wo", 0, 4, PH, PL)
            mlp(1, (QH, QL), (PH, PL))
            column_sums("last")
            spread_scales("last")
            for c in range(KC):
                pe.wait_ge(y_normed, c + 1)
                if c >= 2:
                    pe.wait_ge((y_even, y_odd)[c % 2], c // 2)
                for b in range(TB):
                    mm = pe.transpose(TR[c % 2][:, b * P:(b + 1) * P], X[:, c, b * P:(b + 1) * P], IDENT)
                mm.then_inc(y_t, 1)

        @block.vector
        def _(dve):
            def low(norm, c, gain, hi, lo):
                dve.wait_ge(op_hi, NOPERAND[norm] + c + 1)
                dve.scalar_tensor_tensor(lo, X[:, bass.ds(c, 1), :], column(gain, c), hi, ALU.mult, ALU.subtract)\
                   .then_inc(op_lo, 1)

            def newton(r, v, y):
                dve.tensor_tensor(y, r, r, ALU.mult)
                dve.drain()
                dve.scalar_tensor_tensor(y, y, -0.5, v, ALU.mult, ALU.mult)
                dve.drain()
                dve.scalar_tensor_tensor(r, y, 1.5, r, ALU.add, ALU.mult)
                dve.drain()

            def scales(norm, n):
                k = NORM[norm] + 1
                dve.wait_ge(st_sum, k)
                dve.tensor_scalar(V4[:], ST[:, 0:TB], 1.0 / n, EPS, ALU.mult, ALU.add).then_inc(st_var, 1)
                dve.wait_ge(st_std, k)
                dve.reciprocal(R4[:], SD4[:])
                dve.drain()
                newton(R4[:], V4[:], SD4[:])
                dve.tensor_tensor(DIAG[:].rearrange("p (b t) -> p b t", b=TB),
                                  IDENT[:, None, :].to_broadcast([P, TB, P]),
                                  R4[:, :, None].to_broadcast([P, TB, P]), ALU.mult).then_inc(st_diag, 1)
                dve.wait_ge(st_bc, k)
                dve.tensor_copy(RS[:], ST[:]).then_inc(st_rs, 1)
                dve.drain()

            dve.wait_ge(mem_sq, MB)
            dve.tensor_scalar(V4[:, 0:MB], V4[:, 0:MB], 1.0 / D, EPS, ALU.mult, ALU.add).then_inc(mem_var, 1)
            for c in range(KC):
                dve.wait_ge(x_t, c + 1)
                dve.tensor_copy(X[:, c, :], TR[c % 2][:]).then_inc(x_ready, 1)
                if c == 0:
                    dve.wait_ge(vec_t, 1)
                    for t in range(3):
                        last = dve.tensor_copy(VEC[:, t, 0:ROWS[t]], ST[:, t * P:t * P + ROWS[t]])
                    last.then_inc(vec_c, 1)
                    dve.drain()
                    dve.wait_ge(mem_std, 1)
                    dve.reciprocal(R4[:, 0:MB], SD4[:, 0:MB])
                    dve.drain()
                    newton(R4[:, 0:MB], V4[:, 0:MB], SD4[:, 0:MB])
                    for b in range(MB):
                        dve.tensor_scalar(MROW[:, b, :], MROW[:, b, :], R4[:, b:b + 1], None, ALU.mult)\
                           .then_inc(mem_scaled, 1)
                if c >= 1:
                    low("mix", c - 1, "norm_mix_g", PH[:, c - 1, :], PL[:, c - 1, :])
            low("mix", KC - 1, "norm_mix_g", PH[:, KC - 1, :], PL[:, KC - 1, :])
            for c in range(KC):
                dve.wait_ge(mem_hi, c + 1)
                dve.scalar_tensor_tensor(ML[:, c, :], S[c % 2][:, 0:NMEM], column("norm_mem_g", c), MH[:, c, :],
                                         ALU.mult, ALU.subtract).then_inc(mem_lo, 1)
            dve.wait_ge(pos_in, 16)
            dve.tensor_copy(COS[:], POSI[:])
            dve.drain()
            dve.tensor_scalar(SIN[:], COS[:], FREQ, None, ALU.mult)
            dve.drain()
            dve.tensor_scalar(COS[:], SIN[:], 1.0 / (2.0 * np.pi), MAGIC, ALU.mult, ALU.add)
            dve.drain()
            dve.tensor_scalar(COS[:], COS[:], -MAGIC, None, ALU.add)
            for part in TWO_PI:
                dve.drain()
                dve.scalar_tensor_tensor(SIN[:], COS[:], -part, SIN[:], ALU.mult, ALU.add)
            dve.drain()
            dve.tensor_scalar(SIN[:], SIN[:], PI_BELOW, -PI_BELOW, ALU.min, ALU.max)
            dve.drain()
            dve.scalar_tensor_tensor(COS[:], SIN[:], -1.0, SIN[:], ALU.mult, ALU.max)
            dve.drain()
            dve.tensor_scalar(COS[:], COS[:], -1.0, float(np.pi / 2), ALU.mult, ALU.add).then_inc(ang, 1)
            scales("mix", D)
            dve.wait_ge(u_zero, 1)

            def glu(i):
                u = unit_at("glu", i, 0)
                if not isinstance(i, int):
                    dve.wait_ge(gate_sig, i)
                dve.wait_ge(unit_done, u + 1)
                dve.tensor_tensor(TA, ACC[0][:], RS[:], ALU.mult).then_inc(unit_out, 1)
                dve.wait_ge(unit_done, u + 2)
                dve.tensor_tensor(TB_, ACC[1][:], RS[:], ALU.mult).then_inc(unit_out, 1)
                dve.drain().then_inc(gate_raw, 1)
                dve.wait_ge(gate_sig, i + 1)
                dve.tensor_tensor(U[:, bass.ds(i, 1), PAD:PAD + T], TA, TB_, ALU.mult)
                dve.drain()

            glu(0)
            with dve.Fori(1, 4) as i:
                glu(i)
            SCALE = [1.0, 0.125, 0.125, 1.0, 0.125, 0.125, 0.125, 0.125]
            for j in range(8):
                u = START["in"] + j
                dve.wait_ge(unit_done, u + 1)
                dve.scalar_tensor_tensor(DS[:, j, :], ACC[j % 2][:], SCALE[j], RS[:], ALU.mult, ALU.mult)\
                   .then_inc(unit_out, 1)
            for j in range(8):
                rows = P if j not in (0, 3) else 64
                to = KD[0:64, j // 3, :] if j in (0, 3) else DS[:, j, :]
                dve.wait_ge(rot_done, j + 1)
                dve.tensor_tensor(E[0:rows, j % 2, :], TR[j % 2][0:rows, :], SIN[0:rows, :], ALU.mult)\
                   .then_inc(rot_used, 1)
                dve.drain()
                dve.wait_ge(rope_cos, j + 1)
                dve.tensor_tensor(to, DS[0:rows, j, :], E[0:rows, j % 2, :], ALU.add).then_inc(rope_done, 1)
            dve.wait_ge(wi_t, 1)
            dve.tensor_scalar(WI[:].rearrange("p b h -> p (b h)"), O[:, 0:TB * 4], 0.5, None, ALU.mult)
            for half in range(2):
                cols = slice(half * 64, half * 64 + 64)
                dve.wait_ge(v_hi, 2)
                dve.tensor_tensor(VSL[0][:, :, half, cols], S[0][:, 0:TB * 64].rearrange("p (b f) -> p b f", b=TB),
                                  VSH[0][:, :, half, cols], ALU.subtract).then_inc(v_lo, 1)
            for n in range(3 * IDXH):
                qb, h = n // IDXH + 1, n % IDXH
                nk = (qb + 1) * P
                dve.drain()
                dve.wait_ge(index_relu, n + 1)
                if h == 0:
                    ins = dve.tensor_scalar(SC[:, qb - 1, 0:nk], E[:, n % 2, 0:nk], WI[:, qb, h:h + 1], None, ALU.mult)
                else:
                    ins = dve.scalar_tensor_tensor(SC[:, qb - 1, 0:nk], E[:, n % 2, 0:nk], WI[:, qb, h:h + 1],
                                                   SC[:, qb - 1, 0:nk], ALU.mult, ALU.add)
                ins.then_inc(index_sum, 1)
            dve.tensor_copy(SEL[:, 0, 0:P], TRI).then_inc(sel_ready, 1)
            dve.wait_ge(index_masked, 3)
            with dve.Fori(0, TOPK // 8) as r:
                for b in range(3):
                    dve.max(M8[:, b, :], SC[:, b, 0:(b + 2) * P])
                dve.drain()
                for b in range(3):
                    dve.match_replace(SC[:, b, 0:(b + 2) * P], M8[:, b, :], SC[:, b, 0:(b + 2) * P], TAKEN)
                dve.drain()
            for b in range(3):
                dve.tensor_scalar(SEL[:, b + 1, 0:(b + 2) * P], SC[:, b, 0:(b + 2) * P], TAKEN, -BIG,
                                  ALU.not_equal, ALU.mult).then_inc(sel_ready, 1)
            with dve.Fori(0, BCH) as c:
                def tap(k):
                    return U[:, bass.ds(c, 1), k:k + T]

                dve.tensor_scalar(CV[:, bass.ds(c, 1), :], tap(0), column("conv_b_w", c), column("conv_b_b", c),
                                  ALU.mult, ALU.add)
                for k in range(1, CONVW):
                    dve.drain()
                    ins = dve.scalar_tensor_tensor(CV[:, bass.ds(c, 1), :], tap(k), column("conv_b_w", BCH * k + c),
                                                   CV[:, bass.ds(c, 1), :], ALU.mult, ALU.add)
                ins.then_inc(conv_done, 1)

            def negative_max(kind, n, t):
                nk, j = keys(kind, t % SIZE[kind]), t % SLOTS[kind]
                dve.wait_ge(s_ready, n + 1)
                dve.wait_ge(e_done, n + 5 - SLOTS[kind])
                dve.tensor_reduce(NMX[:, j, :], SB[j][:, 0:nk], AX, ALU.max, negate=True).then_inc(mx_ready, 1)

            def divide(kind, n, t):
                nk, j = keys(kind, t), t % SLOTS[kind]
                dve.wait_ge(e_done, n + 5)
                dve.reciprocal(REC[:, j, :], SUM[:, j, :])
                dve.drain()
                dve.tensor_scalar(ET4[j][:, 0:nk], ET4[j][:, 0:nk], REC[:, j, :], None, ALU.mult).then_inc(e_scaled, 1)

            def turned_low(n, t, qb, kb):
                to = (slice(None), slice(0, kb), slice(qb * P, (qb + 1) * P))
                dve.wait_ge(pt_hi, n + 1)
                dve.tensor_tensor(PTL[to], TT[t % 2][:, 0:kb * P].rearrange("p (k q) -> p k q", q=P), PTH[to],
                                  ALU.subtract).then_inc(pt_lo, 1)

            def low_out(bank_, lo, hi, k):
                dve.wait_ge(o_hi, k + 1)
                dve.tensor_tensor(lo, bank_[:], hi, ALU.subtract).then_inc(o_lo, 1)

            def out_low(kind, c):
                hi, lo = OUT[kind]
                for m in range(1 + (kind == "cross")):
                    k = 2 * c + m if kind == "cross" else c
                    low_out((O, ST)[m], lo[:, bass.ds(k, 1), :], hi[:, bass.ds(k, 1), :], PAIRS[kind] + k)

            def values_low(kind, c, b):
                if kind == "cross":
                    dve.wait_ge(v_hi, c + 4)
                    dve.tensor_tensor(CVL[b][:], SB[3].rearrange("p (b f) -> p b f", b=MB), CVH[b][:], ALU.subtract)\
                       .then_inc(v_lo, 1)
                if kind == "fox":
                    dve.wait_ge(v_hi, 9 + 2 * c)
                    for half in range(2):
                        cols = slice(half * 64, half * 64 + 64)
                        dve.tensor_tensor(VSL[b][:, :, half, cols],
                                          ST[:].rearrange("p (b h f) -> p b h f", b=TB, h=2)[:, :, half, :],
                                          VSH[b][:, :, half, cols], ALU.subtract).then_inc(v_lo, 1)

            def attend(kind, n_groups):
                size, ahead = SIZE[kind], 2

                def low_tile(c, t):
                    turned_low(TILES[kind] + size * c + t, t, t % TB, keys(kind, t) // P)

                def group(c, b, first, last):
                    n = TILES[kind] + size * c
                    for t in range(size):
                        divide(kind, n + t, t)
                        if t == 0 and not first:
                            low_tile(c - 1, size - 1)
                        if not last or t + ahead < size:
                            negative_max(kind, n + t + ahead, t + ahead)
                        if t:
                            low_tile(c, t - 1)
                        if t == 1 and not first:
                            out_low(kind, c - 1)
                        if t == size - 1 and not last:
                            values_low(kind, c + 1, 1 - b)

                values_low(kind, 0, 0)
                for t in range(ahead):
                    negative_max(kind, TILES[kind] + t, t)
                groups(dve, n_groups, group)
                low_tile(n_groups - 1, size - 1)
                out_low(kind, n_groups - 1)

            dve.sem_inc(pt_lo, 2)
            attend("sparse", 4)
            dve.wait_ge(mean_sum, 1)
            for c in range(BCH):
                dve.scalar_tensor_tensor(CV[:, c, :], S[0][:], -1.0 / (BCH * P), CV[:, c, :], ALU.mult, ALU.add)\
                   .then_inc(centred, 1)
            scales("ln", BCH * P)
            for c in range(BCH):
                dve.tensor_tensor(CV[:, c, :], CV[:, c, :], RS[:], ALU.mult).then_inc(ln_scaled, 1)

            def residual(name, norm, gain, hi, lo, i):
                for s in range(2):
                    c = 2 * i + s
                    x = X[:, bass.ds(c, 1), :]
                    dve.wait_ge(unit_done, START[name] + c + 1)
                    dve.tensor_tensor(x, x, ACC[s][:], ALU.add).then_inc(unit_out, 1)
                    low(norm, c, gain, hi[:, bass.ds(c, 1), :], lo[:, bass.ds(c, 1), :])

            with dve.Fori(0, 4) as i:
                residual("out", "cross", "norm_cross_g", PH, PL, i)
            scales("cross", D)

            def scaled(name, i, to, k=1.0):
                for s in range(2):
                    u = unit_at(name, i, s)
                    dve.wait_ge(unit_done, u + 1)
                    dve.scalar_tensor_tensor(to[:, bass.ds(2 * i + s, 1), :], ACC[s][:], k, RS[:], ALU.mult, ALU.mult)\
                       .then_inc(unit_out, 1)

            with dve.Fori(0, 4) as i:
                scaled("qc", i, QT, 1.0 / 16)
            dve.wait_ge(row_t, 1)
            dve.tensor_copy(LAM[:].rearrange("p a b -> p (a b)"), O[:, 0:3 * JP])
            for j in range(4):
                dve.wait_ge(c_t, j + 1)
                for g in range(2):
                    rows = slice(64 * g, 64 * g + 64)
                    src = TR[j % 2][rows, :].rearrange("p (j g c) -> p j g c", g=2, c=16)[:, :, g, :]
                    ins = dve.tensor_scalar(CC[rows, j // 2, j % 2 * 16:j % 2 * 16 + 16, :], src, (1.0, -1.0)[j // 2],
                                            None, ALU.mult)
                ins.then_inc(c_out, 1)
            w = [SW[:, k, :] for k in range(10)]

            def exponential(out, x, n, r, q):
                dve.drain()
                dve.tensor_scalar(n, x, float(1.0 / np.log(2.0)), MAGIC, ALU.mult, ALU.add)
                dve.drain()
                dve.tensor_scalar(n, n, -MAGIC, -126.0, ALU.add, ALU.max)
                dve.drain()
                dve.scalar_tensor_tensor(r, n, -LN2[0], x, ALU.mult, ALU.add)
                dve.drain()
                dve.scalar_tensor_tensor(r, n, -LN2[1], r, ALU.mult, ALU.add)
                dve.tensor_scalar(POW2[:], n, 127.0, float(2 ** 23), ALU.add, ALU.mult)
                dve.drain()
                dve.tensor_scalar(q, r, 1.0 / 5040, None, ALU.mult)
                for k in (720.0, 120.0, 24.0, 6.0, 2.0, 1.0):
                    dve.drain()
                    dve.scalar_tensor_tensor(q, q, 1.0 / k, r, ALU.add, ALU.mult)
                dve.drain()
                dve.scalar_tensor_tensor(out, q, 1.0, POW2[:].bitcast(F32), ALU.add, ALU.mult)
                dve.drain()

            exponential(LAM[:, 2, :], LAM[:, 2, :], w[3], w[4], w[5])
            dve.tensor_tensor(w[0], LAM[:, 0, :], LAM[:, 2, :], ALU.mult)
            dve.tensor_tensor(w[1], LAM[:, 1, :], LAM[:, 2, :], ALU.mult)
            dve.tensor_tensor(w[7], LAM[:, 0, :], LAM[:, 0, :], ALU.mult)
            dve.tensor_tensor(w[8], LAM[:, 1, :], LAM[:, 1, :], ALU.mult)
            dve.drain()
            dve.tensor_tensor(w[7], w[7], w[8], ALU.add)
            dve.tensor_scalar(w[3], w[1], 1.0 / (2.0 * np.pi), MAGIC, ALU.mult, ALU.add)
            dve.drain()
            dve.reciprocal(w[8], w[7]).then_inc(den_inv, 1)
            dve.tensor_scalar(w[3], w[3], -MAGIC, None, ALU.add)
            for part in TWO_PI:
                dve.drain()
                dve.scalar_tensor_tensor(w[1], w[3], -part, w[1], ALU.mult, ALU.add)
            dve.drain()
            dve.tensor_scalar(w[1], w[1], PI_BELOW, -PI_BELOW, ALU.min, ALU.max)
            dve.drain()
            dve.scalar_tensor_tensor(w[9], w[1], -1.0, w[1], ALU.mult, ALU.max)
            exponential(w[2], w[0], w[3], w[4], w[5])
            dve.tensor_scalar(w[9], w[9], -1.0, float(np.pi / 2), ALU.mult, ALU.add)
            dve.tensor_tensor(w[3], w[2], w[2], ALU.mult)
            dve.drain()
            dve.tensor_tensor(w[5], w[3], w[3], ALU.mult)
            dve.drain()
            dve.tensor_tensor(RHO8[:], w[5], w[5], ALU.mult)
            dve.drain().then_inc(angle_ready, 1)
            attend("cross", 4)
            with dve.Fori(0, 4) as i:
                residual("oc", "ffn", "norm_ffn_g", PH, PL, i)
            def turn_table(k):
                if k == 0:
                    dve.wait_ge(params, 1)
                    dve.memset(ET[:, 0, :, 0], 1.0)
                    dve.memset(ET[:, 1, :, 0], 0.0)
                    dve.drain()
                n = 2 ** k
                TMP = at(f"TMP{k}", [P, 2, JP, n], F32, 155648 + 6208)
                for ri in range(2):
                    for j in range(2):
                        u = UT[:, j if ri == 0 else 1 - j, :, None].to_broadcast([P, JP, n])
                        dve.tensor_tensor(TMP[:, j], ET[:, j, :, 0:n], u, ALU.mult)
                    dve.drain()
                    dve.tensor_tensor(ET[:, ri, :, n:2 * n], TMP[:, 0], TMP[:, 1], (ALU.subtract, ALU.add)[ri])
                    dve.drain()
                if k < 5:
                    t = [SW[:, j, :] for j in range(3)]
                    dve.tensor_tensor(t[0], UT[:, 0, :], UT[:, 0, :], ALU.mult)
                    dve.tensor_tensor(t[1], UT[:, 1, :], UT[:, 1, :], ALU.mult)
                    dve.tensor_tensor(t[2], UT[:, 0, :], UT[:, 1, :], ALU.mult)
                    dve.drain()
                    dve.tensor_tensor(UT[:, 0, :], t[0], t[1], ALU.subtract)
                    dve.tensor_scalar(UT[:, 1, :], t[2], 2.0, None, ALU.mult)
                    dve.drain()

            def hidden_low(k, x, value, hi=QH, lo=QL):
                dve.wait_ge(hid_hi, value)
                dve.tensor_tensor(lo[:, bass.ds(k, 1), :], x, hi[:, bass.ds(k, 1), :], ALU.subtract).then_inc(hid_lo, 1)

            scales("ffn", D)
            dve.wait_ge(g_zero, 1)
            for g, n in FFN_GROUPS:
                turn_table(g // 4)
                with dve.Fori(0, n) as i:
                    u = unit_at(f"ffn{g}", i, 0)
                    f = i + g
                    dve.wait_ge(unit_done, u + 1)
                    dve.tensor_tensor(G[:, 2:2 + T], ACC[0][:], RS[:], ALU.mult).then_inc(unit_out, 1)
                    dve.drain()
                    dve.tensor_scalar(H1[:], G[:, 0:T], column("ffn_conv_w", f), column("ffn_conv_b", f), ALU.mult, ALU.add)
                    dve.drain()
                    dve.scalar_tensor_tensor(H1[:], G[:, 1:1 + T], column("ffn_conv_w", f + FC), H1[:], ALU.mult, ALU.add)
                    dve.drain()
                    dve.scalar_tensor_tensor(H1[:], G[:, 2:2 + T], column("ffn_conv_w", f + 2 * FC), H1[:], ALU.mult, ALU.add)\
                       .then_inc(gate_conv, 1)
                    dve.wait_ge(unit_done, u + 2)
                    dve.tensor_tensor(H2[:], ACC[1][:], RS[:], ALU.mult).then_inc(unit_out, 1)
                    dve.drain()
                    dve.wait_ge(gate_act, f + 1)
                    dve.tensor_tensor(H2[:], H2[:], H1[:], ALU.mult).then_inc(hid_ready, 1)
                    hidden_low(i, H2[:], f + 1)
                turn_table(g // 4 + 1)
                with dve.Fori(0, 4) as i:
                    for s in range(2):
                        x = X[:, bass.ds(2 * i + s, 1), :]
                        dve.wait_ge(unit_done, unit_at(f"down{g}", i, s) + 1)
                        dve.tensor_tensor(x, x, ACC[s][:], ALU.add).then_inc(unit_out, 1)
                dve.drain()
            scales("final", D)
            for c in range(KC):
                dve.scalar_tensor_tensor(X[:, c, :], X[:, c, :], column("norm_final_g", c), RS[:], ALU.mult, ALU.mult)\
                   .then_inc(normed_x, 1)
            scales("s5", D)
            for c in range(KC):
                dve.scalar_tensor_tensor(U5[:, c, :], X[:, c, :], column("mix_norm_2", c), RS[:], ALU.mult, ALU.mult)\
                   .then_inc(u5_ready, 1)

            def kernel_in(c, b):
                dve.wait_ge(k_mm, c + 1)
                if not isinstance(c, int) or c >= 2:
                    dve.wait_ge(y_mm, c - 1)
                for j in range(4):
                    rows = slice(32 * j, 32 * j + 32)
                    ins = dve.tensor_copy(KB[rows, b, :, 32 * j:32 * j + 32],
                                          O[rows, 0:256].rearrange("p (k c) -> p k c", k=8))
                ins.then_inc(kb_in, 1)

            def mixer(c, b, more):
                four = bass.ds(4 * c, 4)
                cos, sin = ET[:, 0, four, :], ET[:, 1, four, :]
                dve.wait_ge(l_mm, c + 1)
                for ri, (x, y, op) in enumerate(((0, 1, ALU.add), (1, 0, ALU.subtract))):
                    dve.tensor_tensor(RT[:, 0], FOUR[:, :, x * 64:x * 64 + 64], cos, ALU.mult)
                    ins = dve.tensor_tensor(RT[:, 1], FOUR[:, :, y * 64:y * 64 + 64], sin, ALU.mult)
                    if ri:
                        ins.then_inc(l_used, 1)
                    dve.drain()
                    dve.tensor_tensor(VR[:, ri], RT[:, 0], RT[:, 1], op)
                    dve.drain()
                dve.tensor_copy(RHOT[:, :, 1:64], RHO8[:, four, None].to_broadcast([P, 4, 63]))
                dve.drain()
                for ri in range(2):
                    dve.tensor_tensor_scan(WR[:, ri].rearrange("p a b -> p (a b)"), RHOT[:].rearrange("p a b -> p (a b)"),
                                           VR[:, ri].rearrange("p a b -> p (a b)"), 0.0, ALU.mult, ALU.add)
                dve.drain()
                if not isinstance(c, int) or c:
                    dve.wait_ge(y_mm, c)
                cos, sin = ET[:, 0, four, 0:63], ET[:, 1, four, 0:63]
                for ri, (x, y, op) in enumerate(((0, 1, ALU.subtract), (1, 0, ALU.add))):
                    dve.tensor_tensor(RT[:, 0, :, 0:63], WR[:, x, :, 0:63], cos, ALU.mult)
                    dve.tensor_tensor(RT[:, 1, :, 0:63], WR[:, y, :, 0:63], sin, ALU.mult)
                    dve.drain()
                    dve.tensor_tensor(SPV[:, ri, :, 1:64], RT[:, 0, :, 0:63], RT[:, 1, :, 0:63], op)
                    dve.drain()
                dve.nop().then_inc(sp_ready, 1)
                if more:
                    kernel_in(c + 1, 1 - b)
                dve.wait_ge(y_mm, c + 1)
                if not isinstance(c, int) or c >= 2:
                    dve.wait_ge(hid_hi, HIDDEN["s5"] + c - 1)
                dve.scalar_tensor_tensor(YC[:, b, :], U5[:, bass.ds(c, 1), :], column("ssm_d_2", c), ST[:],
                                         ALU.mult, ALU.add).then_inc(y_out, 1)
                hidden_low(c, YC[:, b, :], HIDDEN["s5"] + c + 1)

            dve.wait_ge(zeroed, 1)
            kernel_in(0, 0)
            mixer(0, 0, True)
            mixer(1, 1, True)
            with dve.Fori(1, 3) as i:
                for b in range(2):
                    mixer(2 * i + b, b, True)
            mixer(6, 0, True)
            mixer(7, 1, False)
            dve.drain()
            with dve.Fori(0, 8) as c:
                u = unit_at("s5glu", c, 0)
                x = X[:, bass.ds(c, 1), :]
                dve.wait_ge(unit_done, u + 1)
                dve.tensor_copy(TA, ACC[0][:]).then_inc(unit_out, 1)
                dve.drain()
                dve.wait_ge(gate_sig, 4 + c + 1)
                dve.tensor_tensor(TA, TA, TB_, ALU.mult).then_inc(unit_out, 1)
                dve.drain()
                dve.tensor_tensor(x, x, TA, ALU.add).then_inc(glu_out, 1)
                low("mlp0", c, "mlp_norm_2", PH[:, bass.ds(c, 1), :], PL[:, bass.ds(c, 1), :])

            def mlp(l, hi, lo):
                norm = f"mlp{l}"
                for g in range(GROUPS):
                    with dve.Fori(0, 4) as i:
                        for s in range(2):
                            k = 2 * i + s
                            h = (H1, H2)[s]
                            dve.wait_ge(unit_done, unit_at(f"up{l}{g}", i, s) + 1)
                            dve.tensor_tensor(h[:], ACC[s][:], RS[:], ALU.mult).then_inc(unit_out, 1)
                            dve.drain()
                            dve.scalar_tensor_tensor(h[:], h[:], 0.0, h[:], ALU.max, ALU.mult).then_inc(hid_ready, 1)
                            dve.drain()
                            hidden_low(k, h[:], HIDDEN[norm] + g * KC + k + 1, hi, lo)
                    if g < GROUPS - 1:
                        with dve.Fori(0, 4) as i:
                            for s in range(2):
                                x = X[:, bass.ds(2 * i + s, 1), :]
                                dve.wait_ge(unit_done, unit_at(f"dn{l}{g}", i, s) + 1)
                                dve.tensor_tensor(x, x, ACC[s][:], ALU.add).then_inc(unit_out, 1)
                        dve.drain()

            scales("mlp0", D)
            mlp(0, QH, QL)
            with dve.Fori(0, 4) as i:
                residual(f"dn0{GROUPS - 1}", "kv", "kv_norm_2", PH, PL, i)
            scales("kv", D)
            for j, to in enumerate((KT, VT)):
                with dve.Fori(0, 4) as i:
                    for s in range(2):
                        c = 2 * i + s
                        dve.wait_ge(unit_done, START["kv"] + j * 8 + c + 1)
                        dve.tensor_tensor(to[:, bass.ds(c, 1), :], ACC[s][:], RS[:], ALU.mult).then_inc(unit_out, 1)
                    c = i + 4 * j
                    low("wq", c, ("mix_norm_2", KC), QH[:, bass.ds(c, 1), :], QL[:, bass.ds(c, 1), :])
            dve.wait_ge(f_mm, 1)
            dve.tensor_tensor(FZ[:], O[:], RS[:], ALU.mult)
            dve.drain()
            dve.tensor_scalar(FZ[:], FZ[:], BF[:], None, ALU.add)
            dve.drain()
            dve.scalar_tensor_tensor(F[:], FZ[:], -1.0, FZ[:], ALU.mult, ALU.max).then_inc(f_abs, 1)
            dve.wait_ge(f_ln, 1)
            dve.scalar_tensor_tensor(FZ[:], FZ[:], 0.0, F[:], ALU.min, ALU.subtract)
            dve.drain()
            dve.tensor_tensor_scan(F[:], ONES[:, 0:1].to_broadcast([P, T]), FZ[:], 0.0, ALU.mult, ALU.add)\
               .then_inc(f_sum, 1)
            with dve.Fori(0, 4) as i:
                scaled("wq", i, QT, 0.125)
            dve.wait_ge(f_ready, 1)
            dve.tensor_tensor(FL[:], F[:], FH[:], ALU.subtract)
            dve.drain()
            dve.memset(LF[0:64, :].bitcast(F32), 0.0)
            dve.memset(RF[64:P, :].bitcast(F32), 0.0)
            dve.tensor_scalar(RF[32:64, :], FL[32:64, :].bitcast(F32), -1.0, None, ALU.mult)
            dve.tensor_copy(LF[96:P, :], FL[96:P, :].bitcast(F32))
            dve.wait_ge(f_ready, 2)
            dve.drain().then_inc(f_ready, 1)
            attend("fox", 8)
            with dve.Fori(0, 4) as i:
                residual("wo", "mlp1", ("mlp_norm_2", KC), QH, QL, i)
            scales("mlp1", D)
            mlp(1, PH, PL)
            with dve.Fori(0, 4) as i:
                for s in range(2):
                    x = X[:, bass.ds(2 * i + s, 1), :]
                    dve.wait_ge(unit_done, unit_at(f"dn1{GROUPS - 1}", i, s) + 1)
                    dve.tensor_tensor(x, x, ACC[s][:], ALU.add).then_inc(unit_out, 1)
            scales("last", D)
            for c in range(KC):
                dve.scalar_tensor_tensor(X[:, c, :], X[:, c, :], column("final_norm_2", c), RS[:], ALU.mult, ALU.mult)\
                   .then_inc(y_normed, 1)
            for c in range(1, KC, 2):
                dve.wait_ge(y_t, c + 1)
                dve.tensor_copy(YROW[:, :, c * P:(c + 1) * P], TR[1][:].rearrange("p (b f) -> p b f", f=P))\
                   .then_inc(y_odd, 1)


_INS = ["x", "mem", "positions", "norm_mix_g", "w_in", "w_out", "conv_b_w", "conv_b_b", "ln_b_g", "ln_b_b",
        "norm_cross_g", "norm_mem_g", "w_q_cross", "w_k_cross", "w_v_cross", "w_o_cross", "norm_ffn_g", "w_gate",
        "w_up", "ffn_conv_w", "ffn_conv_b", "w_down", "norm_final_g", "mix_norm_2", "mlp_norm_2", "mlp_w1_2",
        "mlp_w2_2", "ssm_log_dt_2", "ssm_a_re_2", "ssm_a_im_2", "ssm_b_re_2", "ssm_b_im_2", "ssm_c_re_2",
        "ssm_c_im_2", "ssm_d_2", "ssm_w_glu_2", "kv_norm_2", "w_kvf_2", "b_f_2", "attn_wq_2", "attn_wo_2",
        "final_norm_2", "constants"]
_OUTS = [((1, 512, 1024), "float32")]


def kernel(**inputs):
    import concourse.bacc as bacc
    from concourse.bass_utils import run_bass_kernel_spmd

    nc = bacc.Bacc("TRN2", target_bir_lowering=False, num_devices=1)
    inputs = dict(inputs, constants=constants())
    arrays, args = {}, {}
    for name in _INS:
        a = np.ascontiguousarray(inputs[name])
        arrays[f"in_{name}_dram"] = a
        args[name] = nc.dram_tensor(f"in_{name}_dram", a.shape, mybir.dt.from_np(a.dtype), kind="ExternalInput").ap()
    shape, dtype = _OUTS[0]
    out = nc.dram_tensor("out_0_dram", shape, mybir.dt.from_np(np.dtype(dtype)), kind="ExternalOutput").ap()
    build_program(nc, args, out)
    r = run_bass_kernel_spmd(nc, [arrays], core_ids=[0])
    return r.results[0]["out_0_dram"]
```

```python
from contextlib import ExitStack

import numpy as np
import concourse.bass as bass
from concourse import mybir

F32 = mybir.dt.float32
F32R = mybir.dt.float32r
I32 = mybir.dt.int32
ALU = mybir.AluOpType
ACT = mybir.ActivationFunctionType
AX = mybir.AxisListType.X

P = 128
T = 512
TB = T // P
D = 1024
KC = D // P
NMEM = 256
MB = NMEM // P
IDXH = 4
TOPK = 128
CONVW = 31
PAD = CONVW - 1
BCH = 4
TAPS = 8
DFF = 2816
FC = DFF // P
EPS = 1e-6
THETA = 500000.0
ROT = 16
NHEAD = 16
NCST = 4 * P + 1 + 2 * NHEAD
BIG = float(2.0 ** 100)
FAR = -1.0e30
TAKEN = -3.0e38
LAG = 4
NM = T // LAG
MAGIC = 12582912.0
PI_BELOW = 3.1415925
TWO_PI = (6.28125, 0.0019350051879882812, 6.283185307179586 - 6.28125 - 0.0019350051879882812)
LN2 = (0.693359375, float(np.log(2.0)) - 0.693359375)

FFN_GROUPS = [(g, min(8, FC - g)) for g in range(0, FC, 8)]
ORDER = [("glu", 8), ("in", 8), ("memk", 8), ("memv", 8), ("out", 8), ("qc", 8), ("oc", 8)]
for _g, _n in FFN_GROUPS:
    ORDER += [(f"ffn{_g}", 2 * _n), (f"down{_g}", 8)]
GROUPS = 4 * D // P // 8
_MLP = [[(f"{_n}{_l}{_g}", 8) for _g in range(GROUPS) for _n in ("up", "dn")] for _l in range(2)]
ORDER += [("s5glu", 16)] + _MLP[0] + [("kv", 16), ("wq", 8), ("wo", 8)] + _MLP[1]
START = {}
NUNITS = 0
for _name, _c in ORDER:
    START[_name] = NUNITS
    NUNITS += _c
COUNT = dict(ORDER)

VECTORS = [("norm_mix_g", 8, 0), ("norm_cross_g", 8, 0), ("norm_mem_g", 8, 0), ("norm_ffn_g", 8, 0),
           ("norm_final_g", 8, 0), ("mix_norm_2", 16, 0), ("mlp_norm_2", 16, 0), ("kv_norm_2", 8, 0),
           ("final_norm_2", 8, 0), ("ssm_d_2", 8, 0), ("conv_b_b", 4, 0), ("ln_b_g", 4, 0), ("ln_b_b", 4, 0),
           ("conv_b_w", 124, 1), ("ffn_conv_w", 66, 2), ("ffn_conv_b", 22, 2)]
ROWS = [0, 0, 0]
COLUMN = {}
for _name, _c, _t in VECTORS:
    COLUMN[_name] = (_t, ROWS[_t])
    ROWS[_t] += _c

NORMS = [("mix", 8), ("ln", 4), ("cross", 8), ("ffn", 8), ("final", 8), ("mlp0", 8), ("kv", 8), ("mlp1", 8),
         ("last", 8)]
NORM = {name: n for n, (name, _) in enumerate(NORMS)}
SQUARES = {name: sum(c for _, c in NORMS[:n]) for n, (name, _) in enumerate(NORMS)}
NOPERAND = {"mix": 0, "cross": 8, "ffn": 16, "mlp0": 24, "kv": 32, "wq": 40, "mlp1": 48}
HIDDEN = {"ffn": 0, "s5": FC, "mlp0": FC + KC, "mlp1": FC + KC + 8 * GROUPS}
TILES = {"sparse": 0, "cross": 32, "fox": 48}
PAIRS = {"sparse": 0, "cross": 4, "fox": 12}
STAGED = {"sparse": 0, "cross": 4, "fox": 8}
HALVES = {"sparse": 1, "cross": 9, "fox": 17}


def constants():
    c = np.zeros((P, NCST), np.float32)
    c[:, 0:P] = np.eye(P)
    for m in range(P):
        if m % 64 < ROT // 2:
            c[m + ROT // 2, P + m] = -1.0
        elif m % 64 < ROT:
            c[m - ROT // 2, P + m] = 1.0
    q, k = np.meshgrid(np.arange(P), np.arange(P), indexing="ij")
    c[:, 2 * P:3 * P] = np.where(k > q, -BIG, 0.0)
    c[:, 3 * P:4 * P] = 1.0
    f = (np.float32(THETA) ** (-np.arange(0, ROT, 2, dtype=np.float32) / np.float32(ROT))).astype(np.float32)
    for m in range(P):
        if m % 64 < ROT:
            c[m, 4 * P] = f[m % (ROT // 2)]
    for h in range(NHEAD):
        c[h:64:32, 4 * P + 1 + h] = 1.0
        c[64 + h::32, 4 * P + 1 + NHEAD + h] = 1.0
    return c


def build_program(nc, A, out):
    ctx = ExitStack()
    with ctx:
        first = (nc.sbuf_base + 127) // 128 * 128

        def at(name, shape, dt, offset):
            return nc.alloc_sbuf_tensor_at(name, shape, dt, offset=first + offset)

        def bank(name):
            return ctx.enter_context(nc.psum_tensor(name, [P, 512], F32))

        def sem(name):
            return ctx.enter_context(nc.semaphore(name))

        X = at("X", [P, KC, T], F32, 0)
        PH = at("PH", [P, KC, T], F32R, 16384)
        PL = at("PL", [P, KC, T], F32R, 32768)
        QH = at("QH", [P, KC, T], F32R, 49152)
        QL = at("QL", [P, KC, T], F32R, 65536)
        RAW = at("RAW", [P, 2, KC, P], F32, 81920)
        WH = at("WH", [P, 2, KC, P], F32R, 90112)
        WL = at("WL", [P, 2, KC, P], F32R, 98304)
        QT = at("QT", [P, KC, T], F32, 106496)
        KT = at("KT", [P, KC, T], F32, 122880)
        VT = at("VT", [P, KC, T], F32, 139264)
        PTH = at("PTH", [P, TB, T], F32R, 155648)
        PTL = at("PTL", [P, TB, T], F32R, 163840)
        E = at("E", [P, 2, T], F32, 172032)
        QSH = [at("QSH", [P, T], F32R, 176128), at("QSH1", [P, T], F32R, 65536)]
        QSL = [at("QSL", [P, T], F32R, 178176), at("QSL1", [P, T], F32R, 67584)]
        KSH = [at("KSH", [P, T], F32R, 180224), at("KSH1", [P, T], F32R, 69632)]
        KSL = [at("KSL", [P, T], F32R, 182272), at("KSL1", [P, T], F32R, 71680)]
        VS = at("VS", [P, T], F32, 184320)
        VSH = [at("VSH", [P, TB, 2, P], F32R, 186368), at("VSH1", [P, TB, 2, P], F32R, 73728)]
        VSL = [at("VSL", [P, TB, 2, P], F32R, 190464), at("VSL1", [P, TB, 2, P], F32R, 77824)]
        AQH = [QSH[0], at("AQH1", [P, T], F32R, 43008)]
        AQL = [QSL[0], at("AQL1", [P, T], F32R, 45056)]
        CST = at("CST", [P, NCST], F32, 194560)
        IDR = at("IDR", [P, P], F32R, 196768)
        TRIR = at("TRIR", [P, P], F32R, 197280)
        RS = at("RS", [P, T], F32, 197792)
        SSQ = at("SSQ", [P, T], F32, 199840)
        SQ = at("SQ", [P, 2, T], F32, 201888)
        DIAG = at("DIAG", [P, T], F32, 205984)
        VEC = at("VEC", [P, 3, P], F32, 208032)
        V4 = at("V4", [P, 4], F32, 209568)
        SD4 = at("SD4", [P, 4], F32, 209600)
        R4 = at("R4", [P, 4], F32, 209632)
        WI = at("WI", [P, TB, 4], F32, 209664)
        M8 = at("M8", [P, 3, 8], F32, 209728)
        NMX = at("NMX", [P, 4, 1], F32, 209824)
        SUM = at("SUM", [P, 4, 1], F32, 209856)
        REC = at("REC", [P, 4, 1], F32, 209888)
        XROW = at("XROW", [P, TB, D], F32, 106496)
        MROW = at("MROW", [P, MB, D], F32, 122880)
        VROW = at("VROW", [P, 3, P], F32, 155648)
        POSI = at("POSI", [P, T], I32, 163840)
        MSQ = at("MSQ", [P, D], F32, 157184)
        MV = at("MV", [P, MB], F32, 211200)
        MD = at("MD", [P, MB], F32, 211232)
        MR = at("MR", [P, MB], F32, 211264)
        DS = at("DS", [P, KC, T], F32, 106496)
        KM = at("KM", [P, KC, NMEM], F32, 122880)
        VM = at("VM", [P, KC, NMEM], F32, 131072)
        U = at("U", [P, BCH, PAD + T], F32, 139264)
        COS = at("COS", [P, T], F32, 147968)
        SIN = at("SIN", [P, T], F32, 150016)
        SC = at("SC", [P, 3, T], F32, 16384)
        SEL = at("SEL", [P, TB, T], F32R, 22528)
        KD = at("KD", [P, 2, T], F32, 30720)
        CV = [at(f"CV{c}", [P, T], F32, (184320, 152576, 34816, 36864)[c]) for c in range(BCH)]
        UH = at("UH", [P, 2, PAD + T], F32R, 155648)
        UL = at("UL", [P, 2, PAD + T], F32R, 160000)
        DGH = [at(f"DGH{b}", [P, TAPS, P], F32R, (57344, 73728)[b]) for b in range(2)]
        DGL = [at(f"DGL{b}", [P, TAPS, P], F32R, (61440, 77824)[b]) for b in range(2)]
        WCH = at("WCH", [P, BCH * CONVW], F32R, 210176)
        WCL = at("WCL", [P, BCH * CONVW], F32R, 210688)
        WC = VEC[:, 1, 0:BCH * CONVW]
        G = at("G", [P, 2 + T], F32, 155648)
        H1 = at("H1", [P, T], F32, 157760)
        H2 = at("H2", [P, T], F32, 159808)
        JP = 32
        BB = at("BB", [P, 2, JP, 16], F32, 139264)
        CC = at("CC", [P, 2, JP, 16], F32, 143360)
        PW = at("PW", [P, 2, LAG + 1, JP], F32, 147456)
        UT = at("UT", [P, 2, JP], F32, 149760)
        RHO = at("RHO", [P, JP], F32, 150016)
        LAM = at("LAM", [P, 3, JP], F32, 150144)
        SW = at("SW", [P, 10, JP], F32, 150528)
        S5ROW = at("S5ROW", [JP, 3, P], F32, 151808)
        POW2 = at("POW2", [P, JP], I32, 153600)
        DTROW = at("DTROW", [JP, 2], F32, 153344)
        ET = at("ET", [P, 2, JP, NM], F32, 106496)
        CROW = at("CROW", [P, 2, KC, 2, 64], F32, 122880)
        BRAW = at("BRAW", [P, 2, JP, 16], F32, 176128)
        BT = at("BT", [P, 2, JP, 16], F32, 180224)
        W1T = [at(f"W1T{b}", [P, LAG, 2, 4, 2, 16], F32, 16384 + 4096 * b) for b in range(2)]
        W1 = at("W1", [P, 2 * LAG, P], F32, 24576)
        KB = at("KB", [P, 2, LAG, P], F32, 28672)
        SPV = at("SPV", [P, 2, 4, NM], F32, 32768)
        VR = at("VR", [P, 2, 4, NM], F32, 36864)
        WR = at("WR", [P, 2, 4, NM], F32, 40960)
        SSQ2 = at("SSQ2", [P, T], F32, 186368)
        SQ2 = at("SQ2", [P, 2, T], F32, 188416)
        DIAG2 = at("DIAG2", [P, T], F32, 192512)
        RS2 = at("RS2", [P, T], F32, 153600)
        G12 = at("G12", [P, KC], F32, 211296)
        V5, SD5, R5 = (at(n, [P, 4], F32, x) for n, x in (("V5", 211328), ("SD5", 211360), ("R5", 211392)))
        GC = at("GC", [P, 2, LAG + 1, 4, 16], F32, 45056)
        CL = at("CL", [P, 2, 2, LAG + 1, 4, 2, 16], F32, 155648)
        GT = at("GT", [P, 2, LAG, 4, 16], F32, 165888)
        RHOT = at("RHOT", [P, 4, NM], F32, 167936)
        RT = at("RT", [P, 2, 4, NM], F32, 169984)
        YC = at("YC", [P, 2, T], F32, 174080)
        UC = at("UC", [P, 2, T], F32, 178176)
        UN = at("UN", [P, 2, T], F32, 182272)
        CQH = [at("CQH", [P, 2, T], F32R, 176128), at("CQH1", [P, 2, T], F32R, 32768)]
        CQL = [at("CQL", [P, 2, T], F32R, 180224), at("CQL1", [P, 2, T], F32R, 36864)]
        CVS = at("CVS", [P, 2, NMEM], F32, 184320)
        CKH = [at("CKH", [P, 2, NMEM], F32R, 186368), at("CKH1", [P, 2, NMEM], F32R, 40960)]
        CKL = [at("CKL", [P, 2, NMEM], F32R, 188416), at("CKL1", [P, 2, NMEM], F32R, 43008)]
        CVH = [at("CVH", [P, MB, 2 * P], F32R, 190464), at("CVH1", [P, MB, 2 * P], F32R, 45056)]
        CVL = [at("CVL", [P, MB, 2 * P], F32R, 192512), at("CVL1", [P, MB, 2 * P], F32R, 47104)]
        MH = QH[:, 0:4, :].rearrange("p a (b n) -> p (a b) n", n=NMEM)
        ML = QL[:, 0:4, :].rearrange("p a (b n) -> p (a b) n", n=NMEM)
        FWR = at("FWR", [P, KC, P], F32, 163840)
        FWH = at("FWH", [P, KC, P], F32R, 167936)
        FWL = at("FWL", [P, KC, P], F32R, 176128)
        FZ = at("FZ", [P, T], F32, 172032)
        F = at("F", [P, T], F32, 174080)
        BF = at("BF", [P, 1], F32, 209920)
        LQ = at("LQ", [P, 4, T], F32R, 49152)
        RK = at("RK", [P, 4, T], F32R, 57344)
        LF = at("LF", [P, T], F32R, 201888)
        RF = at("RF", [P, T], F32R, 203936)
        FH = at("FH", [P, T], F32R, 199840)
        FL = at("FL", [P, T], F32R, 205984)
        YROW = at("YROW", [P, TB, D], F32, 106496)
        HOT = CST[:, 4 * P + 1:NCST]
        IDENT, ROTM, TRI, ONES = (CST[:, i * P:(i + 1) * P] for i in range(4))
        FREQ = CST[:, 4 * P:4 * P + 1]
        E4 = {kind: [E[:, 0, :], E[:, 1, :]] + [at(f"E{j}{kind}", [P, T], F32, x)[:] for j, x in ((2, a), (3, b))]
              for kind, a, b in (("sparse", 38912, 40960), ("cross", 199840, 205984), ("fox", 199840, 205984))}
        TA, TB_ = E[:, 0, :], E[:, 1, :]

        def column(name, i):
            name, first = name if isinstance(name, tuple) else (name, 0)
            t, base = COLUMN[name][0], COLUMN[name][1] + first
            return VEC[:, t, bass.ds(base + i, 1)]

        ACC = [bank("ACC0"), bank("ACC1")]
        ST = bank("ST")
        FOUR = ctx.enter_context(nc.psum_tensor("FOUR", [P, 4, 512], F32))
        S = [FOUR[:, 0, :], FOUR[:, 1, :]]
        TR = [FOUR[:, 2, :], FOUR[:, 3, :]]
        O = bank("O")
        SB = [FOUR[:, j, :] for j in range(4)]
        TT = ACC

        w_landed = [sem("w_landed0"), sem("w_landed1")]
        w_hi = sem("w_hi")
        w_lo = sem("w_lo")
        unit_done = sem("unit_done")
        unit_out = sem("unit_out")
        cst_in = sem("cst_in")
        vec_in = sem("vec_in")
        x_in = [sem(f"x_in{j}") for j in range(4)]
        mem_in = sem("mem_in")
        cst_r = sem("cst_r")
        vec_t = sem("vec_t")
        vec_c = sem("vec_c")
        x_t = sem("x_t")
        x_ready = sem("x_ready")
        op_hi = sem("op_hi")
        op_lo = sem("op_lo")
        sq_ready = sem("sq_ready")
        sq_used = sem("sq_used")
        st_sum, st_var, st_std, st_diag, st_bc, st_rs = (
            sem(n) for n in ("st_sum", "st_var", "st_std", "st_diag", "st_bc", "st_rs"))
        mem_sq, mem_var, mem_std, mem_scaled, mem_t, mem_hi, mem_lo = (
            sem(n) for n in ("mem_sq", "mem_var", "mem_std", "mem_scaled", "mem_t", "mem_hi", "mem_lo"))
        pos_in, ang, tables = sem("pos_in"), sem("ang"), sem("tables")
        u_zero, gate_raw, gate_sig = sem("u_zero"), sem("gate_raw"), sem("gate_sig")
        rot_done, rot_used, rope_cos, rope_done = (
            sem(n) for n in ("rot_done", "rot_used", "rope_cos", "rope_done"))
        kd_in = [sem("kd_in0"), sem("kd_in1")]
        wi_t, v_t, pad_zero, v_hi, v_lo = (sem(n) for n in ("wi_t", "v_t", "pad_zero", "v_hi", "v_lo"))
        index_mm, index_relu, index_sum, index_masked, sel_ready = (
            sem(n) for n in ("index_mm", "index_relu", "index_sum", "index_masked", "sel_ready"))
        u_ready, u_hi, u_lo, wc_hi, diag_ready, diag_used, conv_pe, conv_done, mean_sum, centred, ln_scaled, silu_done, branch_hi, branch_lo = (
            sem(n) for n in ("u_ready", "u_hi", "u_lo", "wc_hi", "diag_ready", "diag_used",
                             "conv_pe", "conv_done", "mean_sum", "centred", "ln_scaled", "silu_done", "branch_hi", "branch_lo"))
        g_zero, gate_conv, gate_act, hid_ready, hid_hi, hid_lo = (
            sem(n) for n in ("g_zero", "gate_conv", "gate_act", "hid_ready", "hid_hi", "hid_lo"))
        row_in, c_in, b_in, row_t, row_out, c_t, c_out = (
            sem(n) for n in ("s5_row_in", "s5_c_in", "s5_b_in", "s5_row_t", "s5_row_out", "s5_c_t", "s5_c_out"))
        angle_ready, sin_cos, den_inv, params = (
            sem(n) for n in ("angle_ready", "sin_cos", "den_inv", "s5_params"))
        zeroed, gen_ready, cl_ready, w1_t, w1_in, k_mm, kb_in, l_mm, l_used, sp_ready, y_mm, y_out, gelu_done = (
            sem(n) for n in ("s5_zeroed", "gen_ready", "cl_ready", "w1_t", "w1_in", "k_mm", "kb_in", "l_mm", "l_used", "sp_ready",
                             "y_mm", "y_out", "gelu_done"))
        un_ready, uc_ready = sem("un_ready"), sem("uc_ready")
        glu_out = sem("glu_out")
        sq2_ready, sq2_used, var2, std2, diag2, bc2 = (sem(n) for n in ("sq2_ready", "sq2_used", "var2", "std2", "diag2", "bc2"))
        fw_zero, fw_in, fw_hi, fw_lo, f_mm, f_abs, f_exp, f_ln, f_sum, f_ready = (
            sem(n) for n in ("fw_zero", "fw_in", "fw_hi", "fw_lo", "f_mm", "f_abs", "f_exp", "f_ln", "f_sum", "f_ready"))
        y_normed, y_t, y_even, y_odd, stored = (sem(n) for n in ("y_normed", "y_t", "y_even", "y_odd", "stored"))
        q_hi = sem("q_hi")
        s_ready = sem("s_ready")
        mx_ready = sem("mx_ready")
        e_done = sem("e_done")
        e_scaled = sem("e_scaled")
        t_ready = sem("t_ready")
        pt_hi = sem("pt_hi")
        pt_lo = sem("pt_lo")
        pv_done = sem("pv_done")
        cvs_in, k_lo = sem("cvs_in"), sem("k_lo")
        staged = sem("staged")
        o_hi, o_lo = sem("o_hi"), sem("o_lo")

        def weights(name):
            return A[name].rearrange("l (c p) n -> (l c) p n", p=P).rearrange("c p n -> p c n")

        w_in, w_out = weights("w_in"), weights("w_out")
        w_k, w_v = weights("w_k_cross"), weights("w_v_cross")
        w_qc, w_oc = weights("w_q_cross"), weights("w_o_cross")
        w_gate, w_up, w_down = weights("w_gate"), weights("w_up"), weights("w_down")
        w_glu, w_q, w_o = weights("ssm_w_glu_2"), weights("attn_wq_2"), weights("attn_wo_2")
        w_kvf = A["w_kvf_2"].rearrange("(c p) n -> p c n", p=P)
        w_up2 = [A["mlp_w1_2"][l].rearrange("(c p) n -> p c n", p=P) for l in range(2)]
        w_down2 = [A["mlp_w2_2"][l].rearrange("(c p) n -> p c n", p=P) for l in range(2)]
        IN_COLS = [896, 640, 768, 512, 0, 128, 256, 384]
        GA, GG = 964, 1476

        def groups(eng, n, group, between=(None, None)):
            group(0, 0, True, False)
            if between[0]:
                between[0]()
            with eng.Fori(0, n // 2 - 1) as i:
                group(2 * i + 1, 1, False, False)
                group(2 * i + 2, 0, False, False)
            if between[1]:
                between[1]()
            group(n - 1, 1, False, True)

        def keys(kind, t):
            return NMEM if kind == "cross" else (t % TB + 1) * P

        SLOTS = {"sparse": 4, "cross": 2, "fox": 4}
        AHEAD = {"sparse": 3, "cross": 2, "fox": 3}
        SIZE = {"sparse": 8, "cross": 4, "fox": 8}
        OUT = {"sparse": (QH, QL), "cross": (QH, QL), "fox": (PH, PL)}

        def unit_at(name, i, s, g=0):
            return START[name] + 2 * i + s

        block = ctx.enter_context(nc.Block())

        @block.sync
        def _(sp):
            def load(u, s, src):
                if not isinstance(u, int) or u >= 2:
                    sp.wait_ge(w_lo, u - 1)
                sp.dma_start(RAW[:, s, 0:src.shape[1], :], src).then_inc(w_landed[s], 16)

            sp.dma_start(CST[:], A["constants"]).then_inc(cst_in, 16)
            for j in range(4):
                cols = slice(j * 2 * P, (j + 1) * 2 * P)
                sp.dma_start(XROW[:, :, cols], A["x"][0].rearrange("(b p) d -> p b d", p=P)[:, :, cols]).then_inc(x_in[j], 16)
            for s in range(2):
                load(s, s, w_in[:, :, (GA, GG)[s]:(GA, GG)[s] + P])
            sp.dma_start(MROW[:], A["mem"][0].rearrange("(b p) d -> p b d", p=P)).then_inc(mem_in, 16)
            with sp.Fori(1, 4) as i:
                for s in range(2):
                    load(unit_at("glu", i, s), s, w_in[:, :, bass.ds(i * P + (GA, GG)[s], P)])
            for j, c in enumerate(IN_COLS):
                load(START["in"] + j, j % 2, w_in[:, :, c:c + P])
            for name, w in (("memk", w_k), ("memv", w_v), ("out", w_out), ("qc", w_qc), ("oc", w_oc)):
                if name == "oc":
                    for s in range(2):
                        load(START[name] + s, s, w[:, :, s * P:(s + 1) * P])
                    sp.wait_ge(staged, STAGED["fox"])
                    sp.wait_ge(cvs_in, 4)
                    sp.wait_ge(pv_done, HALVES["cross"] + 6)
                    for ri, x in enumerate(("ssm_b_re_2", "ssm_b_im_2")):
                        sp.dma_start(BRAW[:, ri], A[x][0].rearrange("(j g) p c -> (g p) j c", g=2)).then_inc(b_in, 16)
                    for ri, x in enumerate(("ssm_c_re_2", "ssm_c_im_2")):
                        rows = A[x][0].rearrange("(k g) c p -> (g c) k p", k=KC)
                        for twice in range(2):
                            sp.dma_start(CROW[:, ri, :, twice, :], rows).then_inc(c_in, 16)
                with sp.Fori(name == "oc", 4) as i:
                    for s in range(2):
                        load(unit_at(name, i, s), s, w[:, :, bass.ds(i * 2 * P + s * P, P)])
                if name == "qc":
                    sp.wait_ge(branch_lo, BCH)
                    for j, x in enumerate(("ssm_a_re_2", "ssm_a_im_2")):
                        sp.dma_start(S5ROW[:, j, :], A[x][0].rearrange("(j g) p -> j (g p)", g=2)).then_inc(row_in, 16)
                    sp.dma_start(DTROW[:], A["ssm_log_dt_2"][0].rearrange("(j g) -> j g", g=2)).then_inc(row_in, 16)
            for g, n in FFN_GROUPS:
                with sp.Fori(0, n) as i:
                    for s, w in enumerate((w_gate, w_up)):
                        load(unit_at(f"ffn{g}", i, s), s, w[:, :, bass.ds(i * P + g * P, P)])
                with sp.Fori(0, 4) as i:
                    for s in range(2):
                        load(unit_at(f"down{g}", i, s), s, w_down[:, g:g + n, bass.ds(i * 2 * P + s * P, P)])
            def loads(name, n, w, rows=slice(0, KC), first=0):
                with sp.Fori(0, n // 2) as i:
                    for s in range(2):
                        load(unit_at(name, i, s), s, w[:, rows, bass.ds(i * 2 * P + (s * P + first), P)])

            def mlp(l):
                for g in range(GROUPS):
                    loads(f"up{l}{g}", 8, w_up2[l], first=g * KC * P)
                    loads(f"dn{l}{g}", 8, w_down2[l], slice(g * KC, (g + 1) * KC))

            with sp.Fori(0, 8) as i:
                for s in range(2):
                    load(unit_at("s5glu", i, s), s, w_glu[:, :, bass.ds(i * P + s * D, P)])
            mlp(0)
            sp.wait_ge(fw_zero, 1)
            for j in range(4):
                sp.dma_start(FWR[:, :, 32 * j:32 * j + NHEAD], w_kvf[:, :, 2 * D:2 * D + NHEAD]).then_inc(fw_in, 16)
                sp.dma_start(BF[32 * j:32 * j + NHEAD, :], A["b_f_2"].rearrange("(h o) -> h o", o=1)).then_inc(fw_in, 16)
            loads("kv", 16, w_kvf)
            loads("wq", 8, w_q)
            loads("wo", 8, w_o)
            mlp(1)
            for c in range(KC):
                sp.wait_ge((y_even, y_odd)[c % 2], c // 2 + 1)
                sp.dma_start(out[0].rearrange("(b p) d -> p b d", p=P)[:, :, c * P:(c + 1) * P],
                             YROW[:, :, c * P:(c + 1) * P]).then_inc(stored, 16)
            sp.wait_ge(stored, 16 * KC)

        @block.scalar
        def _(act):
            def round_weights(u, s):
                act.wait_ge(w_landed[s], (u - s) * 8 + 16)
                if not isinstance(u, int) or u >= 2:
                    act.wait_ge(unit_done, u - 1)
                act.activation(WH[:, s], RAW[:, s], ACT.Copy).then_inc(w_hi, 1)

            def prepare(norm, c, gain, hi, s, ready):
                square_free(norm, c)
                act.wait_ge(*ready)
                act.activation(hi, X[:, bass.ds(c, 1), :], ACT.Copy, scale=column(gain, c)).then_inc(op_hi, 1)
                act.activation(SQ[:, s, :], X[:, bass.ds(c, 1), :], ACT.Square).then_inc(sq_ready, 1)

            def square_free(norm, c):
                if not isinstance(c, int) or SQUARES[norm] + c >= 2:
                    act.wait_ge(sq_used, SQUARES[norm] + c - 1)

            def square(norm, c, x, s):
                square_free(norm, c)
                act.activation(SQ[:, s, :], x[:, bass.ds(c, 1), :], ACT.Square).then_inc(sq_ready, 1)

            def standard_deviation(norm):
                act.wait_ge(st_var, NORM[norm] + 1)
                act.activation(SD4[:], V4[:], ACT.Sqrt).then_inc(st_std, 1)

            act.dma_start(POSI[:], A["positions"].to_broadcast([P, T])).then_inc(pos_in, 16)
            for name, rows, t in VECTORS:
                r = COLUMN[name][1]
                flat = A[name] if len(A[name].shape) == 1 else A[name].rearrange(
                    "a b -> (a b)") if len(A[name].shape) == 2 else A[name].rearrange("a b c -> (a b c)")
                act.dma_start(VROW[r:r + rows, t, :], flat.rearrange("(r p) -> r p", p=P)).then_inc(vec_in, 16)
            act.wait_ge(cst_in, 16)
            act.activation(IDR[:], IDENT, ACT.Copy).then_inc(cst_r, 1)
            act.activation(TRIR[:], TRI, ACT.Copy).then_inc(cst_r, 1)
            round_weights(0, 0)
            act.wait_ge(vec_c, 1)
            act.activation(WCH[:], WC, ACT.Copy).then_inc(wc_hi, 1)
            for c in range(KC):
                prepare("mix", c, "norm_mix_g", PH[:, c, :], c % 2, (x_ready, c + 1))
            def glu(i):
                for s in range(2):
                    round_weights(unit_at("glu", i, s) + 1, 1 - s)
                    if s == 0 and i == 0:
                        standard_deviation("mix")
                act.wait_ge(gate_raw, i + 1)
                act.activation(TB_, TB_, ACT.Sigmoid).then_inc(gate_sig, 1)

            act.wait_ge(mem_in, 16)
            for b in range(MB):
                act.activation(MSQ[:], MROW[:, b, :], ACT.Square, accum_out=MV[:, b:b + 1]).then_inc(mem_sq, 1)
                act.drain()
            def memory(first):
                for c in range(first, first + 2):
                    act.wait_ge(mem_t, c + 1)
                    act.activation(MH[:, c, :], S[c % 2][:, 0:NMEM], ACT.Copy, scale=column("norm_mem_g", c))\
                       .then_inc(mem_hi, 1)

            glu(0)
            act.wait_ge(mem_var, 1)
            act.activation(MD[:], MV[:], ACT.Sqrt).then_inc(mem_std, 1)
            glu(1)
            memory(0)
            glu(2)
            act.wait_ge(ang, 1)
            act.activation(SIN[:], SIN[:], ACT.Sin).then_inc(tables, 1)
            act.activation(COS[:], COS[:], ACT.Sin).then_inc(tables, 1)

            memory(2)
            glu(3)
            memory(4)
            for u in range(START["in"], START["memk"]):
                round_weights(u + 1, (u + 1) % 2)
                if u == START["in"] + 1:
                    memory(6)
                if u == START["in"]:
                    for j in range(2):
                        act.wait_ge(u_ready, 3 + j)
                        act.activation(UH[:, j, :], U[:, 2 + j, :], ACT.Copy).then_inc(u_hi, 1)
            act.wait_ge(rope_done, 1)
            act.dma_start(KD[64:P, 0, :], KD[0:64, 0, :]).then_inc(kd_in[0], 16)
            act.wait_ge(v_t, 1)
            act.wait_ge(pad_zero, 2)
            for half in range(2):
                act.activation(VSH[0][:, :, half, half * 64:half * 64 + 64],
                               S[0][:, 0:TB * 64].rearrange("p (b f) -> p b f", b=TB), ACT.Copy).then_inc(v_hi, 1)
            act.wait_ge(rope_done, 4)
            act.dma_start(KD[64:P, 1, :], KD[0:64, 1, :]).then_inc(kd_in[1], 16)
            act.wait_ge(kd_in[1], 16)
            act.activation(KSH[0][:], KD[:, 1, :], ACT.Copy).then_inc(v_hi, 1)
            act.wait_ge(rope_done, 8)
            for n in range(3 * IDXH):
                nk = (n // IDXH + 2) * P
                act.wait_ge(index_mm, n + 1)
                if n >= 2:
                    act.wait_ge(index_sum, n - 1)
                act.activation(E[:, n % 2, 0:nk], S[n % 2][:, 0:nk], ACT.Relu).then_inc(index_relu, 1)
            for name, to in (("memk", KM), ("memv", VM)):
                with act.Fori(0, 4) as i:
                    for s in range(2):
                        u = unit_at(name, i, s)
                        round_weights(u + 1, 1 - s)
                        act.wait_ge(unit_done, u + 1)
                        act.activation(to[:, bass.ds(2 * i + s, 1), :], ACC[s][:, 0:NMEM], ACT.Copy)\
                           .then_inc(unit_out, 1)

            def exponentials(kind, n, t):
                nk, j = keys(kind, t % SIZE[kind]), t % SLOTS[kind]
                act.wait_ge(mx_ready, n + 1)
                act.wait_ge(t_ready, n + 5 - SLOTS[kind])
                act.activation(E4[kind][j][:, 0:nk], SB[j][:, 0:nk], ACT.Exp, bias=NMX[:, j, :],
                               accum_out=SUM[:, j, :]).then_inc(e_done, 1)

            def turned_high(kind, c, t):
                n, qb, kb = TILES[kind] + SIZE[kind] * c + t, t % TB, keys(kind, t) // P
                act.wait_ge(t_ready, n + 5)
                if qb == 0:
                    act.wait_ge(pv_done, HALVES[kind] + 2 * c + t // TB)
                act.activation(PTH[:, 0:kb, qb * P:(qb + 1) * P],
                               TT[t % 2][:, 0:kb * P].rearrange("p (k q) -> p k q", q=P), ACT.Copy).then_inc(pt_hi, 1)

            def out_high(kind, c):
                for m in range(1 + (kind == "cross")):
                    chunk = bass.ds(2 * c + m if kind == "cross" else c, 1)
                    high_out((O, ST)[m], OUT[kind][0][:, chunk, :],
                             HALVES[kind] + 2 * c + (m + 1 if kind == "cross" else 2))

            def values_high(kind, c, b):
                if kind == "cross":
                    act.wait_ge(v_t, c + 2)
                    act.activation(CVH[b][:], SB[3].rearrange("p (b f) -> p b f", b=MB), ACT.Copy).then_inc(v_hi, 1)
                if kind == "fox":
                    act.wait_ge(v_t, c + 6)
                    for half in range(2):
                        act.activation(VSH[b][:, :, half, half * 64:half * 64 + 64],
                                       ST[:].rearrange("p (b h f) -> p b h f", b=TB, h=2)[:, :, half, :], ACT.Copy)\
                           .then_inc(v_hi, 1)

            def heads_high(c, b):
                act.activation(CQH[b][:], QT[:, bass.ds(2 * c, 2), :], ACT.Copy).then_inc(q_hi, 1)
                act.activation(CKH[b][:], KM[:, bass.ds(2 * c, 2), :], ACT.Copy).then_inc(q_hi, 1)

            def attend(kind, n_groups, between=(None, None)):
                size, ahead = SIZE[kind], 2

                def group(c, b, first, last):
                    n = TILES[kind] + size * c
                    for t in range(size):
                        if not last or t + ahead < size:
                            exponentials(kind, n + t + ahead, t + ahead)
                        turned_high(kind, c, t)
                        if t == 0 and not first:
                            out_high(kind, c - 1)
                        if t == 1 and kind == "cross" and (first or b == 1 and not last):
                            heads_high(c + 2, b)
                        if t == size - 2 and not last:
                            values_high(kind, c + 1, 1 - b)

                values_high(kind, 0, 0)
                for t in range(ahead):
                    exponentials(kind, TILES[kind] + t, t)
                if kind == "cross":
                    heads_high(1, 1)
                groups(act, n_groups, group, between)
                out_high(kind, n_groups - 1)

            def high_out(bank_, to, k):
                act.wait_ge(pv_done, k)
                act.activation(to, bank_[:], ACT.Copy).then_inc(o_hi, 1)

            def hidden(ready, k, to, value, hi=QH):
                act.wait_ge(ready, value)
                act.activation(hi[:, bass.ds(k, 1), :], to, ACT.Copy).then_inc(hid_hi, 1)

            for j in range(2):
                act.wait_ge(diag_used, 4 * j + 4)
                act.activation(CV[2 + j][:], (ST, O)[j][:], ACT.Identity, bias=column("conv_b_b", 2 + j))\
                   .then_inc(conv_pe, 1)
            act.sem_inc(e_done, 4)
            for c in range(BCH):
                act.wait_ge(centred, c + 1)
                square_free("ln", c)
                act.activation(SQ[:, c % 2, :], CV[c][:], ACT.Square).then_inc(sq_ready, 1)
            def silu_branch():
                for c in range(BCH):
                    act.wait_ge(ln_scaled, c + 1)
                    act.activation(CV[c][:], CV[c][:], ACT.Silu, bias=column("ln_b_b", c),
                                   scale=column("ln_b_g", c)).then_inc(silu_done, 1)
                    act.wait_ge(silu_done, c + 1)
                    act.activation(QH[:, 4 + c, :], CV[c][:], ACT.Copy).then_inc(branch_hi, 1)

            attend("sparse", 4, (lambda: standard_deviation("ln"), silu_branch))

            def residual(name, norm, gain, hi, i, g=None):
                for s in range(2):
                    u = START[name] + 2 * i + s
                    c = 2 * i + s
                    round_weights(u + 1, 1 - s)
                    prepare(norm, c, gain, hi[:, bass.ds(c, 1), :], s, (unit_out, u + 1))

            residual("out", "cross", "norm_cross_g", PH, 0)
            with act.Fori(1, 4) as i:
                residual("out", "cross", "norm_cross_g", PH, i)

            def plain(name, i, norm=None):
                for s in range(2):
                    round_weights(unit_at(name, i, s) + 1, 1 - s)
                    if s == 0 and norm:
                        standard_deviation(norm)

            plain("qc", 0, "cross")
            plain("qc", 1)
            act.wait_ge(unit_out, START["qc"] + 2)
            heads_high(0, 0)
            with act.Fori(2, 4) as i:
                plain("qc", i)
            attend("cross", 4)
            residual("oc", "ffn", "norm_ffn_g", PH, 0)
            residual("oc", "ffn", "norm_ffn_g", PH, 1)
            act.wait_ge(angle_ready, 1)
            act.activation(SW[:, 4, :], SW[:, 1, :], ACT.Sin)
            act.activation(SW[:, 6, :], SW[:, 9, :], ACT.Sin).then_inc(sin_cos, 1)
            with act.Fori(2, 4) as i:
                residual("oc", "ffn", "norm_ffn_g", PH, i)
            for g, n in FFN_GROUPS:
                def ffn(i):
                    for s in range(2):
                        round_weights(unit_at(f"ffn{g}", i, s) + 1, 1 - s)
                        if s == 0 and isinstance(i, int):
                            standard_deviation("ffn")
                    act.wait_ge(gate_conv, g + i + 1)
                    act.activation(H1[:], H1[:], ACT.Silu).then_inc(gate_act, 1)
                    hidden(hid_ready, i, H2[:], g + i + 1)

                if g == 0:
                    ffn(0)
                with act.Fori(g == 0, n) as i:
                    ffn(i)
                with act.Fori(0, 4) as i:
                    for s in range(2):
                        u = unit_at(f"down{g}", i, s)
                        round_weights(u + 1, 1 - s)
                        if g == FFN_GROUPS[-1][0]:
                            c = 2 * i + s
                            square_free("final", c)
                            act.wait_ge(sq2_used, c + 1)
                            act.wait_ge(unit_out, u + 1)
                            act.activation(SQ2[:, s, :], X[:, bass.ds(c, 1), :], ACT.Square,
                                           scale=column("norm_final_g", c)).then_inc(sq2_ready, 1)
                            act.activation(SQ[:, s, :], X[:, bass.ds(c, 1), :], ACT.Square).then_inc(sq_ready, 1)
            standard_deviation("final")
            act.wait_ge(var2, 1)
            act.activation(SD5[:], V5[:], ACT.Sqrt).then_inc(std2, 1)

            def mixer_input(c, b):
                act.wait_ge(un_ready, c + 1)
                if not isinstance(c, int) or c >= 2:
                    act.wait_ge(y_mm, c - 1)
                act.activation(UC[:, b, :].rearrange("p (i m) -> p m i", i=LAG),
                               UN[:, b, :].rearrange("p (m i) -> p m i", i=LAG), ACT.Copy)\
                   .then_inc(uc_ready, 1)

            def mixer(c, b, more):
                act.wait_ge(k_mm, c + 1)
                if not isinstance(c, int) or c >= 2:
                    act.wait_ge(y_mm, c - 1)
                for j in range(4):
                    rows = slice(32 * j, 32 * j + 32)
                    act.activation(KB[rows, b, :, 32 * j:32 * j + 32],
                                   O[rows, 0:32 * LAG].rearrange("p (k c) -> p k c", k=LAG), ACT.Copy).then_inc(kb_in, 1)
                if more:
                    for k in range(2):
                        act.wait_ge(w1_t, 2 * c + 2 + k + 1)
                        if k == 0:
                            act.wait_ge(l_mm, c + 1)
                        act.activation(W1[:, 4 * k:4 * k + 4, :], ACC[k % 2][:].rearrange("p (a b) -> p a b", b=P),
                                       ACT.Copy).then_inc(w1_in, 1)
                act.wait_ge(y_out, c + 1)
                act.activation(YC[:, b, :], YC[:, b, :], ACT.Gelu_apprx_tanh).then_inc(gelu_done, 1)
                hidden(gelu_done, c, YC[:, b, :], c + 1)
                if not isinstance(c, int):
                    mixer_input(c + 2, b)

            for c in range(2):
                mixer_input(c, c)
            for k in range(2):
                act.wait_ge(w1_t, k + 1)
                act.activation(W1[:, 4 * k:4 * k + 4, :], ACC[k % 2][:].rearrange("p (a b) -> p a b", b=P),
                               ACT.Copy).then_inc(w1_in, 1)
            mixer(0, 0, True)
            mixer_input(2, 0)
            mixer(1, 1, True)
            mixer_input(3, 1)
            with act.Fori(1, 3) as i:
                for b in range(2):
                    mixer(2 * i + b, b, True)
            mixer(6, 0, True)
            mixer(7, 1, False)

            with act.Fori(0, 4) as i:
                for b in range(2):
                    c = 2 * i + b
                    for s in range(2):
                        round_weights(unit_at("s5glu", c, s) + 1, 1 - s)
                    act.wait_ge(unit_done, unit_at("s5glu", c, 1) + 1)
                    act.activation(TB_, ACC[1][:], ACT.Sigmoid).then_inc(gate_sig, 1)
                    prepare("mlp0", c, "mlp_norm_2", PH[:, bass.ds(c, 1), :], b, (glu_out, c + 1))

            def mlp(l, hi, following):
                norm = f"mlp{l}"
                for g in range(GROUPS):
                    def up(i):
                        for s in range(2):
                            round_weights(unit_at(f"up{l}{g}", i, s) + 1, 1 - s)
                            if s == 0 and isinstance(i, int):
                                standard_deviation(norm)
                            hidden(hid_ready, 2 * i + s, (H1, H2)[s][:], HIDDEN[norm] - KC + g * KC + 2 * i + s + 1, hi)

                    if g == 0:
                        up(0)
                    with act.Fori(g == 0, 4) as i:
                        up(i)
                    if g < GROUPS - 1:
                        with act.Fori(0, 4) as i:
                            for s in range(2):
                                round_weights(unit_at(f"dn{l}{g}", i, s) + 1, 1 - s)
                following()

            def mlp0_end():
                with act.Fori(0, 4) as i:
                    residual(f"dn0{GROUPS - 1}", "kv", "kv_norm_2", PH, i)

            def mlp1_end():
                def down(i, last):
                    for s in range(2):
                        u = unit_at(f"dn1{GROUPS - 1}", i, s)
                        if s == 0 or not last:
                            round_weights(u + 1, 1 - s)
                        act.wait_ge(unit_out, u + 1)
                        square("last", 2 * i + s, X, s)

                with act.Fori(0, 3) as i:
                    down(i, False)
                down(3, True)

            mlp(0, QH, mlp0_end)
            act.wait_ge(fw_in, 128)
            act.activation(FWH[:], FWR[:], ACT.Copy).then_inc(fw_hi, 1)

            def kv(i, b):
                c = 2 * i + b
                for s in range(2):
                    round_weights(unit_at("kv", c, s) + 1, 1 - s)
                    if s == 0 and isinstance(c, int) and c == 0:
                        standard_deviation("kv")
                if b == 0 and isinstance(i, int):
                    act.wait_ge(unit_done, START["kv"])
                act.activation(QH[:, bass.ds(c, 1), :], X[:, bass.ds(c, 1), :], ACT.Copy,
                               scale=column(("mix_norm_2", KC), c)).then_inc(op_hi, 1)

            kv(0, 0)
            kv(0, 1)
            with act.Fori(1, 4) as i:
                for b in range(2):
                    kv(i, b)
            act.wait_ge(f_abs, 1)
            act.activation(F[:], F[:], ACT.Exp, scale=-1.0).then_inc(f_exp, 1)
            act.wait_ge(f_exp, 1)
            act.activation(F[:], F[:], ACT.Ln, bias=ONES[:, 0:1]).then_inc(f_ln, 1)
            with act.Fori(0, 4) as i:
                plain("wq", i)
            act.wait_ge(unit_done, START["wo"])
            act.wait_ge(f_sum, 1)
            act.activation(FH[:], F[:], ACT.Copy).then_inc(f_ready, 1)
            act.wait_ge(f_ready, 1)
            act.activation(RF[0:32, :], FH[0:32, :].bitcast(F32), ACT.Copy, scale=-1.0)
            act.activation(LF[64:96, :], FH[64:96, :].bitcast(F32), ACT.Copy)
            act.drain().then_inc(f_ready, 1)
            attend("fox", 8)
            with act.Fori(0, 4) as i:
                residual("wo", "mlp1", ("mlp_norm_2", KC), QH, i)
            mlp(1, PH, mlp1_end)
            standard_deviation("last")
            for c in range(0, KC, 2):
                act.wait_ge(y_t, c + 1)
                act.activation(YROW[:, :, c * P:(c + 1) * P], TR[0][:].rearrange("p (b f) -> p b f", f=P), ACT.Copy)\
                   .then_inc(y_even, 1)

        @block.gpsimd
        def _(pool):
            def remainder(u, s):
                pool.wait_ge(w_hi, u + 1)
                pool.tensor_tensor(WL[:, s], RAW[:, s], WH[:, s], ALU.subtract).then_inc(w_lo, 1)

            def add_square(norm, c, s):
                pool.wait_ge(sq_ready, SQUARES[norm] + c + 1)
                if isinstance(c, int) and c == 0:
                    if NORM[norm]:
                        pool.wait_ge(st_sum, NORM[norm])
                    pool.tensor_copy(SSQ[:], SQ[:, s, :]).then_inc(sq_used, 1)
                else:
                    pool.tensor_tensor(SSQ[:], SSQ[:], SQ[:, s, :], ALU.add).then_inc(sq_used, 1)
                pool.drain()

            pool.memset(U[:, :, 0:PAD], 0.0).then_inc(u_zero, 1)
            pool.memset(VSH[0][:].bitcast(F32), 0.0).then_inc(pad_zero, 1)
            pool.memset(VSL[0][:].bitcast(F32), 0.0).then_inc(pad_zero, 1)
            remainder(0, 0)
            for c in range(KC):
                add_square("mix", c, c % 2)
            with pool.Fori(0, 4) as i:
                for s in range(2):
                    remainder(unit_at("glu", i, s) + 1, 1 - s)
            for j in range(8):
                remainder(START["in"] + j + 1, (j + 1) % 2)
                if j in (2, 3):
                    pool.wait_ge(u_hi, j - 1)
                    pool.tensor_tensor(UL[:, j - 2, :], U[:, j, :], UH[:, j - 2, :], ALU.subtract).then_inc(u_lo, 1)
            pool.wait_ge(wc_hi, 1)
            pool.tensor_tensor(WCL[:], WC, WCH[:], ALU.subtract)
            pool.drain()

            def diagonals(j):
                c, first = 2 + j // 4, j % 4 * TAPS
                n = min(TAPS, CONVW - first)
                if j >= 2:
                    pool.wait_ge(diag_used, j - 1)
                for to, w in ((DGH, WCH), (DGL, WCL)):
                    taps = w[:].rearrange("p (k c) -> p k c", c=BCH)[:, first:first + n, c]
                    ins = pool.tensor_tensor(to[j % 2][:, 0:n, :], IDENT[:, None, :].to_broadcast([P, n, P]),
                                             taps.bitcast(F32)[:, :, None].to_broadcast([P, n, P]), ALU.mult)
                ins.then_inc(diag_ready, 1)

            for j in range(8):
                rows = P if j not in (0, 3) else 64
                pool.wait_ge(rot_done, j + 1)
                pool.tensor_tensor(DS[0:rows, j, :], DS[0:rows, j, :], COS[0:rows, :], ALU.mult).then_inc(rope_cos, 1)
            pool.wait_ge(v_hi, 3)
            pool.tensor_tensor(KSL[0][:], KD[:, 1, :], KSH[0][:], ALU.subtract).then_inc(k_lo, 1)
            diagonals(0)
            diagonals(1)
            for qb in range(1, TB):
                diagonal = SC[:, qb - 1, qb * P:(qb + 1) * P]
                pool.wait_ge(index_sum, IDXH * qb)
                pool.affine_select(out=diagonal, in_=diagonal, compare_op=ALU.is_ge, fill=FAR, base=0,
                                   pattern=[[-1, P]], channel_multiplier=1).then_inc(index_masked, 1)
            for name in ("memk", "memv"):
                with pool.Fori(0, 4) as i:
                    for s in range(2):
                        remainder(unit_at(name, i, s) + 1, 1 - s)
            def free(kind, c, first):
                if not first:
                    pool.wait_ge(e_done, TILES[kind] + SIZE[kind] * (c - 1) + 4)

            def queries(c, b, first, last):
                free("sparse", c, first)
                pool.tensor_copy(AQH[b][:], DS[:, bass.ds(c + 4, 1), :])
                pool.drain()
                pool.tensor_tensor(AQL[b][:], DS[:, bass.ds(c + 4, 1), :], AQH[b][:], ALU.subtract).then_inc(staged, 1)

            queries(0, 0, True, False)
            for j in range(2, 8):
                diagonals(j)
            queries(1, 1, True, False)
            for c in range(BCH):
                add_square("ln", c, c % 2)
            for c in range(2, 4):
                queries(c, c % 2, False, False)
            for c in range(BCH):
                pool.wait_ge(branch_hi, c + 1)
                pool.tensor_tensor(QL[:, 4 + c, :], CV[c][:], QH[:, 4 + c, :], ALU.subtract).then_inc(branch_lo, 1)

            def residual(name, norm, i, last=False):
                for s in range(2):
                    if not last or s == 0:
                        remainder(START[name] + 2 * i + s + 1, 1 - s)
                    add_square(norm, 2 * i + s, s)
                    if norm == "final":
                        pool.wait_ge(sq2_ready, 2 * i + s + 1)
                        if isinstance(i, int) and 2 * i + s == 0:
                            pool.tensor_copy(SSQ2[:], SQ2[:, s, :]).then_inc(sq2_used, 1)
                        else:
                            pool.tensor_tensor(SSQ2[:], SSQ2[:], SQ2[:, s, :], ALU.add).then_inc(sq2_used, 1)
                        pool.drain()

            residual("out", "cross", 0)
            with pool.Fori(1, 4) as i:
                residual("out", "cross", i)
            def heads_low(c):
                b = c % 2
                pool.wait_ge(q_hi, 2 * c + 1)
                pool.tensor_tensor(CQL[b][:], QT[:, 2 * c:2 * c + 2, :], CQH[b][:], ALU.subtract)
                pool.wait_ge(q_hi, 2 * c + 2)
                pool.tensor_tensor(CKL[b][:], KM[:, 2 * c:2 * c + 2, :], CKH[b][:], ALU.subtract).then_inc(staged, 1)

            def heads(c):
                heads_low(c)
                pool.wait_ge(v_t, c + 1)
                pool.tensor_copy(CVS[:], VM[:, 2 * c:2 * c + 2, :]).then_inc(cvs_in, 1)

            with pool.Fori(0, 2) as i:
                for s in range(2):
                    remainder(unit_at("qc", i, s) + 1, 1 - s)
            heads(0)
            with pool.Fori(2, 4) as i:
                for s in range(2):
                    remainder(unit_at("qc", i, s) + 1, 1 - s)
            pool.wait_ge(row_in, 48)
            pool.tensor_copy(S5ROW[:, 2, :].rearrange("j (g p) -> j g p", g=2),
                             DTROW[:, :, None].to_broadcast([JP, 2, 64])).then_inc(row_out, 1)
            for c in range(1, 4):
                heads(c)
            residual("oc", "ffn", 0)
            with pool.Fori(1, 4) as i:
                residual("oc", "ffn", i)
            pool.memset(G[:, 0:2], 0.0).then_inc(g_zero, 1)
            pool.sem_inc(sq2_used, 2)
            for g, n in FFN_GROUPS:
                with pool.Fori(0, n) as i:
                    for s in range(2):
                        remainder(unit_at(f"ffn{g}", i, s) + 1, 1 - s)
                if g != FFN_GROUPS[-1][0]:
                    with pool.Fori(0, 4) as i:
                        for s in range(2):
                            remainder(unit_at(f"down{g}", i, s) + 1, 1 - s)
            residual(f"down{g}", "final", 0)
            with pool.Fori(1, 4) as i:
                residual(f"down{g}", "final", i)
            pool.wait_ge(params, 1)
            for x in (W1T[0], W1T[1], KB, CL, SPV, RHOT):
                pool.memset(x[:], 0.0)
            pool.drain()
            pool.nop().then_inc(zeroed, 1)

            def generate(c, b):
                four = bass.ds(4 * c, 4)
                if not isinstance(c, int) or c >= 2:
                    pool.wait_ge(k_mm, c - 1)
                for ri in range(2):
                    for j in range(2):
                        a = PW[:, j if ri == 0 else 1 - j, 0:LAG, four][:, :, :, None].to_broadcast([P, LAG, 4, 16])
                        d = BB[:, j, four, :][:, None, :, :].to_broadcast([P, LAG, 4, 16])
                        pool.tensor_tensor(GT[:, j], a, d, ALU.mult)
                    pool.drain()
                    for g in range(2):
                        rows = slice(64 * g, 64 * g + 64)
                        pool.tensor_tensor(W1T[b][rows, :, ri, :, g, :], GT[rows, 0], GT[rows, 1],
                                           (ALU.subtract, ALU.add)[ri])
                    pool.drain()
                pool.nop().then_inc(gen_ready, 1)

            def generate_c(c, b):
                four = bass.ds(4 * c, 4)
                if not isinstance(c, int) or c >= 2:
                    pool.wait_ge(y_mm, c - 1)
                for ri in range(2):
                    for j in range(2):
                        a = PW[:, j if ri == 0 else 1 - j, :, four][:, :, :, None].to_broadcast([P, LAG + 1, 4, 16])
                        d = CC[:, j, four, :][:, None, :, :].to_broadcast([P, LAG + 1, 4, 16])
                        pool.tensor_tensor(GC[:, j], a, d, ALU.mult)
                    pool.drain()
                    for g in range(2):
                        rows = slice(64 * g, 64 * g + 64)
                        pool.tensor_tensor(CL[rows, b, ri, :, :, g, :], GC[rows, ri], GC[rows, 1 - ri],
                                          (ALU.add, ALU.subtract)[ri])
                    pool.drain()
                pool.nop().then_inc(cl_ready, 1)

            generate(0, 0)
            generate_c(0, 0)
            generate(1, 1)
            generate_c(1, 1)
            with pool.Fori(1, 4) as i:
                for b in range(2):
                    generate(2 * i + b, b)
                    generate_c(2 * i + b, b)

            def glu(i):
                for b in range(2):
                    c = 2 * i + b
                    for s in range(2):
                        remainder(unit_at("s5glu", c, s) + 1, 1 - s)
                    add_square("mlp0", c, b)

            glu(0)
            with pool.Fori(1, 4) as i:
                glu(i)
            pool.memset(FWR[:], 0.0)
            pool.memset(BF[:], 0.0)
            pool.memset(VSH[0][:].bitcast(F32), 0.0)
            pool.memset(VSL[0][:].bitcast(F32), 0.0)
            pool.drain().then_inc(fw_zero, 1)

            def mlp(l, norm):
                def remainders(name):
                    with pool.Fori(0, 4) as i:
                        for s in range(2):
                            remainder(unit_at(name, i, s) + 1, 1 - s)

                for g in range(GROUPS):
                    remainders(f"up{l}{g}")
                    if g < GROUPS - 1:
                        remainders(f"dn{l}{g}")
                name = f"dn{l}{GROUPS - 1}"
                residual(name, norm, 0)
                with pool.Fori(1, 3) as i:
                    residual(name, norm, i)
                residual(name, norm, 3, last=l == 1)

            mlp(0, "kv")
            pool.wait_ge(fw_hi, 1)
            pool.tensor_tensor(FWL[:], FWR[:], FWH[:], ALU.subtract).then_inc(fw_lo, 1)
            with pool.Fori(0, 8) as i:
                for s in range(2):
                    remainder(unit_at("kv", i, s) + 1, 1 - s)
            def keys_split(c, b):
                pool.tensor_copy(KSH[b][:], KT[:, bass.ds(c, 1), :])
                pool.drain()
                pool.tensor_tensor(KSL[b][:], KT[:, bass.ds(c, 1), :], KSH[b][:], ALU.subtract)

            def queries_split(c, b):
                pool.tensor_copy(QSH[b][:], QT[:, bass.ds(c, 1), :])
                pool.drain()
                pool.tensor_tensor(QSL[b][:], QT[:, bass.ds(c, 1), :], QSH[b][:], ALU.subtract)

            def values_out(c):
                pool.wait_ge(v_t, 5 + c)
                pool.tensor_copy(VS[:], VT[:, bass.ds(c, 1), :]).then_inc(cvs_in, 1)

            for i in range(4):
                for s in range(2):
                    remainder(unit_at("wq", i, s) + 1, 1 - s)
                if i == 0:
                    pool.wait_ge(unit_out, START["wq"])
                    keys_split(0, 0)
                    values_out(0)
                if i == 2:
                    pool.wait_ge(unit_out, START["wq"] + 1)
                    queries_split(0, 0)

            def heads(c, b, first, last):
                free("fox", c, first)
                if not first:
                    queries_split(c, b)
                    keys_split(c, b)
                for half in range(2):
                    for j, (to, fixed) in enumerate(((LQ, LF), (RK, RF))):
                        head = HOT[:, bass.ds(2 * c + half + NHEAD * j, 1)]
                        pool.tensor_tensor(to[:, 2 * b + half, :], fixed[:], head.to_broadcast([P, T]), ALU.add)
                    pool.drain().then_inc(staged, 1)
                    if half == 0 and not first:
                        values_out(c)

            def padding():
                pool.memset(VSH[1][:].bitcast(F32), 0.0)
                pool.memset(VSL[1][:].bitcast(F32), 0.0)
                pool.drain().then_inc(pad_zero, 1)

            pool.wait_ge(f_ready, 3)
            groups(pool, 8, heads, (padding, None))
            residual("wo", "mlp1", 0)
            with pool.Fori(1, 4) as i:
                residual("wo", "mlp1", i)
            mlp(1, "last")

        @block.tensor
        def _(pe):
            def unit(u, s, xh, xl, n=T, kc=KC, chunks=None):
                pe.wait_ge(w_hi, u + 1)
                if not isinstance(u, int) or u >= 2:
                    pe.wait_ge(unit_out, u - 1)
                for k in range(kc):
                    if chunks:
                        pe.wait_ge(chunks[0], chunks[1] + k + 1)
                    pe.matmul(ACC[s][:, 0:n], WH[:, s, k, :], xh[:, k, :], start=(k == 0), stop=False)
                    pe.matmul(ACC[s][:, 0:n], WH[:, s, k, :], xl[:, k, :], start=False, stop=False)
                pe.wait_ge(w_lo, u + 1)
                for k in range(kc):
                    mm = pe.matmul(ACC[s][:, 0:n], WL[:, s, k, :], xh[:, k, :], start=False, stop=(k == kc - 1))
                mm.then_inc(unit_done, 1)

            def column_sums(norm):
                pe.wait_ge(sq_used, SQUARES[norm] + dict(NORMS)[norm])
                if NORM[norm]:
                    pe.wait_ge(st_rs, NORM[norm])
                for b in range(TB):
                    mm = pe.matmul(ST[:, b:b + 1], SSQ[:, b * P:(b + 1) * P], ONES[:, 0:1], start=True, stop=True)
                mm.then_inc(st_sum, 1)

            def spread_scales(norm):
                pe.wait_ge(st_diag, NORM[norm] + 1)
                pe.matmul(ST[:], ONES, DIAG[:], start=True, stop=True).then_inc(st_bc, 1)

            pe.wait_ge(cst_in, 16)
            for c in range(KC):
                if c % 2 == 0:
                    pe.wait_ge(x_in[c // 2], 16)
                if c >= 2:
                    pe.wait_ge(x_ready, c - 1)
                for b in range(TB):
                    mm = pe.transpose(TR[c % 2][:, b * P:(b + 1) * P], XROW[:, b, c * P:(c + 1) * P], IDENT)
                mm.then_inc(x_t, 1)
                if c == 0:
                    pe.wait_ge(vec_in, 16 * len(VECTORS))
                    for t in range(3):
                        mm = pe.transpose(ST[:, t * P:t * P + ROWS[t]], VROW[0:ROWS[t], t, :], IDENT[0:ROWS[t], 0:ROWS[t]])
                    mm.then_inc(vec_t, 1)
            unit(0, 0, PH, PL, chunks=(op_lo, NOPERAND["mix"]))
            column_sums("mix")
            unit(1, 1, PH, PL)
            spread_scales("mix")

            def memory(first):
                pe.wait_ge(mem_scaled, MB)
                for c in range(first, first + 2):
                    if c >= 2:
                        pe.wait_ge(mem_lo, c - 1)
                    for b in range(MB):
                        mm = pe.transpose(S[c % 2][:, b * P:(b + 1) * P], MROW[:, b, c * P:(c + 1) * P], IDENT)
                    mm.then_inc(mem_t, 1)

            for i in range(1, 4):
                for s in range(2):
                    unit(unit_at("glu", i, s), s, PH, PL)
                memory(2 * i - 2)
            for s in range(2):
                unit(START["in"] + s, s, PH, PL)
            memory(6)
            with pe.Fori(1, 4) as i:
                for s in range(2):
                    unit(unit_at("in", i, s), s, PH, PL)
            for j in range(8):
                rows = P if j not in (0, 3) else 64
                pe.wait_ge(unit_out, START["in"] + j + 1)
                if j >= 2:
                    pe.wait_ge(rot_used, j - 1)
                pe.matmul(TR[j % 2][0:rows, :], ROTM[0:rows, 0:rows], DS[0:rows, j, :], start=True, stop=True)\
                  .then_inc(rot_done, 1)
                if j == 3:
                    for b in range(TB):
                        mm = pe.transpose(O[:, b * 4:b * 4 + 4], DS[64:68, 0, b * P:(b + 1) * P], IDENT[64:68, 64:68])
                    mm.then_inc(wi_t, 1)
                    for b in range(TB):
                        mm = pe.transpose(S[0][:, b * 64:(b + 1) * 64], DS[64:P, 3, b * P:(b + 1) * P], IDENT[64:P, 64:P])
                    mm.then_inc(v_t, 1)
            pe.wait_ge(kd_in[0], 16)
            pe.wait_ge(rope_done, 3)
            pe.wait_ge(v_lo, 2)
            for n in range(3 * IDXH):
                qb, h = n // IDXH + 1, n % IDXH
                rows = slice(h % 2 * 64, h % 2 * 64 + 64)
                if n >= 2:
                    pe.wait_ge(index_relu, n - 1)
                pe.matmul(S[n % 2][:, 0:(qb + 1) * P], DS[rows, 1 + h // 2, qb * P:(qb + 1) * P],
                          KD[rows, 0, 0:(qb + 1) * P], start=True, stop=True).then_inc(index_mm, 1)
            pe.wait_ge(mem_lo, KC)
            for name in ("memk", "memv"):
                with pe.Fori(0, 4) as i:
                    for s in range(2):
                        unit(unit_at(name, i, s), s, MH, ML, n=NMEM)

            def three(out, ah, al, bh, bl, first, last):
                pe.matmul(out, ah, bh, start=first, stop=False)
                pe.matmul(out, ah, bl, start=False, stop=False)
                return pe.matmul(out, al, bh, start=False, stop=last)

            def scores(kind, c, b, t):
                n = TILES[kind] + SIZE[kind] * c + t
                half, qb, nk = t // TB, t % TB, keys(kind, t)
                s = SB[t % SLOTS[kind]]
                q = slice(qb * P, (qb + 1) * P)
                if kind == "fox" and t % TB == 0:
                    pe.wait_ge(staged, STAGED[kind] + 2 * c + t // TB + 1)
                elif t == 0:
                    pe.wait_ge(staged, STAGED[kind] + c + 1)
                pe.wait_ge(e_done, n + 5 - SLOTS[kind])
                if kind == "cross":
                    for k in range(2):
                        mm = three(s[:, 0:nk], CQH[b][:, k, q], CQL[b][:, k, q], CKH[b][:, k, :], CKL[b][:, k, :], k == 0, k == 1)
                else:
                    rows = slice(half * 64, half * 64 + 64)
                    qh, ql, kh, kl = ((AQH[b], AQL[b], KSH[0], KSL[0]) if kind == "sparse" else
                                      (QSH[b], QSL[b], KSH[b], KSL[b]))
                    three(s[:, 0:nk], qh[rows, q], ql[rows, q], kh[rows, 0:nk], kl[rows, 0:nk], True, False)
                    if kind == "sparse":
                        mm = pe.matmul(s[:, 0:nk], IDR[:], SEL[:, qb, 0:nk], start=False, stop=True)
                    else:
                        pe.matmul(s[:, 0:nk], LQ[:, 2 * b + half, q], RK[:, 2 * b + half, 0:nk], start=False, stop=False)
                        mm = pe.matmul(s[:, q], IDR[:], TRIR[:], start=False, stop=True)
                mm.then_inc(s_ready, 1)

            def turn(kind, c, t):
                n = TILES[kind] + SIZE[kind] * c + t
                pe.wait_ge(e_scaled, n + 1)
                pe.wait_ge(pt_lo, n + 1)
                for k in range(keys(kind, t) // P):
                    mm = pe.transpose(TT[t % 2][:, k * P:(k + 1) * P], E4[kind][t % SLOTS[kind]][:, k * P:(k + 1) * P], IDENT)
                mm.then_inc(t_ready, 1)

            def values(kind, c, b, half):
                pe.wait_ge(pt_lo, TILES[kind] + SIZE[kind] * c + 4 * half + 6)
                if kind == "cross":
                    pe.wait_ge(v_lo, c + 3)
                    pe.wait_ge(o_lo, PAIRS["cross"] + 2 * c)
                    for m in range(2):
                        for k in range(MB):
                            mm = three((O, ST)[m][:], CVH[b][:, k, m * P:(m + 1) * P], CVL[b][:, k, m * P:(m + 1) * P],
                                       PTH[:, k, :], PTL[:, k, :], k == 0, k == MB - 1)
                        mm.then_inc(pv_done, 1)
                    return
                if kind == "fox" and half == 0:
                    pe.wait_ge(v_lo, 6 + 2 * c + 2)
                if half == 0 and not (kind == "sparse" and isinstance(c, int) and c == 0):
                    pe.wait_ge(o_lo, PAIRS[kind] + c)
                vh, vl = (VSH[0], VSL[0]) if kind == "sparse" else (VSH[b], VSL[b])
                for k in range(TB):
                    mm = three(O[:, k * P:T], vh[:, k, half, :], vl[:, k, half, :], PTH[:, k, k * P:T],
                               PTL[:, k, k * P:T], half == 0 and k == 0, half == 1 and k == TB - 1)
                mm.then_inc(pv_done, 1)

            def turn_values(kind, c, first):
                if kind == "cross":
                    pe.wait_ge(cvs_in, c + 1)
                    if not first:
                        pe.wait_ge(v_lo, c + 2)
                    for m in range(2):
                        for k in range(MB):
                            mm = pe.transpose(SB[3][:, k * 2 * P + m * P:k * 2 * P + (m + 1) * P],
                                              CVS[:, m, k * P:(k + 1) * P], IDENT)
                    mm.then_inc(v_t, 1)
                if kind == "fox":
                    pe.wait_ge(cvs_in, c + 5)
                    if not first:
                        pe.wait_ge(v_lo, 6 + 2 * c)
                    for k in range(TB):
                        mm = pe.transpose(ST[:, k * P:(k + 1) * P], VS[:, k * P:(k + 1) * P], IDENT)
                    mm.then_inc(v_t, 1)

            def attend(kind, n_groups, between=(None, None)):
                size, ahead = SIZE[kind], AHEAD[kind]
                halves = size // TB

                def group(c, b, first, last):
                    for t in range(size):
                        if t + ahead < size:
                            scores(kind, c, b, t + ahead)
                        elif not last:
                            scores(kind, c + 1, 1 - b, t + ahead - size)
                        turn(kind, c, t)
                        if t == 0 and not first:
                            values(kind, c - 1, 1 - b, halves - 1)
                        if t == TB:
                            values(kind, c, b, 0)
                        if t == size // 2 and not last:
                            turn_values(kind, c + 1, False)

                turn_values(kind, 0, True)
                for t in range(ahead):
                    scores(kind, 0, 0, t)
                groups(pe, n_groups, group, between)
                values(kind, n_groups - 1, 1, halves - 1)

            pe.wait_ge(u_lo, 2)
            for j in range(8):
                c, first = j // 4, j % 4 * TAPS
                n = min(TAPS, CONVW - first)
                out_ = (ST, O)[c][:]
                pe.wait_ge(diag_ready, j + 1)
                for k in range(n):
                    x = slice(first + k, first + k + T)
                    mm = three(out_, DGH[j % 2][:, k, :], DGL[j % 2][:, k, :], UH[:, c, x], UL[:, c, x],
                               first + k == 0, first + k == CONVW - 1)
                mm.then_inc(diag_used, 1)
            pe.sem_inc(t_ready, 4)
            pe.sem_inc(pv_done, 1)
            pe.wait_ge(sel_ready, TB)
            pe.wait_ge(k_lo, 1)
            pe.wait_ge(conv_done, 2)
            pe.wait_ge(conv_pe, 2)
            for c in range(BCH):
                mm = pe.matmul(ST[:], ONES, CV[c][:], start=(c == 0), stop=(c == BCH - 1))
            mm.then_inc(mean_sum, 1)
            attend("sparse", 4, (lambda: column_sums("ln"), lambda: spread_scales("ln")))
            pe.wait_ge(o_lo, PAIRS["sparse"] + 4)
            pe.wait_ge(branch_lo, BCH)
            with pe.Fori(0, 4) as i:
                for s in range(2):
                    unit(unit_at("out", i, s), s, QH, QL)

            def normed(name, norm, xh, xl, pairs):
                unit(START[name], 0, xh, xl, chunks=(op_lo, NOPERAND[norm]))
                column_sums(norm)
                unit(START[name] + 1, 1, xh, xl)
                spread_scales(norm)
                with pe.Fori(1, pairs) as i:
                    for s in range(2):
                        unit(unit_at(name, i, s), s, xh, xl)

            normed("qc", "cross", PH, PL, 4)
            attend("cross", 4)
            pe.wait_ge(row_out, 1)
            for j in range(3):
                mm = pe.transpose(S[1][:, j * JP:(j + 1) * JP], S5ROW[:, j, :], IDENT[0:JP, 0:JP])
            mm.then_inc(row_t, 1)
            pe.wait_ge(c_in, 64)
            for j in range(4):
                ri, first = j // 2, j % 2 * 4
                if j >= 2:
                    pe.wait_ge(c_out, j - 1)
                for k in range(4):
                    mm = pe.transpose(TR[j % 2][:, k * P:(k + 1) * P],
                                      CROW[:, ri, first + k, :, :].rearrange("p a b -> p (a b)"), IDENT)
                mm.then_inc(c_t, 1)
            pe.wait_ge(c_out, 4)
            pe.wait_ge(o_lo, PAIRS["cross"] + 8)
            with pe.Fori(0, 4) as i:
                for s in range(2):
                    unit(unit_at("oc", i, s), s, QH, QL)
            for g, n in FFN_GROUPS:
                if g == 0:
                    normed("ffn0", "ffn", PH, PL, n)
                else:
                    with pe.Fori(0, n) as i:
                        for s in range(2):
                            unit(unit_at(f"ffn{g}", i, s), s, PH, PL)
                unit(START[f"down{g}"], 0, QH, QL, kc=n, chunks=(hid_lo, g))
                unit(START[f"down{g}"] + 1, 1, QH, QL, kc=n)
                with pe.Fori(1, 4) as i:
                    for s in range(2):
                        unit(unit_at(f"down{g}", i, s), s, QH, QL, kc=n)
            pe.wait_ge(sq2_used, 2 + KC)
            for b in range(TB):
                pe.matmul(ST[:, TB + b:TB + b + 1], SSQ2[:, b * P:(b + 1) * P], ONES[:, 0:1], start=True, stop=True)
            column_sums("final")
            pe.wait_ge(diag2, 1)
            pe.matmul(O[:], ONES, DIAG2[:], start=True, stop=True).then_inc(bc2, 1)
            spread_scales("final")

            def turn_b(c, b):
                pe.wait_ge(gen_ready, c + 1)
                for k in range(2):
                    for m in range(4):
                        mm = pe.transpose(ACC[k % 2][:, m * P:(m + 1) * P],
                                          W1T[b][:, 2 * k + m // 2, m % 2].rearrange("p a b c -> p (a b c)"), IDENT)
                    mm.then_inc(w1_t, 1)

            def kernel_lags(c, b):
                pe.wait_ge(cl_ready, c + 1)
                if not isinstance(c, int) or c:
                    pe.wait_ge(kb_in, 4 * c)
                for j in range(4):
                    for ri in range(2):
                        mm = pe.matmul(O[32 * j:32 * j + 32, 0:32 * LAG].rearrange("p (k c) -> p k c", k=LAG),
                                       W1T[b][:, 0, ri, j].rearrange("p a b -> p (a b)"),
                                       CL[:, b, ri, 0:LAG, j].rearrange("p k a b -> p k (a b)"),
                                       start=(ri == 0), stop=(ri == 1))
                mm.then_inc(k_mm, 1)

            UCv = UC[:].rearrange("p b (i m) -> p b i m", i=LAG)

            def state_inputs(c, b):
                pe.wait_ge(w1_in, 2 * c + 2)
                pe.wait_ge(uc_ready, c + 1)
                if not isinstance(c, int) or c:
                    pe.wait_ge(l_used, c)
                for i in range(LAG):
                    for ri in range(2):
                        for j in range(4):
                            rows = slice(32 * j, 32 * j + 32)
                            mm = pe.matmul(FOUR[:, j, ri * NM:ri * NM + NM], W1[rows, 2 * (LAG - 1 - i) + ri, :],
                                           UCv[rows, b, i, :], start=(i == 0 and ri == 0), stop=(i == LAG - 1),
                                           skip_group_check=True)
                mm.then_inc(l_mm, 1)

            def mixer(c, b, more):
                kernel_lags(c, b)
                if more:
                    turn_b(c + 1, 1 - b)
                pe.wait_ge(kb_in, 4 * c + 4)
                if not isinstance(c, int) or c:
                    pe.wait_ge(y_out, c)
                Y = ST[:].rearrange("p (i m) -> p i m", i=LAG)
                for lag in range(LAG):
                    pe.matmul(Y[:, lag:LAG, :], KB[:, b, lag, :], UCv[:, b, 0:LAG - lag, :],
                              start=(lag == 0), stop=False, skip_group_check=True)
                if more:
                    state_inputs(c + 1, 1 - b)
                pe.wait_ge(sp_ready, c + 1)
                for i in range(LAG):
                    for ri in range(2):
                        for j in range(4):
                            mm = pe.matmul(Y[32 * j:32 * j + 32, i, :],
                                           CL[:, b, ri, i + 1, j].rearrange("p a b -> p (a b)"), SPV[:, ri, j, :],
                                           start=False, stop=(ri == 1 and i == LAG - 1), skip_group_check=True)
                mm.then_inc(y_mm, 1)

            turn_b(0, 0)
            state_inputs(0, 0)
            mixer(0, 0, True)
            with pe.Fori(0, 3) as i:
                for b in range(2):
                    mixer(2 * i + 1 + b, 1 - b, True)
            mixer(7, 1, False)

            def units(name, first, last, xh, xl):
                with pe.Fori(first, last) as i:
                    for s in range(2):
                        unit(unit_at(name, i, s), s, xh, xl)

            def first_pair(name, xh, xl, chunks):
                unit(START[name], 0, xh, xl, chunks=chunks)
                unit(START[name] + 1, 1, xh, xl)

            def mlp(l, x, h):
                for g in range(GROUPS):
                    if g == 0:
                        normed(f"up{l}{g}", f"mlp{l}", *x, 4)
                    else:
                        units(f"up{l}{g}", 0, 4, *x)
                    first_pair(f"dn{l}{g}", *h, (hid_lo, HIDDEN[f"mlp{l}"] + g * KC))
                    units(f"dn{l}{g}", 1, 4, *h)

            first_pair("s5glu", QH, QL, (hid_lo, HIDDEN["s5"]))
            units("s5glu", 1, 8, QH, QL)
            mlp(0, (PH, PL), (QH, QL))
            normed("kv", "kv", PH, PL, 8)
            pe.wait_ge(fw_lo, 1)
            for k in range(KC):
                mm = three(O[:], FWH[:, k, :], FWL[:, k, :], PH[:, k, :], PL[:, k, :], k == 0, k == KC - 1)
            mm.then_inc(f_mm, 1)
            pe.wait_ge(op_lo, NOPERAND["wq"] + KC)
            units("wq", 0, 4, QH, QL)
            pe.wait_ge(f_ready, 3)
            attend("fox", 8)
            pe.wait_ge(o_lo, PAIRS["fox"] + 8)
            units("wo", 0, 4, PH, PL)
            mlp(1, (QH, QL), (PH, PL))
            column_sums("last")
            spread_scales("last")
            for c in range(KC):
                pe.wait_ge(y_normed, c + 1)
                if c >= 2:
                    pe.wait_ge((y_even, y_odd)[c % 2], c // 2)
                for b in range(TB):
                    mm = pe.transpose(TR[c % 2][:, b * P:(b + 1) * P], X[:, c, b * P:(b + 1) * P], IDENT)
                mm.then_inc(y_t, 1)

        @block.vector
        def _(dve):
            def low(norm, c, gain, hi, lo):
                dve.wait_ge(op_hi, NOPERAND[norm] + c + 1)
                dve.scalar_tensor_tensor(lo, X[:, bass.ds(c, 1), :], column(gain, c), hi, ALU.mult, ALU.subtract)\
                   .then_inc(op_lo, 1)

            def newton(r, v, y):
                dve.tensor_tensor(y, r, r, ALU.mult)
                dve.drain()
                dve.scalar_tensor_tensor(y, y, -0.5, v, ALU.mult, ALU.mult)
                dve.drain()
                dve.scalar_tensor_tensor(r, y, 1.5, r, ALU.add, ALU.mult)
                dve.drain()

            def scales(norm, n):
                variance(norm, n)
                diagonal(norm)
                spread(norm)

            def variance(norm, n):
                dve.wait_ge(st_sum, NORM[norm] + 1)
                dve.tensor_scalar(V4[:], ST[:, 0:TB], 1.0 / n, EPS, ALU.mult, ALU.add).then_inc(st_var, 1)

            def diagonal(norm):
                dve.wait_ge(st_std, NORM[norm] + 1)
                dve.reciprocal(R4[:], SD4[:])
                dve.drain()
                newton(R4[:], V4[:], SD4[:])
                dve.tensor_tensor(DIAG[:].rearrange("p (b t) -> p b t", b=TB),
                                  IDENT[:, None, :].to_broadcast([P, TB, P]),
                                  R4[:, :, None].to_broadcast([P, TB, P]), ALU.mult).then_inc(st_diag, 1)

            def spread(norm):
                dve.wait_ge(st_bc, NORM[norm] + 1)
                dve.tensor_copy(RS[:], ST[:]).then_inc(st_rs, 1)
                dve.drain()

            for c in range(KC):
                dve.wait_ge(x_t, c + 1)
                dve.tensor_copy(X[:, c, :], TR[c % 2][:]).then_inc(x_ready, 1)
                if c == 0:
                    dve.wait_ge(vec_t, 1)
                    for t in range(3):
                        last = dve.tensor_copy(VEC[:, t, 0:ROWS[t]], ST[:, t * P:t * P + ROWS[t]])
                    last.then_inc(vec_c, 1)
                    dve.drain()
                if c >= 1:
                    low("mix", c - 1, "norm_mix_g", PH[:, c - 1, :], PL[:, c - 1, :])
            low("mix", KC - 1, "norm_mix_g", PH[:, KC - 1, :], PL[:, KC - 1, :])
            scales("mix", D)
            dve.wait_ge(u_zero, 1)

            def glu(i):
                u = unit_at("glu", i, 0)
                if i:
                    dve.wait_ge(gate_sig, i)
                dve.wait_ge(unit_done, u + 1)
                dve.tensor_tensor(TA, ACC[0][:], RS[:], ALU.mult).then_inc(unit_out, 1)
                dve.wait_ge(unit_done, u + 2)
                dve.tensor_tensor(TB_, ACC[1][:], RS[:], ALU.mult).then_inc(unit_out, 1)
                dve.drain().then_inc(gate_raw, 1)
                dve.wait_ge(gate_sig, i + 1)
                dve.tensor_tensor(U[:, bass.ds(i, 1), PAD:PAD + T], TA, TB_, ALU.mult).then_inc(u_ready, 1)
                dve.drain()

            def memory(first):
                for c in range(first, first + 2):
                    dve.wait_ge(mem_hi, c + 1)
                    dve.scalar_tensor_tensor(ML[:, c, :], S[c % 2][:, 0:NMEM], column("norm_mem_g", c), MH[:, c, :],
                                             ALU.mult, ALU.subtract).then_inc(mem_lo, 1)

            glu(0)
            dve.wait_ge(mem_sq, MB)
            dve.tensor_scalar(MV[:], MV[:], 1.0 / D, EPS, ALU.mult, ALU.add).then_inc(mem_var, 1)
            dve.wait_ge(mem_std, 1)
            dve.reciprocal(MR[:], MD[:])
            dve.drain()
            newton(MR[:], MV[:], MD[:])
            for b in range(MB):
                dve.tensor_scalar(MROW[:, b, :], MROW[:, b, :], MR[:, b:b + 1], None, ALU.mult)\
                   .then_inc(mem_scaled, 1)
            glu(1)
            memory(0)
            dve.wait_ge(pos_in, 16)
            dve.tensor_copy(COS[:], POSI[:])
            dve.drain()
            dve.tensor_scalar(SIN[:], COS[:], FREQ, None, ALU.mult)
            dve.drain()
            dve.tensor_scalar(COS[:], SIN[:], 1.0 / (2.0 * np.pi), MAGIC, ALU.mult, ALU.add)
            dve.drain()
            dve.tensor_scalar(COS[:], COS[:], -MAGIC, None, ALU.add)
            for part in TWO_PI:
                dve.drain()
                dve.scalar_tensor_tensor(SIN[:], COS[:], -part, SIN[:], ALU.mult, ALU.add)
            dve.drain()
            dve.tensor_scalar(SIN[:], SIN[:], PI_BELOW, -PI_BELOW, ALU.min, ALU.max)
            dve.drain()
            dve.scalar_tensor_tensor(COS[:], SIN[:], -1.0, SIN[:], ALU.mult, ALU.max)
            dve.drain()
            dve.tensor_scalar(COS[:], COS[:], -1.0, float(np.pi / 2), ALU.mult, ALU.add).then_inc(ang, 1)
            glu(2)
            memory(2)
            glu(3)
            memory(4)

            def taps(first, last):
                for k in range(first, last):
                    for c in range(2):
                        x = U[:, c, k:k + T]
                        if k == 0:
                            ins = dve.tensor_scalar(CV[c][:], x, column("conv_b_w", c), column("conv_b_b", c),
                                                    ALU.mult, ALU.add)
                        else:
                            ins = dve.scalar_tensor_tensor(CV[c][:], x, column("conv_b_w", BCH * k + c), CV[c][:],
                                                           ALU.mult, ALU.add)
                        if k == CONVW - 1:
                            ins.then_inc(conv_done, 1)
                    dve.drain()

            SCALE = [1.0, 0.125, 0.125, 1.0, 0.125, 0.125, 0.125, 0.125]
            for j in range(8):
                u = START["in"] + j
                dve.wait_ge(unit_done, u + 1)
                dve.scalar_tensor_tensor(DS[:, j, :], ACC[j % 2][:], SCALE[j], RS[:], ALU.mult, ALU.mult)\
                   .then_inc(unit_out, 1)
                if j == 1:
                    memory(6)
                if j < 6:
                    taps(4 * j, 4 * j + 4)
            for j in range(8):
                rows = P if j not in (0, 3) else 64
                to = KD[0:64, j // 3, :] if j in (0, 3) else DS[:, j, :]
                if j == 6:
                    dve.wait_ge(wi_t, 1)
                    dve.tensor_scalar(WI[:].rearrange("p b h -> p (b h)"), O[:, 0:TB * 4], 0.5, None, ALU.mult)
                    for half in range(2):
                        cols = slice(half * 64, half * 64 + 64)
                        dve.wait_ge(v_hi, 2)
                        dve.tensor_tensor(VSL[0][:, :, half, cols], S[0][:, 0:TB * 64].rearrange("p (b f) -> p b f", b=TB),
                                          VSH[0][:, :, half, cols], ALU.subtract).then_inc(v_lo, 1)
                dve.wait_ge(rot_done, j + 1)
                dve.tensor_tensor(E[0:rows, j % 2, :], TR[j % 2][0:rows, :], SIN[0:rows, :], ALU.mult)\
                   .then_inc(rot_used, 1)
                dve.drain()
                dve.wait_ge(rope_cos, j + 1)
                dve.tensor_tensor(to, DS[0:rows, j, :], E[0:rows, j % 2, :], ALU.add).then_inc(rope_done, 1)
            for n in range(3 * IDXH):
                qb, h = n // IDXH + 1, n % IDXH
                nk = (qb + 1) * P
                dve.drain()
                dve.wait_ge(index_relu, n + 1)
                if h == 0:
                    ins = dve.tensor_scalar(SC[:, qb - 1, 0:nk], E[:, n % 2, 0:nk], WI[:, qb, h:h + 1], None, ALU.mult)
                else:
                    ins = dve.scalar_tensor_tensor(SC[:, qb - 1, 0:nk], E[:, n % 2, 0:nk], WI[:, qb, h:h + 1],
                                                   SC[:, qb - 1, 0:nk], ALU.mult, ALU.add)
                ins.then_inc(index_sum, 1)
            dve.tensor_copy(SEL[:, 0, 0:P], TRI).then_inc(sel_ready, 1)
            dve.wait_ge(index_masked, 3)
            with dve.Fori(0, TOPK // 8) as r:
                for b in range(3):
                    dve.max(M8[:, b, :], SC[:, b, 0:(b + 2) * P])
                dve.drain()
                for b in range(3):
                    dve.match_replace(SC[:, b, 0:(b + 2) * P], M8[:, b, :], SC[:, b, 0:(b + 2) * P], TAKEN)
                dve.drain()
            for b in range(3):
                dve.tensor_scalar(SEL[:, b + 1, 0:(b + 2) * P], SC[:, b, 0:(b + 2) * P], TAKEN, -BIG,
                                  ALU.not_equal, ALU.mult).then_inc(sel_ready, 1)
            taps(24, CONVW)

            def negative_max(kind, n, t):
                nk, j = keys(kind, t % SIZE[kind]), t % SLOTS[kind]
                dve.wait_ge(s_ready, n + 1)
                dve.wait_ge(e_done, n + 5 - SLOTS[kind])
                dve.tensor_reduce(NMX[:, j, :], SB[j][:, 0:nk], AX, ALU.max, negate=True).then_inc(mx_ready, 1)

            def divide(kind, n, t):
                nk, j = keys(kind, t), t % SLOTS[kind]
                dve.wait_ge(e_done, n + 5)
                dve.reciprocal(REC[:, j, :], SUM[:, j, :])
                dve.drain()
                dve.tensor_scalar(E4[kind][j][:, 0:nk], E4[kind][j][:, 0:nk], REC[:, j, :], None, ALU.mult).then_inc(e_scaled, 1)

            def turned_low(n, t, qb, kb):
                to = (slice(None), slice(0, kb), slice(qb * P, (qb + 1) * P))
                dve.wait_ge(pt_hi, n + 1)
                dve.tensor_tensor(PTL[to], TT[t % 2][:, 0:kb * P].rearrange("p (k q) -> p k q", q=P), PTH[to],
                                  ALU.subtract).then_inc(pt_lo, 1)

            def low_out(bank_, lo, hi, k):
                dve.wait_ge(o_hi, k + 1)
                dve.tensor_tensor(lo, bank_[:], hi, ALU.subtract).then_inc(o_lo, 1)

            def out_low(kind, c):
                hi, lo = OUT[kind]
                for m in range(1 + (kind == "cross")):
                    k = 2 * c + m if kind == "cross" else c
                    low_out((O, ST)[m], lo[:, bass.ds(k, 1), :], hi[:, bass.ds(k, 1), :], PAIRS[kind] + k)

            def values_low(kind, c, b):
                if kind == "cross":
                    dve.wait_ge(v_hi, c + 4)
                    dve.tensor_tensor(CVL[b][:], SB[3].rearrange("p (b f) -> p b f", b=MB), CVH[b][:], ALU.subtract)\
                       .then_inc(v_lo, 1)
                if kind == "fox":
                    dve.wait_ge(v_hi, 9 + 2 * c)
                    for half in range(2):
                        cols = slice(half * 64, half * 64 + 64)
                        dve.tensor_tensor(VSL[b][:, :, half, cols],
                                          ST[:].rearrange("p (b h f) -> p b h f", b=TB, h=2)[:, :, half, :],
                                          VSH[b][:, :, half, cols], ALU.subtract).then_inc(v_lo, 1)

            def attend(kind, n_groups, between=(None, None)):
                size, ahead = SIZE[kind], 2

                def low_tile(c, t):
                    turned_low(TILES[kind] + size * c + t, t, t % TB, keys(kind, t) // P)

                def group(c, b, first, last):
                    n = TILES[kind] + size * c
                    for t in range(size):
                        divide(kind, n + t, t)
                        if t == 0 and not first:
                            low_tile(c - 1, size - 1)
                        if not last or t + ahead < size:
                            negative_max(kind, n + t + ahead, t + ahead)
                        if t:
                            low_tile(c, t - 1)
                        if t == 1 and not first:
                            out_low(kind, c - 1)
                        if t == size - 1 and not last:
                            values_low(kind, c + 1, 1 - b)

                values_low(kind, 0, 0)
                for t in range(ahead):
                    negative_max(kind, TILES[kind] + t, t)
                groups(dve, n_groups, group, between)
                low_tile(n_groups - 1, size - 1)
                out_low(kind, n_groups - 1)

            dve.sem_inc(pt_lo, 2)
            dve.wait_ge(mean_sum, 1)
            for c in range(BCH):
                dve.scalar_tensor_tensor(CV[c][:], ST[:], -1.0 / (BCH * P), CV[c][:], ALU.mult, ALU.add)\
                   .then_inc(centred, 1)
            def norm_branch():
                diagonal("ln")
                spread("ln")
                for c in range(BCH):
                    dve.tensor_tensor(CV[c][:], CV[c][:], RS[:], ALU.mult).then_inc(ln_scaled, 1)

            attend("sparse", 4, (lambda: variance("ln", BCH * P), norm_branch))

            def residual(name, norm, gain, hi, lo, i):
                for s in range(2):
                    c = 2 * i + s
                    x = X[:, bass.ds(c, 1), :]
                    dve.wait_ge(unit_done, START[name] + c + 1)
                    dve.tensor_tensor(x, x, ACC[s][:], ALU.add).then_inc(unit_out, 1)
                    low(norm, c, gain, hi[:, bass.ds(c, 1), :], lo[:, bass.ds(c, 1), :])

            with dve.Fori(0, 4) as i:
                residual("out", "cross", "norm_cross_g", PH, PL, i)
            scales("cross", D)

            def scaled(name, i, to, k=1.0):
                for s in range(2):
                    u = unit_at(name, i, s)
                    dve.wait_ge(unit_done, u + 1)
                    dve.scalar_tensor_tensor(to[:, bass.ds(2 * i + s, 1), :], ACC[s][:], k, RS[:], ALU.mult, ALU.mult)\
                       .then_inc(unit_out, 1)

            with dve.Fori(0, 4) as i:
                scaled("qc", i, QT, 1.0 / 16)
            attend("cross", 4)
            dve.wait_ge(row_t, 1)
            dve.tensor_copy(LAM[:].rearrange("p a b -> p (a b)"), S[1][:, 0:3 * JP])
            for j in range(4):
                dve.wait_ge(c_t, j + 1)
                for g in range(2):
                    rows = slice(64 * g, 64 * g + 64)
                    src = TR[j % 2][rows, :].rearrange("p (j g c) -> p j g c", g=2, c=16)[:, :, g, :]
                    ins = dve.tensor_scalar(CC[rows, j // 2, j % 2 * 16:j % 2 * 16 + 16, :], src, (1.0, -1.0)[j // 2],
                                            None, ALU.mult)
                ins.then_inc(c_out, 1)
            w = [SW[:, k, :] for k in range(10)]

            def exponential(out, x, n, r, q):
                dve.drain()
                dve.tensor_scalar(n, x, float(1.0 / np.log(2.0)), MAGIC, ALU.mult, ALU.add)
                dve.drain()
                dve.tensor_scalar(n, n, -MAGIC, -126.0, ALU.add, ALU.max)
                dve.drain()
                dve.scalar_tensor_tensor(r, n, -LN2[0], x, ALU.mult, ALU.add)
                dve.drain()
                dve.scalar_tensor_tensor(r, n, -LN2[1], r, ALU.mult, ALU.add)
                dve.tensor_scalar(POW2[:], n, 127.0, float(2 ** 23), ALU.add, ALU.mult)
                dve.drain()
                dve.tensor_scalar(q, r, 1.0 / 5040, None, ALU.mult)
                for k in (720.0, 120.0, 24.0, 6.0, 2.0, 1.0):
                    dve.drain()
                    dve.scalar_tensor_tensor(q, q, 1.0 / k, r, ALU.add, ALU.mult)
                dve.drain()
                dve.scalar_tensor_tensor(out, q, 1.0, POW2[:].bitcast(F32), ALU.add, ALU.mult)
                dve.drain()

            residual("oc", "ffn", "norm_ffn_g", PH, PL, 0)
            exponential(LAM[:, 2, :], LAM[:, 2, :], w[3], w[4], w[5])
            dve.tensor_tensor(w[0], LAM[:, 0, :], LAM[:, 2, :], ALU.mult)
            dve.tensor_tensor(w[1], LAM[:, 1, :], LAM[:, 2, :], ALU.mult)
            dve.tensor_tensor(w[7], LAM[:, 0, :], LAM[:, 0, :], ALU.mult)
            dve.tensor_tensor(w[8], LAM[:, 1, :], LAM[:, 1, :], ALU.mult)
            dve.drain()
            dve.tensor_tensor(w[7], w[7], w[8], ALU.add)
            dve.tensor_scalar(w[3], w[1], 1.0 / (2.0 * np.pi), MAGIC, ALU.mult, ALU.add)
            dve.drain()
            dve.reciprocal(w[8], w[7]).then_inc(den_inv, 1)
            dve.tensor_scalar(w[3], w[3], -MAGIC, None, ALU.add)
            for part in TWO_PI:
                dve.drain()
                dve.scalar_tensor_tensor(w[1], w[3], -part, w[1], ALU.mult, ALU.add)
            dve.drain()
            dve.tensor_scalar(w[1], w[1], PI_BELOW, -PI_BELOW, ALU.min, ALU.max)
            dve.drain()
            dve.scalar_tensor_tensor(w[9], w[1], -1.0, w[1], ALU.mult, ALU.max)
            residual("oc", "ffn", "norm_ffn_g", PH, PL, 1)
            exponential(w[2], w[0], w[3], w[4], w[5])
            dve.tensor_scalar(w[9], w[9], -1.0, float(np.pi / 2), ALU.mult, ALU.add)
            dve.tensor_tensor(w[3], w[2], w[2], ALU.mult)
            dve.drain()
            dve.tensor_tensor(RHO[:], w[3], w[3], ALU.mult)
            dve.drain().then_inc(angle_ready, 1)
            residual("oc", "ffn", "norm_ffn_g", PH, PL, 2)
            def mul(out, a, b):
                dve.tensor_tensor(out, a, b, ALU.mult)

            def wide(x):
                return x[:, :, None].to_broadcast([P, JP, 16])

            LBR, LBI = PW[:, 0, 1, :], PW[:, 1, 1, :]
            t = [SW[:, k, :] for k in range(10)]
            dve.wait_ge(sin_cos, 1)
            mul(LBR, t[2], t[6])
            mul(LBI, t[2], t[4])
            dve.tensor_copy(UT[:, 0, :], t[6])
            dve.tensor_copy(UT[:, 1, :], t[4])
            dve.memset(PW[:, 0, 0, :], 1.0)
            dve.memset(PW[:, 1, 0, :], 0.0)
            for k in range(1, LAG):
                dve.drain()
                mul(t[0], PW[:, 0, k, :], LBR)
                mul(t[1], PW[:, 1, k, :], LBI)
                mul(t[2], PW[:, 0, k, :], LBI)
                mul(t[3], PW[:, 1, k, :], LBR)
                dve.drain()
                dve.tensor_tensor(PW[:, 0, k + 1, :], t[0], t[1], ALU.subtract)
                dve.tensor_tensor(PW[:, 1, k + 1, :], t[2], t[3], ALU.add)
            for k in range(2):
                dve.drain()
                mul(t[0], UT[:, 0, :], UT[:, 0, :])
                mul(t[1], UT[:, 1, :], UT[:, 1, :])
                mul(t[2], UT[:, 0, :], UT[:, 1, :])
                dve.drain()
                dve.tensor_tensor(UT[:, 0, :], t[0], t[1], ALU.subtract)
                dve.tensor_scalar(UT[:, 1, :], t[2], 2.0, None, ALU.mult)
            dve.drain()
            residual("oc", "ffn", "norm_ffn_g", PH, PL, 3)

            def discretised():
                dve.wait_ge(den_inv, 1)
                dve.tensor_scalar(t[4], LBR, -1.0, None, ALU.add)
                dve.drain()
                mul(t[0], t[4], LAM[:, 0, :])
                mul(t[1], LBI, LAM[:, 1, :])
                mul(t[2], LBI, LAM[:, 0, :])
                mul(t[3], t[4], LAM[:, 1, :])
                dve.drain()
                dve.tensor_tensor(t[5], t[0], t[1], ALU.add)
                dve.tensor_tensor(t[6], t[2], t[3], ALU.subtract)
                dve.drain()
                mul(t[5], t[5], t[8])
                mul(t[6], t[6], t[8])
                dve.drain()
                dve.wait_ge(b_in, 32)
                for ri, (x, y, op) in enumerate(((t[5], t[6], ALU.subtract), (t[6], t[5], ALU.add))):
                    mul(BT[:, 0], wide(x), BRAW[:, 0])
                    mul(BT[:, 1], wide(y), BRAW[:, 1])
                    dve.drain()
                    dve.tensor_tensor(BB[:, ri], BT[:, 0], BT[:, 1], op)
                    dve.drain()
                dve.nop().then_inc(params, 1)

            def turn_table(k, part=0, parts=1):
                if k == 0:
                    dve.memset(ET[:, 0, :, 0], 1.0)
                    dve.memset(ET[:, 1, :, 0], 0.0)
                    dve.drain()
                n, m = 2 ** k, JP // parts
                pairs = slice(part * m, part * m + m)
                TMP = at(f"TMP{k}{part}", [P, 2, m, n], F32, 155648 + 6208)
                for ri in range(2):
                    for j in range(2):
                        u = UT[:, j if ri == 0 else 1 - j, pairs, None].to_broadcast([P, m, n])
                        dve.tensor_tensor(TMP[:, j], ET[:, j, pairs, 0:n], u, ALU.mult)
                    dve.drain()
                    dve.tensor_tensor(ET[:, ri, pairs, n:2 * n], TMP[:, 0], TMP[:, 1], (ALU.subtract, ALU.add)[ri])
                    dve.drain()
                if 2 * n < NM and part == parts - 1:
                    t = [SW[:, j, :] for j in range(3)]
                    dve.tensor_tensor(t[0], UT[:, 0, :], UT[:, 0, :], ALU.mult)
                    dve.tensor_tensor(t[1], UT[:, 1, :], UT[:, 1, :], ALU.mult)
                    dve.tensor_tensor(t[2], UT[:, 0, :], UT[:, 1, :], ALU.mult)
                    dve.drain()
                    dve.tensor_tensor(UT[:, 0, :], t[0], t[1], ALU.subtract)
                    dve.tensor_scalar(UT[:, 1, :], t[2], 2.0, None, ALU.mult)
                    dve.drain()

            def hidden_low(k, x, value, hi=QH, lo=QL):
                dve.wait_ge(hid_hi, value)
                dve.tensor_tensor(lo[:, bass.ds(k, 1), :], x, hi[:, bass.ds(k, 1), :], ALU.subtract).then_inc(hid_lo, 1)

            scales("ffn", D)
            dve.wait_ge(g_zero, 1)
            for g, n in FFN_GROUPS:
                turn_table(g // 4)
                with dve.Fori(0, n) as i:
                    u = unit_at(f"ffn{g}", i, 0)
                    f = i + g
                    dve.wait_ge(unit_done, u + 1)
                    dve.tensor_tensor(G[:, 2:2 + T], ACC[0][:], RS[:], ALU.mult).then_inc(unit_out, 1)
                    dve.drain()
                    dve.tensor_scalar(H1[:], G[:, 0:T], column("ffn_conv_w", f), column("ffn_conv_b", f), ALU.mult, ALU.add)
                    dve.drain()
                    dve.scalar_tensor_tensor(H1[:], G[:, 1:1 + T], column("ffn_conv_w", f + FC), H1[:], ALU.mult, ALU.add)
                    dve.drain()
                    dve.scalar_tensor_tensor(H1[:], G[:, 2:2 + T], column("ffn_conv_w", f + 2 * FC), H1[:], ALU.mult, ALU.add)\
                       .then_inc(gate_conv, 1)
                    dve.wait_ge(unit_done, u + 2)
                    dve.tensor_tensor(H2[:], ACC[1][:], RS[:], ALU.mult).then_inc(unit_out, 1)
                    dve.drain()
                    dve.wait_ge(gate_act, f + 1)
                    dve.tensor_tensor(H2[:], H2[:], H1[:], ALU.mult).then_inc(hid_ready, 1)
                    hidden_low(i, H2[:], f + 1)
                if g == 0:
                    discretised()
                if g != FFN_GROUPS[-1][0]:
                    turn_table(g // 4 + 1)

                def down(i, s):
                    x = X[:, bass.ds(2 * i + s, 1), :]
                    dve.wait_ge(unit_done, unit_at(f"down{g}", i, s) + 1)
                    dve.tensor_tensor(x, x, ACC[s][:], ALU.add).then_inc(unit_out, 1)

                if g == FFN_GROUPS[-1][0]:
                    for j in range(KC):
                        down(j // 2, j % 2)
                        if j < 2:
                            turn_table(g // 4 + 1, j, 2)
                        elif j < 6:
                            turn_table(g // 4 + 2, j - 2, 4)
                else:
                    with dve.Fori(0, 4) as i:
                        for s in range(2):
                            down(i, s)
                dve.drain()
            dve.tensor_tensor(G12[:], VEC[:, COLUMN["norm_final_g"][0], COLUMN["norm_final_g"][1]:COLUMN["norm_final_g"][1] + KC],
                              VEC[:, COLUMN["mix_norm_2"][0], COLUMN["mix_norm_2"][1]:COLUMN["mix_norm_2"][1] + KC], ALU.mult)
            dve.wait_ge(st_sum, NORM["final"] + 1)
            dve.tensor_scalar(V4[:], ST[:, 0:TB], 1.0 / D, EPS, ALU.mult, ALU.add).then_inc(st_var, 1)
            dve.tensor_scalar(V5[:], ST[:, TB:2 * TB], 1.0 / D, None, ALU.mult)
            dve.wait_ge(st_std, NORM["final"] + 1)
            dve.reciprocal(R4[:], SD4[:])
            dve.drain()
            newton(R4[:], V4[:], SD4[:])
            for x in range(2):
                dve.tensor_tensor(V5[:], V5[:], R4[:], ALU.mult)
                dve.drain()
            dve.tensor_scalar(V5[:], V5[:], EPS, None, ALU.add).then_inc(var2, 1)
            dve.wait_ge(std2, 1)
            dve.reciprocal(R5[:], SD5[:])
            dve.drain()
            newton(R5[:], V5[:], SD5[:])
            dve.tensor_tensor(R5[:], R5[:], R4[:], ALU.mult)
            dve.drain()
            for to, r, ready in ((DIAG2, R5, diag2), (DIAG, R4, st_diag)):
                dve.tensor_tensor(to[:].rearrange("p (b t) -> p b t", b=TB), IDENT[:, None, :].to_broadcast([P, TB, P]),
                                  r[:, :, None].to_broadcast([P, TB, P]), ALU.mult).then_inc(ready, 1)
            dve.wait_ge(bc2, 1)
            dve.tensor_copy(RS2[:], O[:])
            dve.wait_ge(st_bc, NORM["final"] + 1)
            dve.tensor_copy(RS[:], ST[:]).then_inc(st_rs, 1)
            dve.drain()

            def chunk_in(c, b):
                if not isinstance(c, int) or c >= 2:
                    dve.wait_ge(uc_ready, c - 1)
                x = X[:, bass.ds(c, 1), :]
                dve.scalar_tensor_tensor(UN[:, b, :], x, G12[:, bass.ds(c, 1)], RS2[:], ALU.mult, ALU.mult)\
                   .then_inc(un_ready, 1)
                dve.scalar_tensor_tensor(x, x, column("norm_final_g", c), RS[:], ALU.mult, ALU.mult)

            def mixer(c, b, more):
                four = bass.ds(4 * c, 4)
                cos, sin = ET[:, 0, four, :], ET[:, 1, four, :]
                dve.wait_ge(l_mm, c + 1)
                for ri, (x, y, op) in enumerate(((0, 1, ALU.add), (1, 0, ALU.subtract))):
                    dve.tensor_tensor(RT[:, 0], FOUR[:, :, x * NM:x * NM + NM], cos, ALU.mult)
                    ins = dve.tensor_tensor(RT[:, 1], FOUR[:, :, y * NM:y * NM + NM], sin, ALU.mult)
                    if ri:
                        ins.then_inc(l_used, 1)
                    dve.drain()
                    dve.tensor_tensor(VR[:, ri], RT[:, 0], RT[:, 1], op)
                    dve.drain()
                dve.tensor_copy(RHOT[:, :, 1:NM], RHO[:, four, None].to_broadcast([P, 4, NM - 1]))
                dve.drain()
                for ri in range(2):
                    dve.tensor_tensor_scan(WR[:, ri].rearrange("p a b -> p (a b)"), RHOT[:].rearrange("p a b -> p (a b)"),
                                           VR[:, ri].rearrange("p a b -> p (a b)"), 0.0, ALU.mult, ALU.add)
                dve.drain()
                if not isinstance(c, int) or c:
                    dve.wait_ge(y_mm, c)
                cos, sin = ET[:, 0, four, 0:NM - 1], ET[:, 1, four, 0:NM - 1]
                for ri, (x, y, op) in enumerate(((0, 1, ALU.subtract), (1, 0, ALU.add))):
                    dve.tensor_tensor(RT[:, 0, :, 0:NM - 1], WR[:, x, :, 0:NM - 1], cos, ALU.mult)
                    dve.tensor_tensor(RT[:, 1, :, 0:NM - 1], WR[:, y, :, 0:NM - 1], sin, ALU.mult)
                    dve.drain()
                    dve.tensor_tensor(SPV[:, ri, :, 1:NM], RT[:, 0, :, 0:NM - 1], RT[:, 1, :, 0:NM - 1], op)
                    dve.drain()
                dve.nop().then_inc(sp_ready, 1)
                dve.wait_ge(y_mm, c + 1)
                if not isinstance(c, int) or c >= 2:
                    dve.wait_ge(hid_hi, HIDDEN["s5"] + c - 1)
                dve.scalar_tensor_tensor(YC[:, b, :].rearrange("p (m i) -> p m i", i=LAG),
                                         UN[:, b, :].rearrange("p (m i) -> p m i", i=LAG),
                                         column("ssm_d_2", c), ST[:].rearrange("p (i m) -> p m i", i=LAG),
                                         ALU.mult, ALU.add).then_inc(y_out, 1)
                dve.drain()
                if more == 2:
                    chunk_in(c + 2, b)
                hidden_low(c, YC[:, b, :], HIDDEN["s5"] + c + 1)

            for c in range(2):
                chunk_in(c, c)
            dve.wait_ge(zeroed, 1)
            mixer(0, 0, 2)
            mixer(1, 1, 2)
            with dve.Fori(1, 3) as i:
                for b in range(2):
                    mixer(2 * i + b, b, 2)
            mixer(6, 0, 1)
            mixer(7, 1, 0)
            dve.drain()
            with dve.Fori(0, 8) as c:
                u = unit_at("s5glu", c, 0)
                x = X[:, bass.ds(c, 1), :]
                dve.wait_ge(unit_done, u + 1)
                dve.tensor_copy(TA, ACC[0][:]).then_inc(unit_out, 1)
                dve.drain()
                dve.wait_ge(gate_sig, 4 + c + 1)
                dve.tensor_tensor(TA, TA, TB_, ALU.mult).then_inc(unit_out, 1)
                dve.drain()
                dve.tensor_tensor(x, x, TA, ALU.add).then_inc(glu_out, 1)
                low("mlp0", c, "mlp_norm_2", PH[:, bass.ds(c, 1), :], PL[:, bass.ds(c, 1), :])

            def mlp(l, hi, lo):
                norm = f"mlp{l}"
                for g in range(GROUPS):
                    with dve.Fori(0, 4) as i:
                        for s in range(2):
                            k = 2 * i + s
                            h = (H1, H2)[s]
                            dve.wait_ge(unit_done, unit_at(f"up{l}{g}", i, s) + 1)
                            dve.tensor_tensor(h[:], ACC[s][:], RS[:], ALU.mult).then_inc(unit_out, 1)
                            dve.drain()
                            dve.scalar_tensor_tensor(h[:], h[:], 0.0, h[:], ALU.max, ALU.mult).then_inc(hid_ready, 1)
                            dve.drain()
                            hidden_low(k, h[:], HIDDEN[norm] + g * KC + k + 1, hi, lo)
                    if g < GROUPS - 1:
                        with dve.Fori(0, 4) as i:
                            for s in range(2):
                                x = X[:, bass.ds(2 * i + s, 1), :]
                                dve.wait_ge(unit_done, unit_at(f"dn{l}{g}", i, s) + 1)
                                dve.tensor_tensor(x, x, ACC[s][:], ALU.add).then_inc(unit_out, 1)
                        dve.drain()

            scales("mlp0", D)
            mlp(0, QH, QL)
            with dve.Fori(0, 4) as i:
                residual(f"dn0{GROUPS - 1}", "kv", "kv_norm_2", PH, PL, i)
            scales("kv", D)
            for j, to in enumerate((KT, VT)):
                with dve.Fori(0, 4) as i:
                    for s in range(2):
                        c = 2 * i + s
                        dve.wait_ge(unit_done, START["kv"] + j * 8 + c + 1)
                        dve.tensor_tensor(to[:, bass.ds(c, 1), :], ACC[s][:], RS[:], ALU.mult).then_inc(unit_out, 1)
                    c = i + 4 * j
                    low("wq", c, ("mix_norm_2", KC), QH[:, bass.ds(c, 1), :], QL[:, bass.ds(c, 1), :])
            dve.wait_ge(f_mm, 1)
            dve.tensor_tensor(FZ[:], O[:], RS[:], ALU.mult)
            dve.drain()
            dve.tensor_scalar(FZ[:], FZ[:], BF[:], None, ALU.add)
            dve.drain()
            dve.scalar_tensor_tensor(F[:], FZ[:], -1.0, FZ[:], ALU.mult, ALU.max).then_inc(f_abs, 1)
            dve.wait_ge(f_ln, 1)
            dve.scalar_tensor_tensor(FZ[:], FZ[:], 0.0, F[:], ALU.min, ALU.subtract)
            dve.drain()
            dve.tensor_tensor_scan(F[:], ONES[:, 0:1].to_broadcast([P, T]), FZ[:], 0.0, ALU.mult, ALU.add)\
               .then_inc(f_sum, 1)
            with dve.Fori(0, 4) as i:
                scaled("wq", i, QT, 0.125)
            dve.wait_ge(f_ready, 1)
            dve.tensor_tensor(FL[:], F[:], FH[:], ALU.subtract)
            dve.drain()
            dve.memset(LF[0:64, :].bitcast(F32), 0.0)
            dve.memset(RF[64:P, :].bitcast(F32), 0.0)
            dve.tensor_scalar(RF[32:64, :], FL[32:64, :].bitcast(F32), -1.0, None, ALU.mult)
            dve.tensor_copy(LF[96:P, :], FL[96:P, :].bitcast(F32))
            dve.wait_ge(f_ready, 2)
            dve.drain().then_inc(f_ready, 1)
            attend("fox", 8)
            with dve.Fori(0, 4) as i:
                residual("wo", "mlp1", ("mlp_norm_2", KC), QH, QL, i)
            scales("mlp1", D)
            mlp(1, PH, PL)
            with dve.Fori(0, 4) as i:
                for s in range(2):
                    x = X[:, bass.ds(2 * i + s, 1), :]
                    dve.wait_ge(unit_done, unit_at(f"dn1{GROUPS - 1}", i, s) + 1)
                    dve.tensor_tensor(x, x, ACC[s][:], ALU.add).then_inc(unit_out, 1)
            scales("last", D)
            for c in range(KC):
                dve.scalar_tensor_tensor(X[:, c, :], X[:, c, :], column("final_norm_2", c), RS[:], ALU.mult, ALU.mult)\
                   .then_inc(y_normed, 1)
            for c in range(1, KC, 2):
                dve.wait_ge(y_t, c + 1)
                dve.tensor_copy(YROW[:, :, c * P:(c + 1) * P], TR[1][:].rearrange("p (b f) -> p b f", f=P))\
                   .then_inc(y_odd, 1)


_INS = ["x", "mem", "positions", "norm_mix_g", "w_in", "w_out", "conv_b_w", "conv_b_b", "ln_b_g", "ln_b_b",
        "norm_cross_g", "norm_mem_g", "w_q_cross", "w_k_cross", "w_v_cross", "w_o_cross", "norm_ffn_g", "w_gate",
        "w_up", "ffn_conv_w", "ffn_conv_b", "w_down", "norm_final_g", "mix_norm_2", "mlp_norm_2", "mlp_w1_2",
        "mlp_w2_2", "ssm_log_dt_2", "ssm_a_re_2", "ssm_a_im_2", "ssm_b_re_2", "ssm_b_im_2", "ssm_c_re_2",
        "ssm_c_im_2", "ssm_d_2", "ssm_w_glu_2", "kv_norm_2", "w_kvf_2", "b_f_2", "attn_wq_2", "attn_wo_2",
        "final_norm_2", "constants"]
_OUTS = [((1, 512, 1024), "float32")]


def kernel(**inputs):
    import concourse.bacc as bacc
    from concourse.bass_utils import run_bass_kernel_spmd

    nc = bacc.Bacc("TRN2", target_bir_lowering=False, num_devices=1)
    inputs = dict(inputs, constants=constants())
    arrays, args = {}, {}
    for name in _INS:
        a = np.ascontiguousarray(inputs[name])
        arrays[f"in_{name}_dram"] = a
        args[name] = nc.dram_tensor(f"in_{name}_dram", a.shape, mybir.dt.from_np(a.dtype), kind="ExternalInput").ap()
    shape, dtype = _OUTS[0]
    out = nc.dram_tensor("out_0_dram", shape, mybir.dt.from_np(np.dtype(dtype)), kind="ExternalOutput").ap()
    build_program(nc, args, out)
    r = run_bass_kernel_spmd(nc, [arrays], core_ids=[0])
    return r.results[0]["out_0_dram"]
```
